# Optimizing a Trainium2 kernel written in Bass

```python
import jax, jax.numpy as jnp
from jax import lax
import numpy as np
import math

D_MODEL = 1024
BATCH = 1
SEQ = 1024
DEPTH = 1

CHUNK = 64
CONV_WIDTH = D_MODEL
CONV_GROUPS = 16
CONV_K = 3
LRU_WIDTH = D_MODEL
LRU_HEADS = 16
LRU_HEAD_DIM = LRU_WIDTH // LRU_HEADS
LRU_CONV_K = 4
LRU_C = 8.0
D_FF = ((-(-8 * D_MODEL // 3)) + 255) // 256 * 256
RMS_EPS = 1e-6
IN_WIDTHS = (CONV_WIDTH, CONV_WIDTH, CONV_WIDTH, LRU_WIDTH, LRU_WIDTH, D_MODEL, D_MODEL)
IN_TOTAL = sum(IN_WIDTHS)
SPLIT_POINTS = tuple(int(v) for v in np.cumsum(IN_WIDTHS)[:-1])


def rmsnorm(x, g):
    xf = x.astype(jnp.float32)
    var = jnp.mean(xf * xf, axis=-1, keepdims=True)
    return (xf * lax.rsqrt(var + RMS_EPS) * g.astype(jnp.float32)).astype(x.dtype)

def causal_depthwise_conv(x, w, b=None):
    K = w.shape[0]
    S = x.shape[1]
    xp = jnp.pad(x, ((0, 0), (K - 1, 0), (0, 0)))
    y = xp[:, 0:S] * w[0]
    for k in range(1, K):
        y = y + xp[:, k:k + S] * w[k]
    if b is not None:
        y = y + b
    return y

def rg_lru(x, w_a, b_a, w_x, b_x, lam):
    Bsz, S, W = x.shape
    f32 = jnp.float32
    xf = x.astype(f32)
    xh = xf.reshape(Bsz, S, LRU_HEADS, LRU_HEAD_DIM)
    r = jax.nn.sigmoid(jnp.einsum('bshd,hde->bshe', xh, w_a.astype(f32)).reshape(Bsz, S, W) + b_a.astype(f32))
    i = jax.nn.sigmoid(jnp.einsum('bshd,hde->bshe', xh, w_x.astype(f32)).reshape(Bsz, S, W) + b_x.astype(f32))
    log_a = -LRU_C * r * jax.nn.softplus(-lam.astype(f32))
    a = jnp.exp(log_a)
    b = jnp.sqrt(-jnp.expm1(2.0 * log_a)) * (i * xf)
    n_chunks = S // CHUNK
    a_c = a.reshape(Bsz, n_chunks, CHUNK, W)
    b_c = b.reshape(Bsz, n_chunks, CHUNK, W)

    def combine(left, right):
        a_l, b_l = left
        a_r, b_r = right
        return a_l * a_r, a_r * b_l + b_r

    a_cum, h_loc = lax.associative_scan(combine, (a_c, b_c), axis=2)

    def step(h_prev, inp):
        a_cum_k, h_loc_k = inp
        h = h_loc_k + a_cum_k * h_prev[:, None, :]
        return h[:, -1], h

    h0 = jnp.zeros((Bsz, W), f32)
    _, hs = lax.scan(step, h0, (jnp.moveaxis(a_cum, 1, 0), jnp.moveaxis(h_loc, 1, 0)))
    return jnp.moveaxis(hs, 0, 1).reshape(Bsz, S, W).astype(x.dtype)

def first_inputs(seed: int = 0) -> dict:
    key = jax.random.key(seed)
    ks = jax.random.split(key, 24)
    f32 = jnp.float32
    nrm = lambda k, shape, fan_in: jax.random.normal(k, shape, f32) * (fan_in ** -0.5)
    x = jax.random.normal(ks[0], (BATCH, SEQ, D_MODEL), f32)
    ln1_g = 1.0 + 0.02 * jax.random.normal(ks[1], (DEPTH, D_MODEL), f32)
    w_in = nrm(ks[2], (DEPTH, D_MODEL, IN_TOTAL), D_MODEL)
    conv_a_w = nrm(ks[3], (DEPTH, CONV_K, CONV_WIDTH), CONV_K)
    conv_b_w = nrm(ks[4], (DEPTH, LRU_CONV_K, LRU_WIDTH), LRU_CONV_K)
    conv_b_b = 0.02 * jax.random.normal(ks[5], (DEPTH, LRU_WIDTH), f32)
    lru_wa = nrm(ks[6], (DEPTH, LRU_HEADS, LRU_HEAD_DIM, LRU_HEAD_DIM), LRU_HEAD_DIM)
    lru_ba = 0.02 * jax.random.normal(ks[7], (DEPTH, LRU_WIDTH), f32)
    lru_wx = nrm(ks[8], (DEPTH, LRU_HEADS, LRU_HEAD_DIM, LRU_HEAD_DIM), LRU_HEAD_DIM)
    lru_bx = 0.02 * jax.random.normal(ks[9], (DEPTH, LRU_WIDTH), f32)
    u = jax.random.uniform(ks[10], (DEPTH, LRU_WIDTH), f32, 0.9, 0.999)
    s = u ** (1.0 / LRU_C)
    lru_lambda = jnp.log(s) - jnp.log1p(-s)
    w_out_a = nrm(ks[11], (DEPTH, CONV_WIDTH, D_MODEL), CONV_WIDTH)
    w_out_b = nrm(ks[12], (DEPTH, LRU_WIDTH, D_MODEL), LRU_WIDTH)
    gate_bias = 0.02 * jax.random.normal(ks[13], (DEPTH, 2, D_MODEL), f32)
    w_o = nrm(ks[14], (DEPTH, D_MODEL, D_MODEL), D_MODEL)
    ln2_g = 1.0 + 0.02 * jax.random.normal(ks[15], (DEPTH, D_MODEL), f32)
    w_ffn_gate = nrm(ks[16], (DEPTH, D_MODEL, D_FF), D_MODEL)
    w_ffn_up = nrm(ks[17], (DEPTH, D_MODEL, D_FF), D_MODEL)
    w_ffn_down = nrm(ks[18], (DEPTH, D_FF, D_MODEL), D_FF)
    final_g = 1.0 + 0.02 * jax.random.normal(ks[19], (D_MODEL,), f32)
    return {"x": x, "ln1_g": ln1_g, "w_in": w_in, "conv_a_w": conv_a_w,
            "conv_b_w": conv_b_w, "conv_b_b": conv_b_b, "lru_wa": lru_wa,
            "lru_ba": lru_ba, "lru_wx": lru_wx, "lru_bx": lru_bx,
            "lru_lambda": lru_lambda, "w_out_a": w_out_a, "w_out_b": w_out_b,
            "gate_bias": gate_bias, "w_o": w_o, "ln2_g": ln2_g,
            "w_ffn_gate": w_ffn_gate, "w_ffn_up": w_ffn_up,
            "w_ffn_down": w_ffn_down, "final_g": final_g}

def first_block(x, ln1_g, w_in, conv_a_w, conv_b_w, conv_b_b, lru_wa, lru_ba,
              lru_wx, lru_bx, lru_lambda, w_out_a, w_out_b, gate_bias, w_o,
              ln2_g, w_ffn_gate, w_ffn_up, w_ffn_down, final_g):
    for l in range(DEPTH):
        h = rmsnorm(x, ln1_g[l])
        proj = h @ w_in[l]
        b_a, c_a, x_a, x_b, g_b, gate_a_logit, gate_b_logit = jnp.split(proj, SPLIT_POINTS, axis=-1)
        y_a = b_a * causal_depthwise_conv(c_a * x_a, conv_a_w[l])
        u_b = causal_depthwise_conv(x_b, conv_b_w[l], conv_b_b[l])
        y_b = rg_lru(u_b, lru_wa[l], lru_ba[l], lru_wx[l], lru_bx[l], lru_lambda[l])
        y_b = y_b * jax.nn.gelu(g_b)
        merged = (jax.nn.sigmoid(gate_a_logit + gate_bias[l, 0]) * (y_a @ w_out_a[l])
                  + jax.nn.sigmoid(gate_b_logit + gate_bias[l, 1]) * (y_b @ w_out_b[l]))
        x = x + merged @ w_o[l]
        h = rmsnorm(x, ln2_g[l])
        x = x + (jax.nn.silu(h @ w_ffn_gate[l]) * (h @ w_ffn_up[l])) @ w_ffn_down[l]
    return rmsnorm(x, final_g)


D_MIX = 2 * D_MODEL
SSD_WIDTH = D_MIX // 2
SSD_HEAD_DIM = 64
SSD_HEADS = SSD_WIDTH // SSD_HEAD_DIM
SSD_GROUPS = 2
SSD_STATE = 128
SSD_CONV = 4
SSD_XBC = SSD_WIDTH + 2 * SSD_GROUPS * SSD_STATE
ML_WIDTH = D_MIX - SSD_WIDTH
ML_HEADS = 8
ML_HEAD_DIM = ML_WIDTH // ML_HEADS
ML_CONV = 4
IN_COLS = (SSD_WIDTH + SSD_XBC + SSD_HEADS) + (4 * ML_WIDTH + 2 * ML_HEADS)
MOE_GROUPS = 4
EXPERTS_PER_GROUP = 8
N_EXPERTS = MOE_GROUPS * EXPERTS_PER_GROUP
TOP_K = 2
D_EXPERT = D_MODEL // 2
EPS = 1e-6
STAB_INIT = -1e30


def rmsnorm_2(x, w):
    xf = x.astype(jnp.float32)
    y = xf * lax.rsqrt(jnp.mean(xf * xf, axis=-1, keepdims=True) + EPS)
    return (y * w.astype(jnp.float32)).astype(x.dtype)

def group_rmsnorm(y, w, groups):
    b, l, c = y.shape
    yg = y.reshape(b, l, groups, c // groups)
    yg = yg * lax.rsqrt(jnp.mean(yg * yg, axis=-1, keepdims=True) + EPS)
    return yg.reshape(b, l, c) * w.astype(jnp.float32)

def causal_dwconv(x, w, b):
    k, c = w.shape
    y = lax.conv_general_dilated(x, w[:, None, :].astype(x.dtype), window_strides=(1,),
                                 padding=[(k - 1, 0)], dimension_numbers=("NWC", "WIO", "NWC"),
                                 feature_group_count=c)
    return y + b.astype(x.dtype)

def ssd_mixer(z, xbc, dt_raw, conv_w, conv_b, dt_bias, a_log, d_skip, norm_w):
    f32 = jnp.float32
    bsz, seq, _ = z.shape
    nc = seq // CHUNK
    r = SSD_HEADS // SSD_GROUPS
    xbc = jax.nn.silu(causal_dwconv(xbc, conv_w, conv_b)).astype(f32)
    xs = xbc[..., :SSD_WIDTH].reshape(bsz, seq, SSD_HEADS, SSD_HEAD_DIM)
    bm = xbc[..., SSD_WIDTH:SSD_WIDTH + SSD_GROUPS * SSD_STATE].reshape(bsz, seq, SSD_GROUPS, SSD_STATE)
    cm = xbc[..., SSD_WIDTH + SSD_GROUPS * SSD_STATE:].reshape(bsz, seq, SSD_GROUPS, SSD_STATE)
    dt = jax.nn.softplus(dt_raw.astype(f32) + dt_bias.astype(f32))
    a = -jnp.exp(a_log.astype(f32))
    xdt = (xs * dt[..., None]).reshape(bsz, nc, CHUNK, SSD_GROUPS, r, SSD_HEAD_DIM)
    xdt = jnp.moveaxis(xdt, 1, 0)
    adt = jnp.transpose((dt * a).reshape(bsz, nc, CHUNK, SSD_GROUPS, r), (1, 0, 3, 4, 2))
    bc = jnp.moveaxis(bm.reshape(bsz, nc, CHUNK, SSD_GROUPS, SSD_STATE), 1, 0)
    cc = jnp.moveaxis(cm.reshape(bsz, nc, CHUNK, SSD_GROUPS, SSD_STATE), 1, 0)
    mask = jnp.tril(jnp.ones((CHUNK, CHUNK), dtype=bool))

    def step(state, inp):
        x_c, a_c, b_c, c_c = inp
        a_cs = jnp.cumsum(a_c, axis=-1)
        seg = jnp.where(mask, a_cs[..., :, None] - a_cs[..., None, :], -jnp.inf)
        lmat = jnp.exp(seg)
        cb = jnp.einsum('blgn,bsgn->bgls', c_c, b_c)
        y = jnp.einsum('bgls,bgrls,bsgrp->blgrp', cb, lmat, x_c)
        y = y + jnp.einsum('blgn,bgrpn,bgrl->blgrp', c_c, state, jnp.exp(a_cs))
        decay = jnp.exp(a_cs[..., -1:] - a_cs)
        state = state * jnp.exp(a_cs[..., -1])[..., None, None] + \
            jnp.einsum('blgn,bgrl,blgrp->bgrpn', b_c, decay, x_c)
        return state, y

    state0 = jnp.zeros((bsz, SSD_GROUPS, r, SSD_HEAD_DIM, SSD_STATE), f32)
    _, y = lax.scan(step, state0, (xdt, adt, bc, cc))
    y = jnp.moveaxis(y, 0, 1).reshape(bsz, seq, SSD_HEADS, SSD_HEAD_DIM)
    y = y + d_skip.astype(f32)[:, None] * xs
    y = y.reshape(bsz, seq, SSD_WIDTH) * jax.nn.silu(z.astype(f32))
    return group_rmsnorm(y, norm_w, SSD_GROUPS).astype(z.dtype)

def mlstm_mixer(qk, v, o_pre, i_pre, f_pre, conv_w, conv_b, i_bias, f_bias, norm_w):
    f32 = jnp.float32
    bsz, seq, _ = v.shape
    nc = seq // CHUNK
    qk = jax.nn.silu(causal_dwconv(qk, conv_w, conv_b)).astype(f32)
    shp = (bsz, nc, CHUNK, ML_HEADS, ML_HEAD_DIM)
    q = jnp.moveaxis(qk[..., :ML_WIDTH].reshape(shp), 1, 0)
    k = jnp.moveaxis(qk[..., ML_WIDTH:].reshape(shp), 1, 0) * (ML_HEAD_DIM ** -0.5)
    vv = jnp.moveaxis(v.astype(f32).reshape(shp), 1, 0)
    ig = i_pre.astype(f32) + i_bias.astype(f32)
    lf = jax.nn.log_sigmoid(f_pre.astype(f32) + f_bias.astype(f32))
    ig = jnp.transpose(ig.reshape(bsz, nc, CHUNK, ML_HEADS), (1, 0, 3, 2))
    lf = jnp.transpose(lf.reshape(bsz, nc, CHUNK, ML_HEADS), (1, 0, 3, 2))
    mask = jnp.tril(jnp.ones((CHUNK, CHUNK), dtype=bool))

    def step(carry, inp):
        cmem, nmem, m = carry
        q_c, k_c, v_c, i_c, f_c = inp
        bcum = jnp.cumsum(f_c, axis=-1)
        dmat = jnp.where(mask, bcum[..., :, None] - bcum[..., None, :] + i_c[..., None, :], -jnp.inf)
        m_inter = bcum + m[..., None]
        m_t = jnp.maximum(m_inter, jnp.max(dmat, axis=-1))
        w = jnp.exp(dmat - m_t[..., None])
        s = jnp.einsum('blhd,bshd->bhls', q_c, k_c) * w
        inter = jnp.exp(m_inter - m_t)
        num = jnp.einsum('bhls,bshv->blhv', s, v_c) + \
            jnp.einsum('blhk,bhkv->blhv', q_c, cmem) * jnp.swapaxes(inter, 1, 2)[..., None]
        den = jnp.sum(s, axis=-1) + inter * jnp.einsum('blhk,bhk->bhl', q_c, nmem)
        den = jnp.maximum(jnp.abs(den), jnp.exp(-m_t))
        h = num / jnp.swapaxes(den, 1, 2)[..., None]
        g = bcum[..., -1]
        a = g[..., None] - bcum + i_c
        m_new = jnp.maximum(g + m, jnp.max(a, axis=-1))
        wc = jnp.exp(a - m_new[..., None])
        carry_scale = jnp.exp(g + m - m_new)
        cmem = cmem * carry_scale[..., None, None] + jnp.einsum('bhs,bshk,bshv->bhkv', wc, k_c, v_c)
        nmem = nmem * carry_scale[..., None] + jnp.einsum('bhs,bshk->bhk', wc, k_c)
        return (cmem, nmem, m_new), h

    carry0 = (jnp.zeros((bsz, ML_HEADS, ML_HEAD_DIM, ML_HEAD_DIM), f32),
              jnp.zeros((bsz, ML_HEADS, ML_HEAD_DIM), f32),
              jnp.full((bsz, ML_HEADS), STAB_INIT, f32))
    _, h = lax.scan(step, carry0, (q, k, vv, ig, lf))
    h = jnp.moveaxis(h, 0, 1).reshape(bsz, seq, ML_HEADS, ML_HEAD_DIM)
    mu = jnp.mean(h, axis=-1, keepdims=True)
    var = jnp.mean((h - mu) ** 2, axis=-1, keepdims=True)
    h = ((h - mu) * lax.rsqrt(var + EPS)).reshape(bsz, seq, ML_WIDTH) * norm_w.astype(f32)
    h = jax.nn.sigmoid(o_pre.astype(f32)) * h
    return h.astype(v.dtype)

def hier_moe(h, wg, bg, we, be, w_gate, w_up, w_down):
    bsz, seq, d = h.shape
    t = bsz * seq
    xf = h.reshape(t, d)
    x32 = xf.astype(jnp.float32)
    p_group = jax.nn.softmax(x32 @ wg.astype(jnp.float32) + bg.astype(jnp.float32), axis=-1)
    pg, g_sel = lax.top_k(p_group, 1)
    e_logits = (x32 @ we.astype(jnp.float32) + be.astype(jnp.float32)).reshape(t, MOE_GROUPS, EXPERTS_PER_GROUP)
    e_in = jnp.take_along_axis(e_logits, g_sel[:, :, None], axis=1)[:, 0]
    top_v, top_i = lax.top_k(e_in, TOP_K)
    gates = jax.nn.softmax(top_v, axis=-1) * pg
    ids = (g_sel * EXPERTS_PER_GROUP + top_i).reshape(-1).astype(jnp.int32)
    order = jnp.argsort(ids)
    tok = order // TOP_K
    xs = xf[tok]
    sizes = jnp.bincount(ids, length=N_EXPERTS).astype(jnp.int32)
    hg = lax.ragged_dot(xs, w_gate.astype(xs.dtype), sizes)
    hu = lax.ragged_dot(xs, w_up.astype(xs.dtype), sizes)
    ys = lax.ragged_dot(jax.nn.silu(hg) * hu, w_down.astype(xs.dtype), sizes)
    ys = ys * gates.reshape(-1)[order][:, None].astype(ys.dtype)
    y = jax.ops.segment_sum(ys, tok, num_segments=t)
    return y.reshape(bsz, seq, d).astype(h.dtype)

def second_inputs(seed: int = 0) -> dict:
    key = jax.random.key(seed)
    ks = jax.random.split(key, 26)
    nrm = lambda k, s, sc: jax.random.normal(k, s, jnp.float32) * sc
    dt0 = jnp.exp(jax.random.uniform(ks[6], (DEPTH, SSD_HEADS), jnp.float32, math.log(1e-3), math.log(1e-1)))
    return {
        "x": jax.random.normal(ks[0], (BATCH, SEQ, D_MODEL), jnp.float32),
        "norm1_w": 1.0 + nrm(ks[1], (DEPTH, D_MODEL), 0.02),
        "w_in": nrm(ks[2], (DEPTH, D_MODEL, IN_COLS), D_MODEL ** -0.5),
        "ssd_conv_w": nrm(ks[3], (DEPTH, SSD_CONV, SSD_XBC), SSD_CONV ** -0.5),
        "ssd_conv_b": nrm(ks[4], (DEPTH, SSD_XBC), 0.02),
        "ssd_dt_bias": dt0 + jnp.log(-jnp.expm1(-dt0)),
        "ssd_a_log": jnp.log(jax.random.uniform(ks[5], (DEPTH, SSD_HEADS), jnp.float32, 1.0, 16.0)),
        "ssd_d": 1.0 + nrm(ks[7], (DEPTH, SSD_HEADS), 0.1),
        "ssd_norm_w": 1.0 + nrm(ks[8], (DEPTH, SSD_WIDTH), 0.02),
        "ml_conv_w": nrm(ks[9], (DEPTH, ML_CONV, 2 * ML_WIDTH), ML_CONV ** -0.5),
        "ml_conv_b": nrm(ks[10], (DEPTH, 2 * ML_WIDTH), 0.02),
        "ml_i_bias": nrm(ks[11], (DEPTH, ML_HEADS), 0.1),
        "ml_f_bias": 3.0 + 3.0 * jax.random.uniform(ks[12], (DEPTH, ML_HEADS), jnp.float32),
        "ml_norm_w": 1.0 + nrm(ks[13], (DEPTH, ML_WIDTH), 0.02),
        "w_out": nrm(ks[14], (DEPTH, D_MIX, D_MODEL), D_MIX ** -0.5),
        "norm2_w": 1.0 + nrm(ks[15], (DEPTH, D_MODEL), 0.02),
        "router_g_w": nrm(ks[16], (DEPTH, D_MODEL, MOE_GROUPS), D_MODEL ** -0.5),
        "router_g_b": nrm(ks[17], (DEPTH, MOE_GROUPS), 0.01),
        "router_e_w": nrm(ks[18], (DEPTH, D_MODEL, N_EXPERTS), D_MODEL ** -0.5),
        "router_e_b": nrm(ks[19], (DEPTH, N_EXPERTS), 0.01),
        "exp_w_gate": nrm(ks[20], (DEPTH, N_EXPERTS, D_MODEL, D_EXPERT), D_MODEL ** -0.5),
        "exp_w_up": nrm(ks[21], (DEPTH, N_EXPERTS, D_MODEL, D_EXPERT), D_MODEL ** -0.5),
        "exp_w_down": nrm(ks[22], (DEPTH, N_EXPERTS, D_EXPERT, D_MODEL), D_EXPERT ** -0.5),
        "norm_f_w": 1.0 + nrm(ks[23], (D_MODEL,), 0.02),
    }

def second_block(x, norm1_w, w_in, ssd_conv_w, ssd_conv_b, ssd_dt_bias, ssd_a_log, ssd_d, ssd_norm_w,
              ml_conv_w, ml_conv_b, ml_i_bias, ml_f_bias, ml_norm_w, w_out, norm2_w,
              router_g_w, router_g_b, router_e_w, router_e_b, exp_w_gate, exp_w_up, exp_w_down, norm_f_w):
    o1 = SSD_WIDTH
    o2 = o1 + SSD_XBC
    o3 = o2 + SSD_HEADS
    o4 = o3 + 2 * ML_WIDTH
    o5 = o4 + ML_WIDTH
    o6 = o5 + ML_WIDTH
    o7 = o6 + ML_HEADS
    for layer in range(DEPTH):
        h = rmsnorm_2(x, norm1_w[layer])
        p = jnp.einsum('bsd,de->bse', h, w_in[layer])
        y_ssd = ssd_mixer(p[..., :o1], p[..., o1:o2], p[..., o2:o3],
                          ssd_conv_w[layer], ssd_conv_b[layer], ssd_dt_bias[layer],
                          ssd_a_log[layer], ssd_d[layer], ssd_norm_w[layer])
        y_ml = mlstm_mixer(p[..., o3:o4], p[..., o4:o5], p[..., o5:o6], p[..., o6:o7], p[..., o7:],
                           ml_conv_w[layer], ml_conv_b[layer], ml_i_bias[layer], ml_f_bias[layer],
                           ml_norm_w[layer])
        mix = jnp.concatenate([y_ssd, y_ml], axis=-1)
        x = x + jnp.einsum('bse,ed->bsd', mix, w_out[layer])
        h2 = rmsnorm_2(x, norm2_w[layer])
        x = x + hier_moe(h2, router_g_w[layer], router_g_b[layer], router_e_w[layer], router_e_b[layer],
                         exp_w_gate[layer], exp_w_up[layer], exp_w_down[layer])
    return rmsnorm_2(x, norm_f_w)


def setup_inputs(seed=0):
    out = dict(first_inputs(seed))
    for name, value in second_inputs(seed + 1).items():
        if name != "x":
            out[name + "_2"] = value
    return out


def reference(
    x, ln1_g, w_in, conv_a_w, conv_b_w, conv_b_b, lru_wa, lru_ba, lru_wx, lru_bx, lru_lambda,
    w_out_a, w_out_b, gate_bias, w_o, ln2_g, w_ffn_gate, w_ffn_up, w_ffn_down, final_g,
    norm1_w_2, w_in_2, ssd_conv_w_2, ssd_conv_b_2, ssd_dt_bias_2, ssd_a_log_2, ssd_d_2,
    ssd_norm_w_2, ml_conv_w_2, ml_conv_b_2, ml_i_bias_2, ml_f_bias_2, ml_norm_w_2, w_out_2,
    norm2_w_2, router_g_w_2, router_g_b_2, router_e_w_2, router_e_b_2, exp_w_gate_2, exp_w_up_2,
    exp_w_down_2, norm_f_w_2,
):
    x = first_block(
        x, ln1_g, w_in, conv_a_w, conv_b_w, conv_b_b, lru_wa, lru_ba, lru_wx, lru_bx,
        lru_lambda, w_out_a, w_out_b, gate_bias, w_o, ln2_g, w_ffn_gate, w_ffn_up, w_ffn_down,
        final_g,
    )
    return second_block(
        x, norm1_w_2, w_in_2, ssd_conv_w_2, ssd_conv_b_2, ssd_dt_bias_2, ssd_a_log_2, ssd_d_2,
        ssd_norm_w_2, ml_conv_w_2, ml_conv_b_2, ml_i_bias_2, ml_f_bias_2, ml_norm_w_2, w_out_2,
        norm2_w_2, router_g_w_2, router_g_b_2, router_e_w_2, router_e_b_2, exp_w_gate_2,
        exp_w_up_2, exp_w_down_2, norm_f_w_2,
    )


_drawn_inputs = setup_inputs


def setup_inputs(seed=0):
    import zlib

    import numpy as np

    out = dict(_drawn_inputs(seed))
    spreads = {}
    factors = {'lru_ba': 8.0,
     'lru_bx': 6.587,
     'gate_bias': 4.955,
     'ml_conv_b_2': 4.792,
     'ml_i_bias_2': 64.0,
     'ml_norm_w_2': 3.8,
     'router_g_b_2': 11.458,
     'router_e_b_2': 12.808,
     'norm_f_w_2': 8.193,
     'ssd_conv_b_2': 3.663,
     'ssd_norm_w_2': 4.361,
     'norm2_w_2': 3.383}
    for name, (base, spread) in spreads.items():
        noise = np.random.default_rng([zlib.crc32(name.encode()), seed]).standard_normal(out[name].shape)
        drawn = base * np.exp(spread * noise) if base else spread * noise
        out[name] = __import__('jax').numpy.asarray(drawn.astype(out[name].dtype))
    for name, factor in factors.items():
        out[name] = (out[name] * factor).astype(out[name].dtype)
    return out
```

```python
from contextlib import ExitStack

import concourse.bass as bass
from concourse import mybir

F32 = mybir.dt.float32
F32R = mybir.dt.float32r
I32 = mybir.dt.int32
U32 = mybir.dt.uint32
ACT = mybir.ActivationFunctionType
ALU = mybir.AluOpType
AX = mybir.AxisListType.X
P = 128
EPS = 1e-6
USED = []


def wait(eng, sem, value):
    if isinstance(value, int) and value <= 0:
        return
    eng.wait_ge(sem, value)


def steps(eng, n, body, end=None):
    body(0)
    body(1)
    with eng.Fori(2, n if end is None else end) as i:
        body(i)


class Chain:

    def __init__(self, eng, sem, per=0):
        self.eng, self.sem, self.per, self.base, self.n = eng, sem, per, 0, 0

    def start(self, i, n=0):
        self.base, self.n = i * self.per, n

    def inc(self, ins):
        ins.then_inc(self.sem, 1)
        self.n += 1

    def wait(self):
        self.eng.wait_ge(self.sem, self.base + self.n)

    def link(self, ins):
        self.inc(ins)
        self.wait()

    def end(self):
        assert self.n == self.per, (self.n, self.per)


class Names:
    pass


class Core:

    def __init__(self, nc, ctx):
        self.nc, self.ctx = nc, ctx

    def sb(self, name, shape, dt=F32):
        return self.ctx.enter_context(self.nc.sbuf_tensor(name, shape, dt))

    def ps(self, name, shape, dt=F32):
        return self.ctx.enter_context(self.nc.psum_tensor(name, shape, dt))

    def sem(self, name):
        s = self.nc.alloc_semaphore(name)
        USED.append(s)
        return s

    def sems(self, name, n):
        return [self.sem(f"{name}{i}") for i in range(n)]


def recycle_semaphores(nc):
    nc.clear_and_free_semaphores(list(USED))
    nc.all_engine_barrier()
    USED.clear()


def f32(ap):
    return ap.bitcast(F32)


def log1p_exp_neg(nc, c, e, z, z2, p):
    v = nc.vector
    c.link(v.tensor_scalar(p, e, 2.0, None, ALU.add))
    c.link(v.reciprocal(p, p))
    c.link(v.tensor_tensor(z, e, p, ALU.mult))
    c.link(v.tensor_tensor(z2, z, z, ALU.mult))
    c.link(v.tensor_scalar(p, z2, 1.0 / 19.0, None, ALU.mult))
    for k in range(8, 0, -1):
        c.link(v.scalar_tensor_tensor(p, p, 1.0 / (2 * k + 1), z2, ALU.add, ALU.mult))
    c.link(v.scalar_tensor_tensor(p, p, 1.0, z, ALU.add, ALU.mult))
    c.link(v.tensor_scalar(p, p, 2.0, None, ALU.mult))


def norm_transpose(nc, tag, x_tm, gain_row, out_hl, x_dram=None, x_out=None, row_gain=None, rows_out=None):
    tiles, d = x_tm.shape[1], x_tm.shape[2]
    kt = d // P
    with ExitStack() as ctx:
        c = Core(nc, ctx)
        ident = c.sb(f"{tag}_ident", [P, P])
        gain = c.sb(f"{tag}_gain", [P, kt])
        square = c.sb(f"{tag}_square", [P, d])
        ssq = c.sb(f"{tag}_ssq", [P, 2 * tiles])
        std = c.sb(f"{tag}_std", [P, 2 * tiles])
        rstd = c.sb(f"{tag}_rstd", [P, 2 * tiles])
        eps = c.sb(f"{tag}_eps", [P, 1])
        xn = c.sb(f"{tag}_xn", [P, 2, d])
        xg = c.sb(f"{tag}_xg", [P, 2, kt, P])
        rowg = c.sb(f"{tag}_rowg", [P, d]) if row_gain is not None else None
        turned = [c.ps(f"{tag}_turned{b}", [P, kt, P]) for b in range(2)]
        if rows_out is not None:
            gain_b, hrow = c.sb(f"{tag}_gain_rows", [P, d]), c.sb(f"{tag}_h_rows", [P, 2, d])
            s_gr, s_hr = c.sem(f"{tag}_gain_rows_loaded"), c.sem(f"{tag}_h_rows_ready")
            s_hs = c.sems(f"{tag}_h_rows_stored", 2)
        s_x = c.sems(f"{tag}_x_loaded", tiles if x_dram is not None else 0)
        s_g = c.sem(f"{tag}_gain_loaded")
        s_id = c.sem(f"{tag}_ident_ready")
        s_sq = c.sem(f"{tag}_squares")
        s_std = c.sem(f"{tag}_std_ready")
        s_rs = c.sem(f"{tag}_rstd_ready")
        s_x2 = c.sem(f"{tag}_x_normed")
        s_xn = c.sem(f"{tag}_scaled")
        s_t = c.sem(f"{tag}_transposed")
        s_xg = c.sem(f"{tag}_gained")
        s_hi = c.sem(f"{tag}_high")
        s_lo = c.sem(f"{tag}_low")
        s_st = c.sem(f"{tag}_x_stored")
        block = ctx.enter_context(nc.Block())

        @block.sync
        def _(sp):
            with nc.allow_non_contiguous_dma(reason="gain column layout"):
                sp.dma_start(gain[:], gain_row.rearrange("(k p) -> p k", p=P)).then_inc(s_g, 16)
            if rowg is not None:
                sp.dma_start(rowg[:], row_gain.rearrange("(a n) -> a n", a=1).broadcast_to([P, d])).then_inc(s_g, 16)
            if x_dram is not None:
                for t in range(tiles):
                    sp.dma_start(x_tm[:, t, :], x_dram[t * P:(t + 1) * P, :]).then_inc(s_x[t], 16)
            if x_out is not None:
                for t in range(tiles):
                    if rowg is not None:
                        sp.wait_ge(s_x2, 2 * t + 2)
                    sp.dma_start(x_out[t * P:(t + 1) * P, :], x_tm[:, t, :]).then_inc(s_st, 16)
            if rows_out is not None:
                sp.dma_start(gain_b[:], gain_row.rearrange("(a n) -> a n", a=1).broadcast_to([P, d])).then_inc(s_gr, 16)
                for t in range(tiles):
                    sp.wait_ge(s_hr, t + 1)
                    sp.dma_start(rows_out[t * P:(t + 1) * P, :], hrow[:, t % 2]).then_inc(s_hs[t % 2], 16)
                for b in range(2):
                    sp.wait_ge(s_hs[b], 16 * (tiles // 2))
            if x_out is not None:
                sp.wait_ge(s_st, 16 * tiles)

        @block.gpsimd
        def _(pool):
            nc.gpsimd.memset(ident[:], 0.0).then_inc(s_id, 1)
            pool.wait_ge(s_id, 1)
            nc.gpsimd.affine_select(out=ident[:], in_=ident[:], compare_op=ALU.not_equal, fill=1.0, base=0,
                                    pattern=[[-1, P]], channel_multiplier=1).then_inc(s_id, 1)
            nc.gpsimd.memset(eps[:], EPS).then_inc(s_id, 1)
            if rows_out is not None:
                pool.wait_ge(s_gr, 16)
                for t in range(tiles):
                    pool.wait_ge(s_xn, t + 1)
                    wait(pool, s_hs[t % 2], 16 * (t // 2))
                    nc.gpsimd.tensor_tensor(hrow[:, t % 2], xn[:, t % 2, :], gain_b[:], ALU.mult).then_inc(s_hr, 1)

        NR = 1 if rowg is None else 2

        @block.scalar
        def _(act):
            def scale(t):
                act.wait_ge(s_rs, NR * (t + 1))
                if t >= 2:
                    act.wait_ge(s_t, t - 1)
                    if rows_out is not None:
                        act.wait_ge(s_hr, t - 1)
                nc.scalar.activation(xn[:, t % 2, :], x_tm[:, t, :], ACT.Copy,
                                     scale=rstd[:, tiles + t:tiles + t + 1]).then_inc(s_xn, 1)

            def deviation(n, t, col):
                nc.scalar.activation(square[:], x_tm[:, t, :], ACT.Square, accum_out=ssq[:, col:col + 1]).then_inc(s_sq, 1)
                act.wait_ge(s_sq, n + 1)
                nc.scalar.activation(std[:, col:col + 1], ssq[:, col:col + 1], ACT.Sqrt, scale=1.0 / d,
                                     bias=eps[:]).then_inc(s_std, 1)

            def high(t):
                act.wait_ge(s_xg, t + 1)
                nc.scalar.activation(out_hl[:, 0, :, t * P:(t + 1) * P], xg[:, t % 2], ACT.Copy).then_inc(s_hi, 1)

            act.wait_ge(s_id, 3)
            for t in range(tiles):
                if x_dram is not None:
                    act.wait_ge(s_x[t], 16)
                if rowg is not None:
                    deviation(NR * t, t, t)
                    act.wait_ge(s_x2, 2 * t + 2)
                deviation(NR * t + NR - 1, t, tiles + t)
                if t >= 1:
                    scale(t - 1)
                if t >= 2:
                    high(t - 2)
            scale(tiles - 1)
            high(tiles - 2)
            high(tiles - 1)

        @block.vector
        def _(dve):
            dve.wait_ge(s_g, 16 if rowg is None else 32)

            def finish(t):
                dve.wait_ge(s_t, t + 1)
                if t >= 2:
                    dve.wait_ge(s_lo, t - 1)
                    dve.wait_ge(s_hi, t - 1)
                nc.vector.tensor_tensor(xg[:, t % 2], turned[t % 2][:], gain[:].unsqueeze(2).to_broadcast([P, kt, P]),
                                        ALU.mult).then_inc(s_xg, 1)
                dve.wait_ge(s_hi, t + 1)
                nc.vector.tensor_tensor(out_hl[:, 1, :, t * P:(t + 1) * P], xg[:, t % 2],
                                        f32(out_hl[:, 0, :, t * P:(t + 1) * P]), ALU.subtract).then_inc(s_lo, 1)

            for t in range(tiles):
                if rowg is not None:
                    dve.wait_ge(s_std, NR * t + 1)
                    nc.vector.reciprocal(rstd[:, t:t + 1], std[:, t:t + 1]).then_inc(s_rs, 1)
                    dve.wait_ge(s_rs, NR * t + 1)
                    nc.vector.tensor_scalar(x_tm[:, t, :], x_tm[:, t, :], rstd[:, t:t + 1], None, ALU.mult).then_inc(s_x2, 1)
                    dve.wait_ge(s_x2, 2 * t + 1)
                    nc.vector.tensor_tensor(x_tm[:, t, :], x_tm[:, t, :], rowg[:], ALU.mult).then_inc(s_x2, 1)
                dve.wait_ge(s_std, NR * (t + 1))
                nc.vector.reciprocal(rstd[:, tiles + t:tiles + t + 1], std[:, tiles + t:tiles + t + 1]).then_inc(s_rs, 1)
                if t >= 2:
                    finish(t - 2)
            finish(tiles - 2)
            finish(tiles - 1)

        @block.tensor
        def _(pe):
            pe.wait_ge(s_id, 3)
            for t in range(tiles):
                pe.wait_ge(s_xn, t + 1)
                if t >= 2:
                    pe.wait_ge(s_xg, t - 1)
                for k in range(kt):
                    last = nc.tensor.transpose(turned[t % 2][:, k, :], xn[:, t % 2, k * P:(k + 1) * P], ident[:])
                last.then_inc(s_t, 1)


def mm3(nc, out, w_hl, x_hl, first, last):
    nc.tensor.matmul(out, w_hl[0], x_hl[0], start=first, stop=False)
    nc.tensor.matmul(out, w_hl[0], x_hl[1], start=False, stop=False)
    return nc.tensor.matmul(out, w_hl[1], x_hl[0], start=False, stop=last)


def first_mixers(nc, A, h_hl, scr):
    S, D = A.x.shape[1], A.x.shape[2]
    KT, FT, HALF = D // P, D // P, S // 2
    C_A, X_A, B_A, X_B, G_B, GATE_A, GATE_B = 1, 2, 0, 3, 4, 5, 6
    ORDER = [C_A, X_A, B_A, X_B, G_B, GATE_A, GATE_B]
    NJ = len(ORDER)
    SLOT = [0, 1, 2, 0, 1, 2, 1]
    USES = [SLOT.count(s) for s in range(3)]
    ORD = [SLOT[:j].count(SLOT[j]) for j in range(NJ)]
    BACK = [next(b for b in range(1, 2 * NJ) if SLOT[(j - b) % NJ] == SLOT[j]) for j in range(NJ)]
    with ExitStack() as ctx:
        c = Core(nc, ctx)
        stage = c.sb("m1_stage", [P, 3, KT, P])
        w_hl = [c.sb(f"m1_w_hl{s}", [P, 2, KT, P], F32R) for s in range(3)]
        cw_a = c.sb("m1_conv_a_w", [P, FT, 3])
        cw_b = c.sb("m1_conv_b_w", [P, FT, 4])
        cols = c.sb("m1_cols", [P, 6, FT])
        CB, BA, BX, GA, GB, LAM = range(6)
        sp_t = c.sb("m1_softplus", [P, 6, FT])
        gate_w = c.sb("m1_gate_w", [P, 2, P])
        ca = c.sb("m1_ca", [P, S])
        cx = c.sb("m1_cx", [P, S + 2])
        acc = c.sb("m1_acc", [P, S])
        ya = c.sb("m1_ya", [P, S])
        xb = c.sb("m1_xb", [P, S + 3])
        u = c.sb("m1_u", [P, S])
        r = c.sb("m1_r", [P, S])
        gi = c.sb("m1_i", [P, S])
        a = c.sb("m1_a", [P, S])
        th = c.sb("m1_t", [P, S])
        g = c.sb("m1_g", [P, S])
        yb = c.sb("m1_yb", [P, S])
        sg = c.sb("m1_sg", [P, 2, S])
        ps = [c.ps(f"m1_ps{s}", [P, 2, HALF]) for s in range(3)]
        ps_g = c.ps("m1_ps_gate", [P, 2, HALF])
        loaded = c.sems("m1_w_loaded", 3)
        s_hi, s_lo, s_mm = c.sem("m1_w_high"), c.sem("m1_w_low"), c.sem("m1_products")
        s_par, s_zero, s_dv, s_spe = c.sem("m1_params"), c.sem("m1_zeroed"), c.sem("m1_dve_chain"), c.sem("m1_sp_exp")
        s_spc = c.sem("m1_sp_chain")
        s_ca, s_cx, s_ya, s_yast = c.sem("m1_ca_ready"), c.sem("m1_cx_ready"), c.sem("m1_ya_ready"), c.sem("m1_ya_stored")
        s_xb, s_u, s_gw = c.sem("m1_xb_ready"), c.sem("m1_u_ready"), c.sem("m1_gate_w_loaded")
        s_rmm, s_r, s_imm, s_i = c.sem("m1_r_product"), c.sem("m1_r_ready"), c.sem("m1_i_product"), c.sem("m1_i_ready")
        s_at, s_g, s_scan, s_yb, s_ybst = (c.sem("m1_a_t_ready"), c.sem("m1_g_ready"), c.sem("m1_scanned"),
                                           c.sem("m1_yb_ready"), c.sem("m1_yb_stored"))
        s_sga, s_sgb, s_sgast, s_sgbst = (c.sem("m1_sga_ready"), c.sem("m1_sgb_ready"), c.sem("m1_sga_stored"),
                                          c.sem("m1_sgb_stored"))
        s_b, s_q, s_root = c.sem("m1_b_ready"), c.sem("m1_ratio_ready"), c.sem("m1_root_ready")
        block = ctx.enter_context(nc.Block())
        w_v = A.w_in[0].rearrange("(k p) (j f m) -> p k j f m", p=P, m=P, f=FT)

        @block.sync
        def _(sp):
            def step(i):
                for j, col in enumerate(ORDER):
                    t, s = NJ * i + j, SLOT[j]
                    wait(sp, s_lo, t - BACK[j] + 1)
                    sp.dma_start(stage[:, s], w_v[:, :, col, i, :]).then_inc(loaded[s], 16)
            for i in range(FT):
                step(i)

        @block.gpsimd
        def _(pool):
            nc.gpsimd.memset(gate_w[:], 0.0).then_inc(s_zero, 1)
            nc.gpsimd.memset(cx[:, 0:2], 0.0).then_inc(s_zero, 1)
            nc.gpsimd.memset(xb[:, 0:3], 0.0).then_inc(s_zero, 1)
            pool.wait_ge(s_zero, 3)
            with nc.allow_non_contiguous_dma(reason="per-channel constants as columns"):
                for k in range(3):
                    pool.dma_start(cw_a[:, :, k], A.conv_a_w[0, k].rearrange("(f p) -> p f", p=P)).then_inc(s_par, 16)
                for k in range(4):
                    pool.dma_start(cw_b[:, :, k], A.conv_b_w[0, k].rearrange("(f p) -> p f", p=P)).then_inc(s_par, 16)
                for n, row in enumerate([A.conv_b_b[0], A.lru_ba[0], A.lru_bx[0], A.gate_bias[0, 0], A.gate_bias[0, 1],
                                         A.lru_lambda[0]]):
                    pool.dma_start(cols[:, n, :], row.rearrange("(f p) -> p f", p=P)).then_inc(s_par, 16)

            def step(i):
                wait(pool, s_imm, i)
                for n, w in enumerate([A.lru_wa, A.lru_wx]):
                    for b in range(2):
                        pool.dma_start(gate_w[64 * b:64 * b + 64, n, 64 * b:64 * b + 64],
                                       w[0].rearrange("(f b) d e -> f b d e", b=2)[i, b]).then_inc(s_gw, 16)
                pool.wait_ge(s_ya, i + 1)
                pool.dma_start(scr.ya[i], ya[:]).then_inc(s_yast, 16)
                pool.wait_ge(s_sga, i + 1)
                pool.dma_start(scr.sga[i], sg[:, 0]).then_inc(s_sgast, 16)
                pool.wait_ge(s_sgb, i + 1)
                pool.dma_start(scr.sgb[i], sg[:, 1]).then_inc(s_sgbst, 16)
                pool.wait_ge(s_yb, i + 1)
                pool.dma_start(scr.yb[i], yb[:]).then_inc(s_ybst, 16)
            for i in range(FT):
                step(i)
            for s in (s_yast, s_sgast, s_sgbst, s_ybst):
                pool.wait_ge(s, 16 * FT)

        NP_DMAS = 13

        @block.scalar
        def _(act):
            act.wait_ge(s_spc, 1)
            nc.scalar.activation(sp_t[:, 1], sp_t[:, 0], ACT.Exp, scale=-1.0).then_inc(s_spe, 1)

            def split(i, j):
                t, s = NJ * i + j, SLOT[j]
                act.wait_ge(loaded[s], 16 * (USES[s] * i + ORD[j] + 1))
                wait(act, s_mm, t - BACK[j] + 1)
                nc.scalar.activation(w_hl[s][:, 0], stage[:, s], ACT.Copy).then_inc(s_hi, 1)

            def after(i, j):
                s = SLOT[j]
                pair = ps[s][:].rearrange("p h n -> p (h n)")
                if ORDER[j] == C_A:
                    act.wait_ge(s_mm, NJ * i + j + 1)
                    wait(act, s_cx, i)
                    nc.scalar.activation(ca[:], pair, ACT.Copy).then_inc(s_ca, 1)
                elif ORDER[j] == X_B:
                    act.wait_ge(s_mm, NJ * i + j + 1)
                    wait(act, s_u, i)
                    act.wait_ge(s_zero, 3)
                    nc.scalar.activation(xb[:, 3:S + 3], pair, ACT.Copy).then_inc(s_xb, 1)
                elif ORDER[j] == G_B:
                    act.wait_ge(s_mm, NJ * i + j + 1)
                    wait(act, s_yb, i)
                    nc.scalar.activation(g[:], pair, ACT.Gelu_apprx_tanh).then_inc(s_g, 1)
                elif ORDER[j] == GATE_A:
                    act.wait_ge(s_rmm, i + 1)
                    wait(act, s_at, 2 * i)
                    nc.scalar.activation(r[:], ps_g[:].rearrange("p h n -> p (h n)"), ACT.Sigmoid,
                                         bias=cols[:, BA, bass.ds(i, 1)]).then_inc(s_r, 1)
                    act.wait_ge(s_mm, NJ * i + j + 1)
                    wait(act, s_sgast, 16 * i)
                    nc.scalar.activation(sg[:, 0], pair, ACT.Sigmoid, bias=cols[:, GA, bass.ds(i, 1)]).then_inc(s_sga, 1)
                elif ORDER[j] == GATE_B:
                    act.wait_ge(s_mm, NJ * i + j + 1)
                    wait(act, s_sgbst, 16 * i)
                    nc.scalar.activation(sg[:, 1], pair, ACT.Sigmoid, bias=cols[:, GB, bass.ds(i, 1)]).then_inc(s_sgb, 1)
                    act.wait_ge(s_imm, i + 1)
                    wait(act, s_scan, i)
                    nc.scalar.activation(gi[:], ps_g[:].rearrange("p h n -> p (h n)"), ACT.Sigmoid,
                                         bias=cols[:, BX, bass.ds(i, 1)]).then_inc(s_i, 1)
                    act.wait_ge(s_r, i + 1)
                    nc.scalar.activation(a[:], r[:], ACT.Exp, scale=sp_t[:, 4, bass.ds(i, 1)]).then_inc(s_at, 1)
                    nc.scalar.activation(th[:], r[:], ACT.Tanh, scale=sp_t[:, 5, bass.ds(i, 1)]).then_inc(s_at, 1)
                    act.wait_ge(s_q, i + 1)
                    nc.scalar.activation(th[:], th[:], ACT.Sqrt, scale=2.0).then_inc(s_root, 1)

            def step(i):
                for j in range(NJ):
                    split(i, j)
                    if j >= 2:
                        after(i, j - 2)
                    elif not (isinstance(i, int) and i == 0):
                        after(i - 1, j - 2 + NJ)
                    elif j == 0:
                        act.wait_ge(s_par, 16 * NP_DMAS)
                        act.wait_ge(s_spc, SPC)

            SPC = 20
            steps(act, FT, step)
            after(FT - 1, NJ - 2)
            after(FT - 1, NJ - 1)

        @block.vector
        def _(dve):
            c0 = Chain(dve, s_spc)
            v = nc.vector
            dve.wait_ge(s_par, 16 * NP_DMAS)
            c0.link(v.scalar_tensor_tensor(sp_t[:, 0], cols[:, LAM], -1.0, cols[:, LAM], ALU.mult, ALU.max))
            dve.wait_ge(s_spe, 1)
            log1p_exp_neg(nc, c0, sp_t[:, 1], sp_t[:, 2], sp_t[:, 3], sp_t[:, 5])
            c0.link(v.tensor_scalar(sp_t[:, 0], cols[:, LAM], -1.0, 0.0, ALU.mult, ALU.max))
            c0.link(v.tensor_tensor(sp_t[:, 5], sp_t[:, 5], sp_t[:, 0], ALU.add))
            c0.link(v.tensor_scalar(sp_t[:, 4], sp_t[:, 5], -8.0, None, ALU.mult))
            c0.link(v.tensor_scalar(sp_t[:, 5], sp_t[:, 5], 8.0, None, ALU.mult))
            chain = Chain(dve, s_dv, 9)

            def split(i, j):
                s = SLOT[j]
                dve.wait_ge(s_hi, NJ * i + j + 1)
                v.tensor_tensor(w_hl[s][:, 1], stage[:, s], f32(w_hl[s][:, 0]), ALU.subtract).then_inc(s_lo, 1)

            def after(i, j):
                s = SLOT[j]
                pair = ps[s][:].rearrange("p h n -> p (h n)")
                w = lambda t, k: t[:, bass.ds(i, 1), k:k + 1].rearrange("p a b -> p (a b)")
                if ORDER[j] == X_A:
                    chain.start(i)
                    dve.wait_ge(s_mm, NJ * i + j + 1)
                    dve.wait_ge(s_ca, i + 1)
                    v.tensor_tensor(cx[:, 2:S + 2], ca[:], pair, ALU.mult).then_inc(s_cx, 1)
                    dve.wait_ge(s_cx, i + 1)
                    chain.link(v.tensor_scalar(acc[:], cx[:, 0:S], w(cw_a, 0), None, ALU.mult))
                    chain.link(v.scalar_tensor_tensor(acc[:], cx[:, 1:S + 1], w(cw_a, 1), acc[:], ALU.mult, ALU.add))
                    chain.link(v.scalar_tensor_tensor(acc[:], cx[:, 2:S + 2], w(cw_a, 2), acc[:], ALU.mult, ALU.add))
                elif ORDER[j] == B_A:
                    dve.wait_ge(s_mm, NJ * i + j + 1)
                    wait(dve, s_yast, 16 * i)
                    v.tensor_tensor(ya[:], acc[:], pair, ALU.mult).then_inc(s_ya, 1)
                elif ORDER[j] == X_B:
                    dve.wait_ge(s_xb, i + 1)
                    chain.link(v.tensor_scalar(u[:], xb[:, 0:S], w(cw_b, 0), cols[:, CB, bass.ds(i, 1)], ALU.mult, ALU.add))
                    for k in (1, 2):
                        chain.link(v.scalar_tensor_tensor(u[:], xb[:, k:S + k], w(cw_b, k), u[:], ALU.mult, ALU.add))
                    v.scalar_tensor_tensor(u[:], xb[:, 3:S + 3], w(cw_b, 3), u[:], ALU.mult, ALU.add).then_inc(s_u, 1)
                elif ORDER[j] == GATE_B:
                    chain.start(i, 6)
                    dve.wait_ge(s_at, 2 * i + 2)
                    dve.wait_ge(s_i, i + 1)
                    chain.link(v.tensor_scalar(acc[:], th[:], 1.0, None, ALU.add))
                    chain.inc(v.tensor_tensor(gi[:], gi[:], u[:], ALU.mult))
                    chain.link(v.reciprocal(acc[:], acc[:]))
                    v.tensor_tensor(th[:], th[:], acc[:], ALU.mult).then_inc(s_q, 1)
                    dve.wait_ge(s_root, i + 1)
                    v.tensor_tensor(th[:], th[:], gi[:], ALU.mult).then_inc(s_b, 1)
                    dve.wait_ge(s_b, i + 1)
                    v.tensor_tensor_scan(acc[:], a[:], th[:], 0.0, ALU.mult, ALU.add).then_inc(s_scan, 1)
                    dve.wait_ge(s_scan, i + 1)
                    dve.wait_ge(s_g, i + 1)
                    wait(dve, s_ybst, 16 * i)
                    v.tensor_tensor(yb[:], acc[:], g[:], ALU.mult).then_inc(s_yb, 1)
                    chain.end()

            def step(i):
                for j in range(NJ):
                    split(i, j)
                    if j >= 2:
                        after(i, j - 2)
                    elif not (isinstance(i, int) and i == 0):
                        after(i - 1, j - 2 + NJ)
            steps(dve, FT, step)
            after(FT - 1, NJ - 2)
            after(FT - 1, NJ - 1)

        @block.tensor
        def _(pe):
            def gate(i, n, done, prev, prev_value):
                wait(pe, prev, prev_value)
                for h in range(2):
                    last = nc.tensor.matmul(ps_g[:, h], gate_w[:, n], u[:, h * HALF:(h + 1) * HALF], start=True, stop=True)
                last.then_inc(done, 1)

            def step(i):
                for j in range(NJ):
                    s = SLOT[j]
                    pe.wait_ge(s_lo, NJ * i + j + 1)
                    prev, pi = (j - BACK[j], i) if j >= BACK[j] else (j - BACK[j] + NJ, i - 1)
                    if not (isinstance(pi, int) and pi < 0):
                        sem, per_step = {C_A: (s_ca, 1), X_A: (s_cx, 1), B_A: (s_ya, 1), X_B: (s_xb, 1), G_B: (s_g, 1),
                                         GATE_A: (s_sga, 1), GATE_B: (s_sgb, 1)}[ORDER[prev]]
                        wait(pe, sem, pi + 1)
                    for k in range(KT):
                        for h in range(2):
                            last = mm3(nc, ps[s][:, h], (w_hl[s][:, 0, k], w_hl[s][:, 1, k]),
                                       (h_hl[:, 0, k, h * HALF:(h + 1) * HALF], h_hl[:, 1, k, h * HALF:(h + 1) * HALF]),
                                       k == 0, k == KT - 1)
                    last.then_inc(s_mm, 1)
                    if ORDER[j] == G_B:
                        pe.wait_ge(s_u, i + 1)
                        pe.wait_ge(s_gw, 64 * (i + 1))
                        gate(i, 0, s_rmm, s_i, i)
                    if ORDER[j] == GATE_A:
                        gate(i, 1, s_imm, s_r, i + 1)
            steps(pe, FT, step)


def merge_mixers(nc, A, scr, hl):
    S, D = A.x.shape[1], A.x.shape[2]
    KT, HALF = D // P, S // 2
    with ExitStack() as ctx:
        c = Core(nc, ctx)
        yb_hl = c.sb("mg_yb_hl", [P, 2, KT, S], F32R)
        ystage = c.sb("mg_y_stage", [P, 2, S])
        sg = c.sb("mg_sg", [P, 2, S])
        part = c.sb("mg_part", [P, KT, S])
        tmp = c.sb("mg_tmp", [P, 1, S])
        stage = c.sb("mg_stage", [P, 2, KT, P])
        w_hl = [c.sb(f"mg_w_hl{s}", [P, 2, KT, P], F32R) for s in range(2)]
        ps = [c.ps(f"mg_ps{s}", [P, 2, HALF]) for s in range(2)]
        y_in, w_in, g_in = c.sems("mg_y_loaded", 2), c.sems("mg_w_loaded", 2), c.sems("mg_sg_loaded", 2)
        s_yh, s_yl, s_wh, s_wl = c.sem("mg_y_high"), c.sem("mg_y_low"), c.sem("mg_w_high"), c.sem("mg_w_low")
        s_mm, s_read, s_sum, s_mh, s_ml, s_tmp = (c.sem("mg_products"), c.sem("mg_gated"), c.sem("mg_summed"),
                                                  c.sem("mg_high"), c.sem("mg_low"), c.sem("mg_tmp"))
        block = ctx.enter_context(nc.Block())
        w_v = [w[0].rearrange("(k p) (m n) -> p k m n", p=P, n=P) for w in (A.w_out_a, A.w_out_b)]
        ysplit = [(hl, k) for k in range(KT)] + [(yb_hl, k) for k in range(KT)]

        @block.sync
        def _(sp):
            def load_w(q, m, j):
                t = KT * q + m
                wait(sp, s_wl, t - 1)
                sp.dma_start(stage[:, j], w_v[q][:, :, m, :]).then_inc(w_in[j], 16)

            load_w(0, 0, 0)
            load_w(0, 1, 1)
            for n in range(2, KT * 2):
                q, m = divmod(n, KT)
                load_w(q, m, n % 2)

        @block.gpsimd
        def _(pool):
            for n in range(2 * KT):
                wait(pool, s_yl, n - 1)
                pool.dma_start(ystage[:, n % 2], (scr.ya if n < KT else scr.yb)[n % KT]).then_inc(y_in[n % 2], 16)
            for n in range(2 * KT):
                wait(pool, s_read, n - 1)
                pool.dma_start(sg[:, n % 2], (scr.sga if n < KT else scr.sgb)[n % KT]).then_inc(g_in[n % 2], 16)

        @block.scalar
        def _(act):
            def y_high(n):
                dst, k = ysplit[n]
                act.wait_ge(y_in[n % 2], 16 * (n // 2 + 1))
                nc.scalar.activation(dst[:, 0, k], ystage[:, n % 2], ACT.Copy).then_inc(s_yh, 1)

            def w_high(t):
                act.wait_ge(w_in[t % 2], 16 * (t // 2 + 1))
                wait(act, s_mm, t - 1)
                nc.scalar.activation(w_hl[t % 2][:, 0], stage[:, t % 2], ACT.Copy).then_inc(s_wh, 1)

            w_high(0)
            for n in range(KT):
                y_high(n)
            w_high(1)
            for n in range(KT, 2 * KT):
                y_high(n)
            for t in range(2, 2 * KT):
                w_high(t)
                if t > KT + 1:
                    m = t - 2 - KT
                    act.wait_ge(s_sum, m + 1)
                    nc.scalar.activation(hl[:, 0, m], part[:, m], ACT.Copy).then_inc(s_mh, 1)
            for m in range(KT - 2, KT):
                act.wait_ge(s_sum, m + 1)
                nc.scalar.activation(hl[:, 0, m], part[:, m], ACT.Copy).then_inc(s_mh, 1)

        @block.vector
        def _(dve):
            v = nc.vector

            def y_low(n):
                dst, k = ysplit[n]
                dve.wait_ge(s_yh, n + 1)
                v.tensor_tensor(dst[:, 1, k], ystage[:, n % 2], f32(dst[:, 0, k]), ALU.subtract).then_inc(s_yl, 1)

            def w_low(t):
                dve.wait_ge(s_wh, t + 1)
                v.tensor_tensor(w_hl[t % 2][:, 1], stage[:, t % 2], f32(w_hl[t % 2][:, 0]), ALU.subtract).then_inc(s_wl, 1)

            def gate(t):
                m = t % KT
                pair = ps[t % 2][:].rearrange("p h n -> p (h n)")
                dve.wait_ge(s_mm, t + 1)
                dve.wait_ge(g_in[t % 2], 16 * (t // 2 + 1))
                if t < KT:
                    v.tensor_tensor(part[:, m], sg[:, t % 2], pair, ALU.mult).then_inc(s_read, 1)
                    return
                wait(dve, s_sum, m)
                v.tensor_tensor(tmp[:, 0], sg[:, t % 2], pair, ALU.mult).then_inc(s_read, 1)
                dve.wait_ge(s_read, t + 1)
                v.tensor_tensor(part[:, m], part[:, m], tmp[:, 0], ALU.add).then_inc(s_sum, 1)

            def low(m):
                dve.wait_ge(s_mh, m + 1)
                v.tensor_tensor(hl[:, 1, m], part[:, m], f32(hl[:, 0, m]), ALU.subtract).then_inc(s_ml, 1)

            w_low(0)
            for n in range(KT):
                y_low(n)
            w_low(1)
            for n in range(KT, 2 * KT):
                y_low(n)
            for t in range(2 * KT):
                gate(t)
                if t + 2 < 2 * KT:
                    w_low(t + 2)
                if t > KT:
                    low(t - 1 - KT)
            low(KT - 1)

        @block.tensor
        def _(pe):
            for t in range(2 * KT):
                pe.wait_ge(s_wl, t + 1)
                wait(pe, s_read, t - 1)
                x_hl = hl if t < KT else yb_hl
                for k in range(KT):
                    if t % KT == 0:
                        pe.wait_ge(s_yl, (t // KT) * KT + k + 1)
                    for h in range(2):
                        last = mm3(nc, ps[t % 2][:, h], (w_hl[t % 2][:, 0, k], w_hl[t % 2][:, 1, k]),
                                   (x_hl[:, 0, k, h * HALF:(h + 1) * HALF], x_hl[:, 1, k, h * HALF:(h + 1) * HALF]),
                                   k == 0, k == KT - 1)
                last.then_inc(s_mm, 1)


def add_product(nc, tag, x_tm, parts, w_v, x_dram=None):
    tiles, D = x_tm.shape[1], x_tm.shape[2]
    HALF = D // 2
    ks = [(hl, k) for hl, n in parts for k in range(n)]
    K = len(ks)
    NB, NS = 4, 4
    with ExitStack() as ctx:
        c = Core(nc, ctx)
        stage = c.sb(f"{tag}_stage", [P, NS, HALF])
        whole = K <= 8
        w_hl = [c.sb(f"{tag}_w_hl{h}", [P, 2, K, HALF], F32R) for h in range(2 if whole else 1)]
        ps = [c.ps(f"{tag}_ps{b}", [P, HALF]) for b in range(NB)]
        s_w, s_x = c.sems(f"{tag}_w_loaded", NS), c.sem(f"{tag}_x_loaded")
        s_hi, s_lo, s_mm, s_add = c.sem(f"{tag}_w_high"), c.sem(f"{tag}_w_low"), c.sem(f"{tag}_products"), c.sem(f"{tag}_added")
        block = ctx.enter_context(nc.Block())

        @block.sync
        def _(sp):
            for n in range(2 * K):
                h, k = divmod(n, K)
                wait(sp, s_lo, n - NS + 1)
                sp.dma_start(stage[:, n % NS], w_v[:, k, h * HALF:(h + 1) * HALF]).then_inc(s_w[n % NS], 16)

        @block.gpsimd
        def _(pool):
            if x_dram is not None:
                pool.dma_start(x_tm[:], x_dram.rearrange("(t p) d -> p t d", p=P)).then_inc(s_x, 16)
                pool.wait_ge(s_x, 16)

        @block.scalar
        def _(act):
            for n in range(2 * K):
                h, k = divmod(n, K)
                act.wait_ge(s_w[n % NS], 16 * (n // NS + 1))
                if h and not whole:
                    act.wait_ge(s_mm, tiles)
                nc.scalar.activation(w_hl[h % len(w_hl)][:, 0, k], stage[:, n % NS], ACT.Copy).then_inc(s_hi, 1)

        @block.vector
        def _(dve):
            def low(n):
                h, k = divmod(n, K)
                dve.wait_ge(s_hi, n + 1)
                w = w_hl[h % len(w_hl)]
                nc.vector.tensor_tensor(w[:, 1, k], stage[:, n % NS], f32(w[:, 0, k]), ALU.subtract).then_inc(s_lo, 1)

            def add(g):
                h, t = divmod(g, tiles)
                dve.wait_ge(s_mm, g + 1)
                dst = x_tm[:, t, h * HALF:(h + 1) * HALF]
                nc.vector.tensor_tensor(dst, dst, ps[g % NB][:], ALU.add).then_inc(s_add, 1)

            for n in range(K):
                low(n)
            if x_dram is not None:
                dve.wait_ge(s_x, 16)
            if whole:
                for g in range(tiles):
                    add(g)
                    low(K + g)
            else:
                for g in range(tiles):
                    add(g)
                for n in range(K, 2 * K):
                    low(n)
            for g in range(tiles, 2 * tiles):
                add(g)

        @block.tensor
        def _(pe):
            for g in range(2 * tiles):
                h, t = divmod(g, tiles)
                wait(pe, s_add, g - NB + 1)
                w = w_hl[h % len(w_hl)]
                for n, (hl, k) in enumerate(ks):
                    if t == 0:
                        pe.wait_ge(s_lo, h * K + n + 1)
                    tok = slice(t * P, (t + 1) * P)
                    last = mm3(nc, ps[g % NB][:], (hl[:, 0, k, tok], hl[:, 1, k, tok]), (w[:, 0, n], w[:, 1, n]),
                               n == 0, n == K - 1)
                last.then_inc(s_mm, 1)


def feed_forward(nc, A, x_tm, hl):
    tiles, D = x_tm.shape[1], x_tm.shape[2]
    S = tiles * P
    KT, HALF = D // P, 512
    NF = A.w_ffn_gate.shape[2] // P
    assert NF % 2 == 0
    ND = 2 * tiles
    NB = 4
    with ExitStack() as ctx:
        c = Core(nc, ctx)
        st = c.sb("ff_stage", [P, 3, S])
        wg_hl = [[c.sb(f"ff_w{n}{b}", [P, 2, KT, P], F32R) for b in range(2)] for n in "gu"]
        wd_hl = [c.sb(f"ff_wd{b}", [P, 2, D], F32R) for b in range(2)]
        silu = c.sb("ff_silu", [P, S])
        act_f = c.sb("ff_act", [P, S])
        a_hl = [c.sb(f"ff_act_hl{b}", [P, 2, S], F32R) for b in range(2)]
        ps_gu = [c.ps(f"ff_ps{n}", [P, 2, HALF]) for n in "gu"]
        ps_d = [c.ps(f"ff_psd{b}", [P, HALF]) for b in range(NB)]
        w_in = c.sems("ff_w_loaded", 3)
        s_hi, s_lo = c.sems("ff_w_high", 3), c.sems("ff_w_low", 3)
        s_g, s_u, s_d, s_down = c.sem("ff_gate_done"), c.sem("ff_up_done"), c.sem("ff_piece_done"), c.sem("ff_down_done")
        s_silu, s_act, s_ah, s_al, s_add = (c.sem("ff_silu_ready"), c.sem("ff_act_ready"), c.sem("ff_act_high"),
                                            c.sem("ff_act_low"), c.sem("ff_added"))
        block = ctx.enter_context(nc.Block())
        w_v = [w[0].rearrange("(k p) (f m) -> p k f m", p=P, m=P) for w in (A.w_ffn_gate, A.w_ffn_up)]
        wd_v = A.w_ffn_down[0].rearrange("(f p) n -> p f n", p=P)
        stage2 = [st[:, n].rearrange("p (k m) -> p k m", m=P) for n in range(2)]

        @block.sync
        def _(sp):
            def step(i):
                for b in range(2):
                    f = 2 * i + b
                    for n in range(2):
                        wait(sp, s_lo[n], f)
                        sp.dma_start(stage2[n], w_v[n][:, :, f, :]).then_inc(w_in[n], 16)
                    wait(sp, s_lo[2], f)
                    sp.dma_start(st[:, 2], wd_v[:, f, :]).then_inc(w_in[2], 16)
            for i in range(NF // 2):
                step(i)

        @block.scalar
        def _(act):
            def high(n, f, b):
                act.wait_ge(w_in[n], 16 * (f + 1))
                wait(act, (s_g, s_u, s_down)[n], f - 1)
                if n < 2:
                    nc.scalar.activation(wg_hl[n][b][:, 0], stage2[n], ACT.Copy).then_inc(s_hi[n], 1)
                else:
                    nc.scalar.activation(wd_hl[b][:, 0], st[:, 2], ACT.Copy).then_inc(s_hi[2], 1)

            def step(i, last=False):
                for b in range(2):
                    f = 2 * i + b
                    if isinstance(i, int) and i == 0 and b == 0:
                        high(0, 0, 0)
                        high(1, 0, 0)
                    if not (last and b == 1):
                        high(0, f + 1, 1 - b)
                        high(1, f + 1, 1 - b)
                    high(2, f, b)
                    act.wait_ge(s_g, f + 1)
                    wait(act, s_act, f)
                    nc.scalar.activation(silu[:], ps_gu[0][:].rearrange("p h n -> p (h n)"), ACT.Silu).then_inc(s_silu, 1)
                    act.wait_ge(s_act, f + 1)
                    wait(act, s_down, f - 1)
                    nc.scalar.activation(a_hl[b][:, 0], act_f[:], ACT.Copy).then_inc(s_ah, 1)
            steps(act, NF // 2, step, end=NF // 2 - 1)
            step(NF // 2 - 1, True)

        @block.vector
        def _(dve):
            v = nc.vector

            def low(n, f, b):
                dve.wait_ge(s_hi[n], f + 1)
                if n < 2:
                    v.tensor_tensor(wg_hl[n][b][:, 1], stage2[n], f32(wg_hl[n][b][:, 0]), ALU.subtract).then_inc(s_lo[n], 1)
                else:
                    v.tensor_tensor(wd_hl[b][:, 1], st[:, 2], f32(wd_hl[b][:, 0]), ALU.subtract).then_inc(s_lo[2], 1)

            def add_down(f):
                for g in range(ND):
                    t, h = divmod(g, 2)
                    dve.wait_ge(s_d, ND * f + g + 1)
                    dst = x_tm[:, t, h * HALF:(h + 1) * HALF]
                    v.tensor_tensor(dst, dst, ps_d[g % NB][:], ALU.add).then_inc(s_add, 1)

            def step(i, last=False):
                for b in range(2):
                    f = 2 * i + b
                    if isinstance(i, int) and i == 0 and b == 0:
                        low(0, 0, 0)
                        low(1, 0, 0)
                    if not (last and b == 1):
                        low(0, f + 1, 1 - b)
                        low(1, f + 1, 1 - b)
                    low(2, f, b)
                    if not (isinstance(i, int) and i == 0 and b == 0):
                        add_down(f - 1)
                    dve.wait_ge(s_u, f + 1)
                    dve.wait_ge(s_silu, f + 1)
                    wait(dve, s_ah, f)
                    wait(dve, s_al, f)
                    v.tensor_tensor(act_f[:], silu[:], ps_gu[1][:].rearrange("p h n -> p (h n)"), ALU.mult).then_inc(s_act, 1)
                    dve.wait_ge(s_ah, f + 1)
                    v.tensor_tensor(a_hl[b][:, 1], act_f[:], f32(a_hl[b][:, 0]), ALU.subtract).then_inc(s_al, 1)
            steps(dve, NF // 2, step, end=NF // 2 - 1)
            step(NF // 2 - 1, True)
            add_down(NF - 1)

        @block.tensor
        def _(pe):
            def down(f, b):
                pe.wait_ge(s_al, f + 1)
                pe.wait_ge(s_lo[2], f + 1)
                for g in range(ND):
                    t, h = divmod(g, 2)
                    tok = slice(t * P, (t + 1) * P)
                    cols = slice(h * HALF, (h + 1) * HALF)
                    wait(pe, s_add, ND * f + g - NB + 1)
                    last = mm3(nc, ps_d[g % NB][:], (a_hl[b][:, 0, tok], a_hl[b][:, 1, tok]),
                               (wd_hl[b][:, 0, cols], wd_hl[b][:, 1, cols]), True, True)
                    last.then_inc(s_d, 1)
                pe.wait_ge(s_d, ND * (f + 1))
                pe.sem_inc(s_down, 1)

            def step(i):
                for b in range(2):
                    f = 2 * i + b
                    for n, (read, done) in enumerate([(s_silu, s_g), (s_act, s_u)]):
                        pe.wait_ge(s_lo[n], f + 1)
                        wait(pe, read, f)
                        for k in range(KT):
                            for h in range(2):
                                last = mm3(nc, ps_gu[n][:, h], (wg_hl[n][b][:, 0, k], wg_hl[n][b][:, 1, k]),
                                           (hl[:, 0, k, h * HALF:(h + 1) * HALF], hl[:, 1, k, h * HALF:(h + 1) * HALF]),
                                           k == 0, k == KT - 1)
                        last.then_inc(done, 1)
                    if not (isinstance(i, int) and i == 0 and b == 0):
                        down(f - 1, 1 - b)
            steps(pe, NF // 2, step)
            down(NF - 1, 1)


def row_product(nc, tag, hl, w_v, out, func, gates=None):
    KT, S = hl.shape[2], hl.shape[3]
    tiles, HALF = S // P, 512
    NH = w_v.shape[2] // HALF
    NB, NS = 4, 4
    with ExitStack() as ctx:
        c = Core(nc, ctx)
        stage = c.sb(f"{tag}_stage", [P, NS, HALF])
        w_hl = [c.sb(f"{tag}_w_hl{h}", [P, 2, KT, HALF], F32R) for h in range(NH)]
        ps = [c.ps(f"{tag}_ps{b}", [P, HALF]) for b in range(NB)]
        s_w = c.sems(f"{tag}_w_loaded", NS)
        s_hi, s_lo, s_mm, s_out = c.sem(f"{tag}_w_high"), c.sem(f"{tag}_w_low"), c.sem(f"{tag}_products"), c.sem(f"{tag}_out")
        if gates is not None:
            NG = gates[0].shape[2]
            gstage = c.sb(f"{tag}_g_stage", [P, KT, NG])
            g_hl = c.sb(f"{tag}_g_hl", [P, 2, KT, NG], F32R)
            ps_g = c.ps(f"{tag}_ps_g", [P, tiles, NG])
            s_g = c.sem(f"{tag}_g_loaded")
            s_gh, s_gl, s_gm, s_go = c.sem(f"{tag}_g_high"), c.sem(f"{tag}_g_low"), c.sem(f"{tag}_g_products"), c.sem(f"{tag}_g_out")
        block = ctx.enter_context(nc.Block())

        @block.sync
        def _(sp):
            if gates is not None:
                with nc.allow_non_contiguous_dma(reason="a few gate columns"):
                    for src, off, n in gates[2]:
                        sp.dma_start(gstage[:, :, off:off + n], src).then_inc(s_g, 16)
            for n in range(NH * KT):
                h, k = divmod(n, KT)
                wait(sp, s_lo, n - NS + 1)
                sp.dma_start(stage[:, n % NS], w_v[:, k, h * HALF:(h + 1) * HALF]).then_inc(s_w[n % NS], 16)

        @block.scalar
        def _(act):
            def high(n):
                h, k = divmod(n, KT)
                act.wait_ge(s_w[n % NS], 16 * (n // NS + 1))
                nc.scalar.activation(w_hl[h][:, 0, k], stage[:, n % NS], ACT.Copy).then_inc(s_hi, 1)

            if gates is not None:
                act.wait_ge(s_g, 16 * len(gates[2]))
                nc.scalar.activation(g_hl[:, 0], gstage[:], ACT.Copy).then_inc(s_gh, 1)
            for n in range(KT):
                high(n)
            for g in range(NH * tiles):
                h, t = divmod(g, tiles)
                if h + 1 < NH:
                    high(KT * (h + 1) + t)
                act.wait_ge(s_mm, g + 1)
                if len(out.shape) == 3:
                    dst, src = out[:, t, h * HALF:(h + 1) * HALF], ps[g % NB][:]
                else:
                    dst = out[:, t, h * HALF // P:(h + 1) * HALF // P, 0:P]
                    src = ps[g % NB][:].rearrange("p (a b) -> p a b", b=P)
                nc.scalar.activation(dst, src, func).then_inc(s_out, 1)

        @block.vector
        def _(dve):
            if gates is not None:
                dve.wait_ge(s_gh, 1)
                nc.vector.tensor_tensor(g_hl[:, 1], gstage[:], f32(g_hl[:, 0]), ALU.subtract).then_inc(s_gl, 1)
            for n in range(NH * KT):
                h, k = divmod(n, KT)
                dve.wait_ge(s_hi, n + 1)
                nc.vector.tensor_tensor(w_hl[h][:, 1, k], stage[:, n % NS], f32(w_hl[h][:, 0, k]), ALU.subtract).then_inc(s_lo, 1)
                if n == 0 and gates is not None:
                    dve.wait_ge(s_gm, 1)
                    nc.vector.tensor_copy(gates[1][:], ps_g[:]).then_inc(s_go, 1)

        @block.tensor
        def _(pe):
            if gates is not None:
                pe.wait_ge(s_gl, 1)
                for t in range(tiles):
                    tok = slice(t * P, (t + 1) * P)
                    for k in range(KT):
                        last = mm3(nc, ps_g[:, t], (hl[:, 0, k, tok], hl[:, 1, k, tok]), (g_hl[:, 0, k], g_hl[:, 1, k]),
                                   k == 0, k == KT - 1)
                last.then_inc(s_gm, 1)
            for g in range(NH * tiles):
                h, t = divmod(g, tiles)
                tok = slice(t * P, (t + 1) * P)
                wait(pe, s_out, g - NB + 1)
                for k in range(KT):
                    if t == 0:
                        pe.wait_ge(s_lo, h * KT + k + 1)
                    last = mm3(nc, ps[g % NB][:], (hl[:, 0, k, tok], hl[:, 1, k, tok]), (w_hl[h][:, 0, k], w_hl[h][:, 1, k]),
                               k == 0, k == KT - 1)
                last.then_inc(s_mm, 1)


def column_product(nc, tag, hl, w_v, n, out=None, conv=None, gain=None, store=None):
    KT, S = hl.shape[2], hl.shape[3]
    HALF = S // 2
    assert n % 2 == 0
    with ExitStack() as ctx:
        c = Core(nc, ctx)
        stage = c.sb(f"{tag}_stage", [P, 2, KT, P])
        w_hl = [c.sb(f"{tag}_w_hl{b}", [P, 2, KT, P], F32R) for b in range(2)]
        ps = [c.ps(f"{tag}_ps{b}", [P, 2, HALF]) for b in range(2)]
        s_w = c.sems(f"{tag}_w_loaded", 2)
        s_hi, s_lo, s_mm, s_read = c.sem(f"{tag}_w_high"), c.sem(f"{tag}_w_low"), c.sem(f"{tag}_products"), c.sem(f"{tag}_psum_read")
        s_par, s_dv, s_res = c.sem(f"{tag}_params"), c.sem(f"{tag}_dve_chain"), c.sem(f"{tag}_result")
        s_fin, s_zero = c.sem(f"{tag}_finished"), c.sem(f"{tag}_zeroed")
        if conv is not None:
            K = conv[0].shape[0]
            xb = [c.sb(f"{tag}_x{b}", [P, S + K - 1]) for b in range(2)]
            u = [c.sb(f"{tag}_u{b}", [P, S]) for b in range(2)]
            cw = c.sb(f"{tag}_conv_w", [P, n, K])
            cb = c.sb(f"{tag}_conv_b", [P, n])
        else:
            res = c.sb(f"{tag}_res", [P, 2, S])
            cb = c.sb(f"{tag}_gain", [P, n])
            s_st = c.sem(f"{tag}_stored0"), c.sem(f"{tag}_stored1")
        block = ctx.enter_context(nc.Block())

        @block.sync
        def _(sp):
            for f in range(n):
                wait(sp, s_lo, f - 1)
                sp.dma_start(stage[:, f % 2], w_v[:, :, f, :]).then_inc(s_w[f % 2], 16)

        @block.gpsimd
        def _(pool):
            with nc.allow_non_contiguous_dma(reason="per-channel constants as columns"):
                pool.dma_start(cb[:], (conv[1] if conv is not None else gain).rearrange("(f p) -> p f", p=P)).then_inc(s_par, 16)
                if conv is not None:
                    for k in range(K):
                        pool.dma_start(cw[:, :, k], conv[0][k].rearrange("(f p) -> p f", p=P)).then_inc(s_par, 16)
                    for b in range(2):
                        nc.gpsimd.memset(xb[b][:, 0:K - 1], 0.0).then_inc(s_zero, 1)
            if store is not None:
                for f in range(n):
                    pool.wait_ge(s_fin, f + 1)
                    pool.dma_start(store[f], res[:, f % 2]).then_inc(s_st[f % 2], 16)
                for b in range(2):
                    pool.wait_ge(s_st[b], 16 * (n // 2))
        NPAR = 16 * (1 + K) if conv is not None else 16

        @block.scalar
        def _(act):
            def high(f, b):
                act.wait_ge(s_w[b], 16 * (f // 2 + 1) if isinstance(f, int) else 8 * f + 16 - 8 * b)
                wait(act, s_mm, f - 1)
                nc.scalar.activation(w_hl[b][:, 0], stage[:, b], ACT.Copy).then_inc(s_hi, 1)

            def read(f, b):
                pair = ps[b][:].rearrange("p h n -> p (h n)")
                act.wait_ge(s_mm, f + 1)
                if conv is not None:
                    wait(act, s_res, f - 1)
                    nc.scalar.activation(xb[b][:, K - 1:], pair, ACT.Copy).then_inc(s_read, 1)
                else:
                    for half in range(1):
                        if isinstance(f, int):
                            wait(act, s_st[b], 16 * (f // 2))
                        else:
                            act.wait_ge(s_st[b], 8 * f - 8 * b)
                    nc.scalar.activation(res[:, b], pair, ACT.Sigmoid).then_inc(s_read, 1)

            def finish(f, b):
                if conv is not None:
                    act.wait_ge(s_res, f + 1)
                    nc.scalar.activation(out[:, bass.ds(f, 1)].rearrange("p a s -> p (a s)"), u[b][:], ACT.Silu).then_inc(s_fin, 1)

            def step(i):
                first = isinstance(i, int) and i == 0
                for b in range(2):
                    f = 2 * i + b
                    high(f, b)
                    if not (first and b == 0):
                        read(f - 1, 1 - b)
                    if not first:
                        finish(f - 2, b)
            if conv is not None:
                act.wait_ge(s_zero, 2)
            steps(act, n // 2, step)
            read(n - 1, 1)
            finish(n - 2, 0)
            finish(n - 1, 1)

        @block.vector
        def _(dve):
            v = nc.vector
            chain = Chain(dve, s_dv, K - 1 if conv is not None else 0)

            def low(f, b):
                dve.wait_ge(s_hi, f + 1)
                v.tensor_tensor(w_hl[b][:, 1], stage[:, b], f32(w_hl[b][:, 0]), ALU.subtract).then_inc(s_lo, 1)

            def work(f, b):
                dve.wait_ge(s_read, f + 1)
                col = cb[:, bass.ds(f, 1)]
                if conv is None:
                    v.tensor_scalar(res[:, b], res[:, b], col, None, ALU.mult).then_inc(s_fin, 1)
                    return
                chain.start(f)
                wait(dve, s_fin, f - 1)
                w = lambda k: cw[:, bass.ds(f, 1), k:k + 1].rearrange("p a b -> p (a b)")
                chain.link(v.tensor_scalar(u[b][:], xb[b][:, 0:S], w(0), col, ALU.mult, ALU.add))
                for k in range(1, K - 1):
                    chain.link(v.scalar_tensor_tensor(u[b][:], xb[b][:, k:S + k], w(k), u[b][:], ALU.mult, ALU.add))
                v.scalar_tensor_tensor(u[b][:], xb[b][:, K - 1:], w(K - 1), u[b][:], ALU.mult, ALU.add).then_inc(s_res, 1)

            def step(i):
                first = isinstance(i, int) and i == 0
                for b in range(2):
                    low(2 * i + b, b)
                    if not (first and b == 0):
                        work(2 * i + b - 1, 1 - b)
            dve.wait_ge(s_par, NPAR)
            if conv is not None:
                dve.wait_ge(s_zero, 2)
            steps(dve, n // 2, step)
            work(n - 1, 1)

        @block.tensor
        def _(pe):
            def step(i):
                for b in range(2):
                    f = 2 * i + b
                    pe.wait_ge(s_lo, f + 1)
                    wait(pe, s_read, f - 1)
                    for k in range(KT):
                        for h in range(2):
                            last = mm3(nc, ps[b][:, h], (w_hl[b][:, 0, k], w_hl[b][:, 1, k]),
                                       (hl[:, 0, k, h * HALF:(h + 1) * HALF], hl[:, 1, k, h * HALF:(h + 1) * HALF]),
                                       k == 0, k == KT - 1)
                    last.then_inc(s_mm, 1)
            steps(pe, n // 2, step)


SSD_HEADS, SSD_GROUPS, ML_HEADS = 16, 2, 8


def gate_values(nc, A, gates, scr):
    tiles = gates.shape[1]
    S = tiles * P
    HS, HM = SSD_HEADS, ML_HEADS
    with ExitStack() as ctx:
        c = Core(nc, ctx)
        bias = c.sb("gv_bias", [P, HS + 2 * HM])
        alog = c.sb("gv_alog", [P, HS])
        sgn = c.sb("gv_x", [P, tiles, HS + HM])
        t1, t2, t3, t4 = (c.sb(f"gv_t{n}", [P, tiles, HS + HM]) for n in range(4))
        ident = c.sb("gv_ident", [P, P])
        rows = c.sb("gv_rows", [HM, 2, S])
        ones = c.sb("gv_ones", [HM, P])
        b_r, u_r = c.sb("gv_b", [HM, S]), c.sb("gv_u", [HM, S])
        m0 = c.sb("gv_m0", [HM, tiles + 1])
        e_in = c.sb("gv_e_in", [HM, 3, S])
        e_out = c.sb("gv_e_out", [HM, 3, S])
        ps_r = c.ps("gv_ps_rows", [HM, 2, S])
        ps_c = c.ps("gv_ps_cols", [P, tiles, 4, HM])
        s_in, s_id, s_ch, s_e = c.sem("gv_loaded"), c.sem("gv_ident_ready"), c.sem("gv_dve_chain"), c.sem("gv_exp")
        s_gate, s_t, s_er, s_t2 = c.sem("gv_gates_ready"), c.sem("gv_rows_turned"), c.sem("gv_rows_exp"), c.sem("gv_cols_turned")
        s_rows, s_fin = c.sem("gv_rows_ready"), c.sem("gv_finished")
        block = ctx.enter_context(nc.Block())

        @block.sync
        def _(sp):
            for row, off in ((A.ssd_dt_bias_2[0], 0), (A.ml_i_bias_2[0], HS), (A.ml_f_bias_2[0], HS + HM)):
                n = row.shape[0]
                sp.dma_start(bias[:, off:off + n], row.rearrange("(a n) -> a n", a=1).broadcast_to([P, n])).then_inc(s_in, 16)
            sp.dma_start(alog[:], A.ssd_a_log_2[0].rearrange("(a n) -> a n", a=1).broadcast_to([P, HS])).then_inc(s_in, 16)

        @block.gpsimd
        def _(pool):
            nc.gpsimd.memset(ones[:], 1.0).then_inc(s_id, 1)
            nc.gpsimd.memset(ident[:], 0.0).then_inc(s_id, 1)
            nc.gpsimd.memset(m0[:, 0:1], -1e30).then_inc(s_id, 1)
            pool.wait_ge(s_id, 3)
            nc.gpsimd.affine_select(out=ident[:], in_=ident[:], compare_op=ALU.not_equal, fill=1.0, base=0,
                                    pattern=[[-1, P]], channel_multiplier=1).then_inc(s_id, 1)

        @block.vector
        def _(dve):
            v, ch = nc.vector, Chain(dve, s_ch)
            dve.wait_ge(s_in, 64)
            dve.wait_ge(s_id, 4)
            wide = lambda ap: ap.unsqueeze(1).to_broadcast([P, tiles, ap.shape[1]])
            ch.link(v.tensor_tensor(gates[:], gates[:], wide(bias[:]), ALU.add))
            ch.inc(v.tensor_copy(sgn[:, :, 0:HS], gates[:, :, 0:HS]))
            ch.link(v.tensor_scalar(sgn[:, :, HS:], gates[:, :, HS + HM:], -1.0, None, ALU.mult))
            ch.link(v.scalar_tensor_tensor(t1[:], sgn[:], -1.0, sgn[:], ALU.mult, ALU.max))
            dve.wait_ge(s_e, 1)
            log1p_exp_neg(nc, ch, t1[:], t2[:], t3[:], t4[:])
            ch.link(v.scalar_tensor_tensor(t4[:], sgn[:], 0.0, t4[:], ALU.max, ALU.add))
            ch.inc(v.tensor_copy(scr.dt[:], t4[:, :, 0:HS]))
            dve.wait_ge(s_e, 2)
            ch.inc(v.scalar_tensor_tensor(scr.adt[:], t4[:, :, 0:HS], -1.0, wide(alog[:]), ALU.mult, ALU.mult))
            v.tensor_scalar(t4[:, :, HS:], t4[:, :, HS:], -1.0, None, ALU.mult).then_inc(s_gate, 1)
            dve.wait_ge(s_t, 1)
            ch.link(v.tensor_copy(rows[:], ps_r[:]))
            for k in range(tiles):
                cut = slice(k * P, (k + 1) * P)
                last = slice((k + 1) * P - 1, (k + 1) * P)
                ch.link(v.tensor_tensor_scan(b_r[:, cut], ones[:], rows[:, 1, cut], 0.0, ALU.mult, ALU.add))
                ch.link(v.tensor_tensor(u_r[:, cut], rows[:, 0, cut], b_r[:, cut], ALU.subtract))
                ch.link(v.tensor_tensor_scan(scr.g[:, cut], u_r[:, cut], u_r[:, cut], m0[:, k:k + 1], ALU.max, ALU.max))
                ch.inc(v.tensor_tensor(m0[:, k + 1:k + 2], b_r[:, last], scr.g[:, last], ALU.add))
                ch.inc(v.tensor_scalar(e_in[:, 0, cut], scr.g[:, cut], m0[:, k:k + 1], -1.0, ALU.subtract, ALU.mult))
                ch.inc(v.scalar_tensor_tensor(e_in[:, 1, cut], b_r[:, cut], -1.0, scr.g[:, cut], ALU.mult, ALU.subtract))
                ch.link(v.tensor_scalar(e_in[:, 2, cut], u_r[:, cut], scr.g[:, last], None, ALU.subtract))
            v.tensor_copy(rows[:, 0], u_r[:]).then_inc(s_rows, 1)
            dve.wait_ge(s_t2, 1)
            v.tensor_copy(scr.cols[:], ps_c[:]).then_inc(s_fin, 1)

        @block.scalar
        def _(act):
            act.wait_ge(s_ch, 4)
            nc.scalar.activation(t1[:], t1[:], ACT.Exp, scale=-1.0).then_inc(s_e, 1)
            act.wait_ge(s_in, 64)
            nc.scalar.activation(alog[:], alog[:], ACT.Exp).then_inc(s_e, 1)
            act.wait_ge(s_rows, 1)
            nc.scalar.activation(e_out[:], e_in[:], ACT.Exp).then_inc(s_er, 1)

        @block.tensor
        def _(pe):
            pe.wait_ge(s_id, 4)
            pe.wait_ge(s_gate, 1)
            for k in range(tiles):
                cut = slice(k * P, (k + 1) * P)
                nc.tensor.transpose(ps_r[:, 0, cut], gates[:, k, HS:HS + HM], ident[:])
                last = nc.tensor.transpose(ps_r[:, 1, cut], t4[:, k, HS:], ident[:])
            last.then_inc(s_t, 1)
            pe.wait_ge(s_er, 1)
            for k in range(tiles):
                cut = slice(k * P, (k + 1) * P)
                for n in range(4):
                    src = rows[:, 0, cut] if n == 0 else e_out[:, n - 1, cut]
                    last = nc.tensor.transpose(ps_c[:, k, n], src, ident[0:HM, 0:HM])
            last.then_inc(s_t2, 1)


def triangle(nc, pool, s_done, s_step, upper, neg):
    nc.gpsimd.memset(upper, 1.0).then_inc(s_step, 1)
    nc.gpsimd.memset(neg, 0.0).then_inc(s_step, 1)
    pool.wait_ge(s_step, 2)
    nc.gpsimd.affine_select(out=upper, in_=upper, compare_op=ALU.is_ge, fill=0.0, base=0, pattern=[[1, P]],
                            channel_multiplier=-1).then_inc(s_done, 1)
    nc.gpsimd.affine_select(out=neg, in_=neg, compare_op=ALU.is_ge, fill=-1e30, base=0,
                            pattern=[[0, neg.shape[1]], [1, P]], channel_multiplier=-1).then_inc(s_done, 1)


def identity(nc, pool, s_done, s_step, ident, steps_before=2):
    nc.gpsimd.memset(ident, 0.0).then_inc(s_step, 1)
    pool.wait_ge(s_step, steps_before + 1)
    nc.gpsimd.affine_select(out=ident, in_=ident, compare_op=ALU.not_equal, fill=1.0, base=0, pattern=[[-1, P]],
                            channel_multiplier=1).then_inc(s_done, 1)


def ssd_chunks(nc, A, xbc, z, scr):
    S = xbc.shape[2]
    NC, H, G, W = S // P, SSD_HEADS, SSD_GROUPS, 1024
    HG, HD, XT = H // G, W // H, W // P
    GW = W // G
    with ExitStack() as ctx:
        c = Core(nc, ctx)
        upper, neg, ident, ones = c.sb("sd_upper", [P, P]), c.sb("sd_neg", [P, 4, P]), c.sb("sd_ident", [P, P]), c.sb("sd_ones", [P, P])
        after = c.sb("sd_after", [P, P])
        d_row, norm, eps = c.sb("sd_d", [P, H]), c.sb("sd_norm", [P, XT]), c.sb("sd_eps", [P, 1])
        e3 = c.sb("sd_e3", [P, 3, H])
        nacs = c.sb("sd_neg_c", [P, H])
        x_r, xdt, xdec, xd = (c.sb(f"sd_{n}", [P, W]) for n in ("x", "xdt", "xdec", "xd"))
        b_r = c.sb("sd_b", [P, G, P])
        lt = c.sb("sd_l", [P, H, P])
        mt = lt
        state = c.sb("sd_state", [P, W])
        y, sq = c.sb("sd_y", [P, W]), c.sb("sd_sq", [P, W])
        ssq, std, rstd = c.sb("sd_ssq", [P, G]), c.sb("sd_std", [P, G]), c.sb("sd_rstd", [P, G])
        yt = c.sb("sd_yt", [P, XT, P])
        psA = c.ps("sd_psA", [P, 2, 512])
        psB = c.ps("sd_psB", [P, 2, 512])
        psC = c.ps("sd_psC", [P, 2, 512])
        psD = c.ps("sd_psD", [P, 512])
        psE = c.ps("sd_psE", [P, 512])
        cbt = psD[:, 0:G * P].rearrange("p (g n) -> p g n", g=G)
        sums = psD[:, G * P:G * P + 3 * H].rearrange("p (n h) -> p n h", n=3)
        (s_in, s_c0, s_c1, s_c2) = (c.sem(f"sd_{n}") for n in ("loaded", "const_steps", "consts", "ones_ready"))
        (p_row, p_turn, p_in, p_inter, p_state, p_out) = (
            c.sem(f"sd_pe_{n}") for n in ("rows", "turned", "intra", "inter", "state", "result"))
        (a_e, a_x, a_l, a_sq, a_std) = (c.sem(f"sd_act_{n}") for n in ("exps", "x", "decay", "squares", "std"))
        (d_xdt, d_m, d_y1, d_y, d_st1, d_st, d_ch, d_rs, d_n, d_yt) = (
            c.sem(f"sd_dve_{n}") for n in ("xdt", "m", "y1", "y", "state1", "state", "chain", "rstd", "normed", "yt"))
        (g_x, s_st) = (c.sem("sd_pool_x"), c.sem("sd_stored"))
        block = ctx.enter_context(nc.Block())
        heads = lambda ap: ap.rearrange("p (h d) -> p h d", d=HD)
        per_head = lambda ap: ap.unsqueeze(2).to_broadcast([P, H, HD])

        @block.sync
        def _(sp):
            sp.dma_start(d_row[:], A.ssd_d_2[0].rearrange("(a n) -> a n", a=1).broadcast_to([P, H])).then_inc(s_in, 16)
            with nc.allow_non_contiguous_dma(reason="gain column layout"):
                sp.dma_start(norm[:], A.ssd_norm_w_2[0].rearrange("(k p) -> p k", p=P)).then_inc(s_in, 16)
            for k in range(NC):
                sp.wait_ge(d_yt, k + 1)
                sp.dma_start(scr.y_ssd[:, :, k * P:(k + 1) * P].rearrange("f p s -> p f s"), yt[:]).then_inc(s_st, 16)
            sp.wait_ge(s_st, 16 * NC)

        @block.gpsimd
        def _(pool):
            triangle(nc, pool, s_c1, s_c0, upper[:], neg[:])
            identity(nc, pool, s_c1, s_c0, ident[:])
            nc.gpsimd.memset(ones[:], 1.0).then_inc(s_c1, 1)
            nc.gpsimd.memset(eps[:], EPS).then_inc(s_c1, 1)
            nc.gpsimd.memset(after[:], 1.0).then_inc(s_c2, 1)
            pool.wait_ge(s_c2, 1)
            nc.gpsimd.affine_select(out=after[:], in_=after[:], compare_op=ALU.is_gt, fill=0.0, base=0, pattern=[[-1, P]],
                                    channel_multiplier=1).then_inc(s_c1, 1)
            pool.wait_ge(s_in, 32)
            for k in range(NC):
                pool.wait_ge(a_x, k + 1)
                if k:
                    pool.wait_ge(d_y, k)
                nc.gpsimd.tensor_tensor(heads(xd[:]), heads(x_r[:]), per_head(d_row[:]), ALU.mult).then_inc(g_x, 1)

        @block.scalar
        def _(act):
            def front(k):
                act.wait_ge(p_turn, k + 1)
                if k:
                    act.wait_ge(d_st1, k)
                    act.wait_ge(d_y1, k)
                nc.scalar.activation(e3[:], sums, ACT.Exp)
                nc.scalar.activation(nacs[:], sums[:, 0], ACT.Copy, scale=-1.0).then_inc(a_e, 1)
                if k:
                    act.wait_ge(g_x, k)
                    act.wait_ge(d_xdt, k)
                    act.wait_ge(p_state, k)
                nc.scalar.activation(x_r[:], psB[:].rearrange("p a n -> p (a n)"), ACT.Copy)
                nc.scalar.activation(b_r[:].rearrange("p g n -> p (g n)"), psE[:, 0:G * P], ACT.Copy).then_inc(a_x, 1)
                act.wait_ge(a_e, k + 1)
                for g in range(G):
                    act.wait_ge(p_row, G * k + g + 1)
                    if k:
                        act.wait_ge(p_in, k)
                    for h in range(HG):
                        last = nc.scalar.activation(lt[:, g * HG + h], psA[:].rearrange("p a (h n) -> p (a h) n", n=P)[:, h],
                                                    ACT.Exp, bias=nacs[:, g * HG + h:g * HG + h + 1])
                    last.then_inc(a_l, 1)

            act.wait_ge(s_c1, 6)
            front(0)
            for k in range(NC):
                if k + 1 < NC:
                    front(k + 1)
                act.wait_ge(d_y, k + 1)
                for g in range(G):
                    cut = slice(g * GW, (g + 1) * GW)
                    nc.scalar.activation(sq[:, cut], y[:, cut], ACT.Square, accum_out=ssq[:, g:g + 1]).then_inc(a_sq, 1)
                act.wait_ge(a_sq, G * (k + 1))
                if k:
                    act.wait_ge(d_rs, k)
                nc.scalar.activation(std[:], ssq[:], ACT.Sqrt, scale=1.0 / GW, bias=eps[:]).then_inc(a_std, 1)

        @block.vector
        def _(dve):
            v, ch = nc.vector, Chain(dve, d_ch)

            def front(k):
                dve.wait_ge(a_x, k + 1)
                if k:
                    dve.wait_ge(p_in, k)
                    dve.wait_ge(p_state, k)
                ch.link(v.tensor_tensor(heads(xdt[:]), heads(x_r[:]), per_head(scr.dt[:, k]), ALU.mult))
                dve.wait_ge(a_e, k + 1)
                v.tensor_tensor(heads(xdec[:]), heads(xdt[:]), per_head(e3[:, 1]), ALU.mult).then_inc(d_xdt, 1)
                for g in range(G):
                    dve.wait_ge(a_l, G * k + g + 1)
                    m = mt[:, g * HG:(g + 1) * HG]
                    v.tensor_tensor(m, m, cbt[:, g].unsqueeze(1).to_broadcast([P, HG, P]), ALU.mult).then_inc(d_m, 1)

            dve.wait_ge(s_in, 32)
            dve.wait_ge(s_c1, 6)
            front(0)
            for k in range(NC):
                both = lambda ps: ps[:].rearrange("p a (h d) -> p (a h) d", d=HD)
                if k:
                    dve.wait_ge(p_inter, k + 1)
                    v.tensor_tensor(heads(y[:]), both(psC), per_head(e3[:, 0]), ALU.mult).then_inc(d_y1, 1)
                    dve.wait_ge(d_y1, k + 1)
                    dve.wait_ge(p_in, k + 1)
                    ch.link(v.tensor_tensor(heads(y[:]), heads(y[:]), both(psB), ALU.add))
                else:
                    dve.wait_ge(p_in, 1)
                    v.tensor_copy(heads(y[:]), both(psB)).then_inc(d_y1, 1)
                    dve.wait_ge(d_y1, 1)
                dve.wait_ge(g_x, k + 1)
                ch.link(v.tensor_tensor(y[:], y[:], xd[:], ALU.add))
                v.tensor_tensor(y[:], y[:], z[:, k], ALU.mult).then_inc(d_y, 1)
                if k:
                    v.tensor_tensor(heads(state[:]), heads(state[:]), per_head(e3[:, 2]), ALU.mult).then_inc(d_st1, 1)
                    dve.wait_ge(d_st1, k + 1)
                    dve.wait_ge(p_state, k + 1)
                    v.tensor_tensor(state[:], state[:], psC[:].rearrange("p a n -> p (a n)"), ALU.add).then_inc(d_st, 1)
                else:
                    dve.wait_ge(p_state, 1)
                    v.tensor_copy(state[:], psC[:].rearrange("p a n -> p (a n)")).then_inc(d_st, 1)
                    dve.sem_inc(d_st1, 1)
                if k + 1 < NC:
                    front(k + 1)
                dve.wait_ge(a_std, k + 1)
                v.reciprocal(rstd[:], std[:]).then_inc(d_rs, 1)
                dve.wait_ge(d_rs, k + 1)
                for g in range(G):
                    cut = slice(g * GW, (g + 1) * GW)
                    v.tensor_scalar(y[:, cut], y[:, cut], rstd[:, g:g + 1], None, ALU.mult).then_inc(d_n, 1)
                dve.wait_ge(p_out, k + 1)
                if k:
                    dve.wait_ge(s_st, 16 * k)
                v.tensor_tensor(yt[:], psA[:].rearrange("p a (t n) -> p (a t) n", n=P),
                                norm[:].unsqueeze(2).to_broadcast([P, XT, P]), ALU.mult).then_inc(d_yt, 1)

        @block.tensor
        def _(pe):
            def front(k):
                tok = slice(k * P, (k + 1) * P)
                adt = scr.adt[:, k]
                if k:
                    pe.wait_ge(d_m, G * k)
                    pe.wait_ge(a_e, k)
                for n, m in enumerate((upper, after, ones)):
                    nc.tensor.matmul(sums[:, n], m[:], adt, start=True, stop=True)
                for g in range(G):
                    nc.tensor.matmul(cbt[:, g], xbc[:, XT + g, tok], xbc[:, XT + G + g, tok], start=True, stop=True)
                if k:
                    pe.wait_ge(d_y1, k)
                    pe.wait_ge(d_y, k)
                    pe.wait_ge(a_x, k)
                for t in range(XT):
                    nc.tensor.transpose(psB[:].rearrange("p a (t n) -> p (a t) n", n=P)[:, t], xbc[:, t, tok], ident[:])
                for g in range(G):
                    last = nc.tensor.transpose(psE[:, g * P:(g + 1) * P], xbc[:, XT + g, tok], ident[:])
                last.then_inc(p_turn, 1)
                if k >= 2:
                    pe.wait_ge(d_yt, k - 1)
                for g in range(G):
                    wait(pe, a_l, G * k + g)
                    for half in range(2):
                        for h in range(4):
                            hh = g * HG + half * 4 + h
                            nc.tensor.matmul(psA[:, half, h * P:(h + 1) * P], adt[:, hh:hh + 1].to_broadcast([P, P]),
                                             upper[:], start=(h == 0), stop=False, skip_group_check=True)
                        last = nc.tensor.matmul(psA[:, half], ident[:], neg[:].rearrange("p h n -> p (h n)"), start=False,
                                                stop=True, skip_group_check=True)
                    last.then_inc(p_row, 1)

            def result(k):
                pe.wait_ge(d_n, G * (k + 1))
                for t in range(XT):
                    last = nc.tensor.transpose(psA[:].rearrange("p a (t n) -> p (a t) n", n=P)[:, t], y[:, t * P:(t + 1) * P], ident[:])
                last.then_inc(p_out, 1)

            pe.wait_ge(s_c1, 6)
            front(0)
            for k in range(NC):
                tok = slice(k * P, (k + 1) * P)
                if k:
                    pe.wait_ge(d_st, k)
                    for g in range(G):
                        last = nc.tensor.matmul(psC[:, g], xbc[:, XT + G + g, tok], state[:, g * GW:(g + 1) * GW], start=True, stop=True)
                    last.then_inc(p_inter, 1)
                else:
                    pe.sem_inc(p_inter, 1)
                pe.wait_ge(d_xdt, k + 1)
                for h in range(H):
                    if h % HG == 0:
                        pe.wait_ge(d_m, G * k + h // HG + 1)
                    last = nc.tensor.matmul(psB[:, h // HG, (h % HG) * HD:(h % HG + 1) * HD], mt[:, h], xdt[:, h * HD:(h + 1) * HD],
                                            start=True, stop=True)
                last.then_inc(p_in, 1)
                pe.wait_ge(d_y1, k + 1) if k else None
                for g in range(G):
                    last = nc.tensor.matmul(psC[:, g], b_r[:, g], xdec[:, g * GW:(g + 1) * GW], start=True, stop=True)
                last.then_inc(p_state, 1)
                if k + 1 < NC:
                    front(k + 1)
                    pe.wait_ge(a_l, G * (k + 2))
                result(k)


def mlstm_chunks(nc, A, qk, v1, scr, hl):
    S = qk.shape[2]
    NC, H, D = S // P, ML_HEADS, P
    SCALE = float(D) ** -0.5
    QH = 4
    NG = H // QH
    CH = 9
    with ExitStack() as ctx:
        c = Core(nc, ctx)
        upper, neg, ident = c.sb("ml_upper", [P, P]), c.sb("ml_neg", [P, QH, P]), c.sb("ml_ident", [P, P])
        last_row = c.sb("ml_last_row", [P, P])
        ones, eps = c.sb("ml_ones", [P, 2]), c.sb("ml_eps", [P, 1])
        nsel = c.sb("ml_neg_select", [H, H, P])
        w = c.sb("ml_w", [P, 2, QH, P])
        kw = c.sb("ml_kw", [P, 2, QH, P])
        state = c.sb("ml_state", [P, H, D])
        nvec = c.sb("ml_n", [P, H])
        carry = c.sb("ml_carry", [P, H])
        h_r = c.sb("ml_h", [P, H, D])
        sq = c.sb("ml_sq", [P, H, D])
        sm = c.sb("ml_small", [P, 6, H])
        gate = c.sb("ml_o", [P, 2, H, P])
        yt = c.sb("ml_yt", [P, 2, QH, P])
        ps_s, ps_w, ps_k, ps_n, ps_i, ps_c, ps_t, ps_v = (c.ps(f"ml_ps_{n}", [P, 512]) for n in "swknictv")
        den_i, den_x, n_up, cs = (ps_v[:, n * H:(n + 1) * H] for n in range(4))
        d_i2 = c.sem("ml_dve_scaled")
        (s_c0, s_c1, s_c2, s_o0, s_o1) = (c.sem(f"ml_{n}") for n in ("const_steps", "consts", "more_steps", "o_loaded0", "o_loaded1"))
        s_o = (s_o0, s_o1)
        (p_s, p_w, p_k, p_n, p_c, p_den, p_nup, p_cs, p_t) = (
            c.sem(f"ml_pe_{n}") for n in ("scores", "rows", "turned_k", "num", "state", "den", "n", "carry", "turned"))
        (a_w, a_sq, a_std, a_h) = (c.sem(f"ml_act_{n}") for n in ("w", "square", "std", "high"))
        (d_p, d_kw, d_i, d_num, d_ch, d_cs, d_st, d_n, d_hc, d_hn, d_y, d_l) = (
            c.sem(f"ml_dve_{n}") for n in ("p", "kw", "inter", "num", "chain", "carry", "state", "n", "centred", "normed", "y", "low"))
        g_st = c.sem("ml_pool_state")
        block = ctx.enter_context(nc.Block())
        grp = lambda ps: ps[:].rearrange("p (h n) -> p h n", n=P)
        per_head = lambda ap, n=QH: ap.unsqueeze(2).to_broadcast([P, n, P])
        col = lambda k, n: scr.cols[:, k, n]

        @block.sync
        def _(sp):
            for k in range(NC):
                if k >= 2:
                    sp.wait_ge(d_y, NG * (k - 1))
                sp.dma_start(gate[:, k % 2], scr.o[:, :, k * P:(k + 1) * P].rearrange("f p s -> p f s")).then_inc(s_o[k % 2], 16)

        @block.gpsimd
        def _(pool):
            triangle(nc, pool, s_c1, s_c0, upper[:], neg[:])
            identity(nc, pool, s_c1, s_c0, ident[:])
            nc.gpsimd.memset(ones[:], 1.0).then_inc(s_c1, 1)
            nc.gpsimd.memset(eps[:], EPS).then_inc(s_c1, 1)
            nc.gpsimd.memset(last_row[:], 1.0).then_inc(s_c2, 1)
            nc.gpsimd.memset(nsel[:], 0.0).then_inc(s_c2, 1)
            pool.wait_ge(s_c2, 2)
            nc.gpsimd.affine_select(out=last_row[:], in_=last_row[:], compare_op=ALU.is_equal, fill=0.0, base=-(P - 1),
                                    pattern=[[0, P]], channel_multiplier=1).then_inc(s_c1, 1)
            nc.gpsimd.affine_select(out=nsel[:], in_=nsel[:], compare_op=ALU.not_equal, fill=-1.0, base=0,
                                    pattern=[[-1, H], [0, P]], channel_multiplier=1).then_inc(s_c1, 1)
            for k in range(1, NC):
                pool.wait_ge(d_cs, k + 1)
                for g in range(NG):
                    pool.wait_ge(p_n, NG * k + g + 1)
                    pool.wait_ge(d_st, NG * (k - 1) + g + 1)
                    st = state[:, g * QH:(g + 1) * QH]
                    nc.gpsimd.tensor_tensor(st, st, per_head(carry[:, g * QH:(g + 1) * QH]), ALU.mult).then_inc(g_st, 1)

        @block.scalar
        def _(act):
            act.wait_ge(s_c1, 7)
            for k in range(NC):
                for g in range(NG):
                    n = NG * k + g
                    act.wait_ge(p_w, n + 1)
                    if k:
                        act.wait_ge(p_den, k)
                    for h in range(QH):
                        last = nc.scalar.activation(w[:, g, h], grp(ps_w)[:, h], ACT.Exp, bias=col(k, 0)[:, g * QH + h:g * QH + h + 1])
                    last.then_inc(a_w, 1)
                act.wait_ge(d_hc, k + 1)
                nc.scalar.activation(sq[:], h_r[:], ACT.Square).then_inc(a_sq, 1)
                act.wait_ge(d_ch, CH * k + CH - 1)
                nc.scalar.activation(sm[:, 4], sm[:, 3], ACT.Sqrt, scale=1.0 / D, bias=eps[:]).then_inc(a_std, 1)
                for g in range(NG):
                    act.wait_ge(d_y, NG * k + g + 1)
                    nc.scalar.activation(hl[:, 0, g * QH:(g + 1) * QH, k * P:(k + 1) * P], yt[:, g], ACT.Copy).then_inc(a_h, 1)

        @block.vector
        def _(dve):
            v, ch = nc.vector, Chain(dve, d_ch, CH)
            dve.wait_ge(s_c1, 7)
            for k in range(NC):
                ch.start(k)
                dve.wait_ge(p_cs, k + 1)
                if k:
                    dve.wait_ge(g_st, NG * (k - 1)) if k > 1 else None
                v.tensor_copy(carry[:], cs).then_inc(d_cs, 1)
                for g in range(NG):
                    n, hs = NG * k + g, slice(g * QH, (g + 1) * QH)
                    dve.wait_ge(a_w, n + 1)
                    dve.wait_ge(p_s, n + 1)
                    v.scalar_tensor_tensor(w[:, g], grp(ps_s), SCALE, w[:, g], ALU.mult, ALU.mult).then_inc(d_p, 1)
                    dve.wait_ge(p_k, n + 1)
                    if k:
                        dve.wait_ge(p_nup, k)
                    v.scalar_tensor_tensor(kw[:, g], grp(ps_k), SCALE, per_head(col(k, 3)[:, hs]), ALU.mult, ALU.mult).then_inc(d_kw, 1)
                    dve.wait_ge(p_n, n + 1)
                    if k:
                        v.tensor_tensor(h_r[:, hs], grp(ps_i), per_head(col(k, 1)[:, hs]), ALU.mult).then_inc(d_i, 1)
                        dve.wait_ge(d_i, n + 1)
                        v.tensor_tensor(h_r[:, hs], h_r[:, hs], grp(ps_n), ALU.add).then_inc(d_num, 1)
                        dve.wait_ge(g_st, NG * (k - 1) + g + 1)
                        dve.wait_ge(p_c, n + 1)
                        v.tensor_tensor(state[:, hs], state[:, hs], grp(ps_c), ALU.add).then_inc(d_st, 1)
                    else:
                        dve.sem_inc(d_i, 1)
                        v.tensor_copy(h_r[:, hs], grp(ps_n)).then_inc(d_num, 1)
                        dve.wait_ge(p_c, n + 1)
                        v.tensor_copy(state[:, hs], grp(ps_c)).then_inc(d_st, 1)
                dve.wait_ge(p_nup, k + 1)
                if k:
                    ch.link(v.tensor_tensor(sm[:, 0], col(k, 1), den_x, ALU.mult))
                    ch.link(v.tensor_tensor(sm[:, 0], sm[:, 0], den_i, ALU.add))
                else:
                    ch.link(v.tensor_copy(sm[:, 0], den_i))
                    ch.link(v.tensor_copy(sm[:, 5], sm[:, 0]))
                ch.link(v.scalar_tensor_tensor(sm[:, 1], sm[:, 0], -1.0, sm[:, 0], ALU.mult, ALU.max))
                ch.link(v.tensor_tensor(sm[:, 1], sm[:, 1], col(k, 2), ALU.max))
                ch.link(v.reciprocal(sm[:, 1], sm[:, 1]))
                if k:
                    ch.inc(v.tensor_tensor(nvec[:], nvec[:], carry[:], ALU.mult))
                else:
                    ch.inc(v.tensor_copy(nvec[:], n_up))
                dve.wait_ge(d_num, NG * (k + 1))
                ch.wait()
                v.tensor_tensor(h_r[:], h_r[:], per_head(sm[:, 1], H), ALU.mult).then_inc(d_i2, 1)
                if k:
                    v.tensor_tensor(nvec[:], nvec[:], n_up, ALU.add).then_inc(d_n, 1)
                else:
                    dve.sem_inc(d_n, 1)
                dve.wait_ge(d_i2, k + 1)
                ch.link(v.tensor_reduce(sm[:, 2], h_r[:], AX, ALU.add))
                if k:
                    dve.wait_ge(a_sq, k)
                v.scalar_tensor_tensor(h_r[:], per_head(sm[:, 2], H), -1.0 / D, h_r[:], ALU.mult, ALU.add).then_inc(d_hc, 1)
                dve.wait_ge(a_sq, k + 1)
                ch.inc(v.tensor_reduce(sm[:, 3], sq[:], AX, ALU.add))
                dve.wait_ge(a_std, k + 1)
                ch.link(v.reciprocal(sm[:, 5], sm[:, 4]))
                ch.end()
                if k:
                    dve.wait_ge(p_t, NG * k)
                v.tensor_tensor(h_r[:], h_r[:], per_head(sm[:, 5], H), ALU.mult).then_inc(d_hn, 1)
                dve.wait_ge(s_o[k % 2], 16 * (k // 2 + 1))
                for g in range(NG):
                    n, hs = NG * k + g, slice(g * QH, (g + 1) * QH)
                    dve.wait_ge(p_t, n + 1)
                    if k:
                        dve.wait_ge(a_h, n - 1)
                        dve.wait_ge(d_l, n - 1)
                    v.tensor_tensor(yt[:, g], grp(ps_t), gate[:, k % 2, hs], ALU.mult).then_inc(d_y, 1)
                    dve.wait_ge(a_h, n + 1)
                    v.tensor_tensor(hl[:, 1, hs, k * P:(k + 1) * P], yt[:, g], f32(hl[:, 0, hs, k * P:(k + 1) * P]),
                                    ALU.subtract).then_inc(d_l, 1)

        @block.tensor
        def _(pe):
            q = lambda h, k: qk[:, h, k * P:(k + 1) * P]
            kk = lambda h, k: qk[:, H + h, k * P:(k + 1) * P]
            mm = nc.tensor.matmul

            def front(k, g):
                n = NG * k + g
                if g == 0:
                    wait(pe, d_cs, k)
                    wait(pe, d_hc, k)
                    wait(pe, d_n, k)
                    mm(cs, last_row[:], col(k, 1), start=True, stop=True).then_inc(p_cs, 1)
                wait(pe, d_p, n)
                for h in range(QH):
                    last = mm(grp(ps_s)[:, h], kk(g * QH + h, k), q(g * QH + h, k), start=True, stop=True)
                last.then_inc(p_s, 1)
                wait(pe, a_w, n)
                for h in range(QH):
                    mm(grp(ps_w)[:, h], nsel[:, g * QH + h], scr.g[:, k * P:(k + 1) * P], start=(h == 0),
                       stop=False, skip_group_check=True)
                last = mm(ps_w[:], ident[:], neg[:].rearrange("p h n -> p (h n)"), start=False, stop=True,
                          skip_group_check=True)
                last.then_inc(p_w, 1)
                wait(pe, d_kw, n)
                for h in range(QH):
                    last = nc.tensor.transpose(grp(ps_k)[:, h], kk(g * QH + h, k), ident[:])
                last.then_inc(p_k, 1)

            def products(k, g):
                n = NG * k + g
                pe.wait_ge(d_p, n + 1)
                wait(pe, d_num, n)
                for h in range(QH):
                    last = mm(grp(ps_n)[:, h], w[:, g, h], v1[:, k, g * QH + h], start=True, stop=True)
                if k:
                    pe.wait_ge(d_st, n - NG + 1)
                    wait(pe, d_i, n)
                    for h in range(QH):
                        last = mm(grp(ps_i)[:, h], q(g * QH + h, k), state[:, g * QH + h], start=True, stop=True)
                last.then_inc(p_n, 1)
                pe.wait_ge(d_kw, n + 1)
                wait(pe, d_st, n)
                for h in range(QH):
                    last = mm(grp(ps_c)[:, h], kw[:, g, h], v1[:, k, g * QH + h], start=True, stop=True)
                last.then_inc(p_c, 1)

            pe.wait_ge(s_c1, 7)
            front(0, 0)
            for k in range(NC):
                front(k, 1)
                products(k, 0)
                products(k, 1)
                pe.wait_ge(d_cs, k + 1)
                for h in range(H):
                    last = mm(den_i[:, h:h + 1], w[:, h // QH, h % QH], ones[:, 0:1], start=True, stop=True)
                    if k:
                        last = mm(den_x[:, h:h + 1], q(h, k), nvec[:, h:h + 1], start=True, stop=True)
                last.then_inc(p_den, 1)
                for h in range(H):
                    last = mm(n_up[:, h:h + 1], kw[:, h // QH, h % QH], ones[:, 0:1], start=True, stop=True)
                last.then_inc(p_nup, 1)
                if k + 1 < NC:
                    front(k + 1, 0)
                pe.wait_ge(d_hn, k + 1)
                for g in range(NG):
                    n = NG * k + g
                    wait(pe, d_y, n)
                    for h in range(QH):
                        last = nc.tensor.transpose(grp(ps_t)[:, h], h_r[:, g * QH + h], ident[:])
                    last.then_inc(p_t, 1)


def load_split(nc, tag, src, hl):
    KT = hl.shape[2]
    with ExitStack() as ctx:
        c = Core(nc, ctx)
        stage = c.sb(f"{tag}_stage", [P, 4, hl.shape[3]])
        s_in = c.sems(f"{tag}_loaded", 4)
        s_hi, s_lo = c.sem(f"{tag}_high"), c.sem(f"{tag}_low")
        block = ctx.enter_context(nc.Block())

        @block.sync
        def _(sp):
            for k in range(KT):
                wait(sp, s_lo, k - 3)
                sp.dma_start(stage[:, k % 4], src[k]).then_inc(s_in[k % 4], 16)

        @block.scalar
        def _(act):
            for k in range(KT):
                act.wait_ge(s_in[k % 4], 16 * (k // 4 + 1))
                nc.scalar.activation(hl[:, 0, k], stage[:, k % 4], ACT.Copy).then_inc(s_hi, 1)

        @block.vector
        def _(dve):
            for k in range(KT):
                dve.wait_ge(s_hi, k + 1)
                nc.vector.tensor_tensor(hl[:, 1, k], stage[:, k % 4], f32(hl[:, 0, k]), ALU.subtract).then_inc(s_lo, 1)


def second_mixers(nc, A, hl, scr):
    KT, S = hl.shape[2], hl.shape[3]
    D, T = KT * P, S // P
    w_in = A.w_in_2[0].rearrange("(k p) n -> p k n", p=P)
    cols = lambda a, n: w_in[:, :, a:a + n]
    tiles = lambda a, n: cols(a, n).rearrange("p k (f m) -> p k f m", m=P)
    Z, XBC, DT = 0, D, D + 1536
    QK = DT + SSD_HEADS
    V = QK + 2 * D
    O = V + D
    IF = O + D
    with ExitStack() as ctx:
        c = Core(nc, ctx)
        small = Names()
        scr.dt, scr.adt = c.sb("dt", [P, T, SSD_HEADS]), c.sb("adt", [P, T, SSD_HEADS])
        scr.cols, scr.g = c.sb("ml_cols", [P, T, 4, ML_HEADS]), c.sb("ml_g", [ML_HEADS, S])
        with nc.sbuf_tensor("silu_z", [P, T, D], F32) as z:
            with nc.sbuf_tensor("gates", [P, T, 32], F32) as gates:
                row_product(nc, "pz", hl, cols(Z, D), z, ACT.Silu,
                            (cols(DT, 32), gates, [(cols(DT, 16), 0, 16), (cols(IF, 16), 16, 16)]))
                gate_values(nc, A, gates, scr)
            with nc.sbuf_tensor("xbc", [P, 12, S], F32) as xbc:
                column_product(nc, "px", hl, tiles(XBC, 1536), 12, out=xbc, conv=(A.ssd_conv_w_2[0], A.ssd_conv_b_2[0]))
                ssd_chunks(nc, A, xbc, z, scr)
        with nc.sbuf_tensor("v_rows", [P, T, ML_HEADS, P], F32) as v1:
            row_product(nc, "pv", hl, cols(V, D), v1, ACT.Copy)
            column_product(nc, "po", hl, tiles(O, D), ML_HEADS, gain=A.ml_norm_w_2[0], store=scr.o)
            with nc.sbuf_tensor("qk", [P, 2 * ML_HEADS, S], F32) as qk:
                column_product(nc, "pq", hl, tiles(QK, 2 * D), 16, out=qk, conv=(A.ml_conv_w_2[0], A.ml_conv_b_2[0]))
                mlstm_chunks(nc, A, qk, v1, scr, hl)


def route(nc, A, hl, scr):
    T, KT = scr.T, hl.shape[2]
    NE, NGR = A.router_e_w_2.shape[2], A.router_g_w_2.shape[2]
    EG, NL = NE // NGR, NE + NGR
    NT, NX = scr.NT, scr.NX
    MOST = T - 1
    with ExitStack() as ctx:
        c = Core(nc, ctx)
        wst = c.sb("rt_w", [P, KT, NL])
        w_hl = c.sb("rt_w_hl", [P, 2, KT, NL], F32R)
        bias = c.sb("rt_bias", [P, NL])
        before, ones = c.sb("rt_before", [P, P]), c.sb("rt_ones", [P, P])
        io_i = c.sb("rt_iota_i", [P, NE + NX + 1], I32)
        io = c.sb("rt_iota", [P, NE])
        iom = c.sb("rt_iota_m", [P, NE])
        jj = c.sb("rt_jj", [P, NX + 1])
        tok_id = c.sb("rt_token", [P, T], I32)
        zero = c.sb("rt_zero", [P, NT], I32)
        gl, ge, gh, gpen, cand4 = (c.sb(f"rt_g{n}", [P, T, NGR]) for n in range(5))
        el, el2, cand, oh1, oh2, o = (c.sb(f"rt_e{n}", [P, T, NE]) for n in range(6))
        jr, q, tl, pa, pb, tmp = (c.sb(f"rt_p{n}", [P, T, NE]) for n in range(6))
        oc = c.sb("rt_oc", [P, T + 1, NE])
        s8 = c.sb("rt_s8", [P, 10, T])
        n_e, nx, xb, xe, dd, one32 = (c.sb(f"rt_n{n}", [P, NE]) for n in range(6))
        ina, inb = c.sb("rt_ina", [P, NX + 1, NE]), c.sb("rt_inb", [P, NX + 1, NE])
        more = c.sb("rt_more", [P, NX + 1])
        sel = c.sb("rt_sel", [P, 4, T])
        place = c.sb("rt_place", [P, 2, T], U32)
        ps_l = c.ps("rt_ps_l", [P, T, NL])
        ps_r = c.ps("rt_ps_r", [P, T, NE])
        ps_n = c.ps("rt_ps_n", [P, NE])
        s_w, s_hi, s_lo, s_mm, s_b = c.sem("rt_w_loaded"), c.sem("rt_w_high"), c.sem("rt_w_low"), c.sem("rt_logits"), c.sem("rt_bias_loaded")
        s_c, s_c0 = c.sem("rt_consts"), c.sem("rt_const_steps")
        s_ch, s_e, s_o, s_rank, s_pos = c.sem("rt_chain"), c.sem("rt_exp"), c.sem("rt_counts_ready"), c.sem("rt_ranked"), c.sem("rt_places")
        s_e2 = c.sem("rt_exp_done")
        s_z, s_sc = c.sem("rt_list_zeroed"), c.sem("rt_list_written")
        block = ctx.enter_context(nc.Block())

        @block.sync
        def _(sp):
            with nc.allow_non_contiguous_dma(reason="few router columns"):
                sp.dma_start(wst[:, :, 0:NGR], A.router_g_w_2[0].rearrange("(k p) n -> p k n", p=P)).then_inc(s_w, 16)
                sp.dma_start(wst[:, :, NGR:], A.router_e_w_2[0].rearrange("(k p) n -> p k n", p=P)).then_inc(s_w, 16)
            sp.dma_start(bias[:, 0:NGR], A.router_g_b_2.broadcast_to([P, NGR])).then_inc(s_b, 16)
            sp.dma_start(bias[:, NGR:], A.router_e_b_2.broadcast_to([P, NE])).then_inc(s_b, 16)

        @block.gpsimd
        def _(pool):
            nc.gpsimd.memset(before[:], 1.0).then_inc(s_c0, 1)
            nc.gpsimd.memset(ones[:], 1.0).then_inc(s_c, 1)
            nc.gpsimd.memset(zero[:], 0).then_inc(s_c0, 1)
            nc.gpsimd.iota(io_i[:, 0:NE], pattern=[[1, NE]], base=0, channel_multiplier=0).then_inc(s_c, 1)
            nc.gpsimd.iota(io_i[:, NE:], pattern=[[1, NX + 1]], base=0, channel_multiplier=0).then_inc(s_c, 1)
            nc.gpsimd.iota(tok_id[:], pattern=[[P, T]], base=0, channel_multiplier=1).then_inc(s_c, 1)
            pool.wait_ge(s_c0, 2)
            nc.gpsimd.affine_select(out=before[:], in_=before[:], compare_op=ALU.is_gt, fill=0.0, base=0, pattern=[[1, P]],
                                    channel_multiplier=-1).then_inc(s_c, 1)
            pool.dma_start(scr.list.rearrange("(p t) a -> p (t a)", t=NT), zero[:]).then_inc(s_z, 16)
            pool.wait_ge(s_z, 16)
            pool.wait_ge(s_pos, 1)
            pool.wait_ge(s_c, 5)
            for n in range(2 * T):
                pool.indirect_dma_start(out=scr.list, out_offset=bass.IndirectOffsetOnAxis(ap=place[:, n // T, n % T:n % T + 1], axis=0),
                                        in_=tok_id[:, n % T:n % T + 1], in_offset=None).then_inc(s_sc, 16)
            pool.wait_ge(s_sc, 16 * 2 * T)

        @block.scalar
        def _(act):
            act.wait_ge(s_w, 32)
            nc.scalar.activation(w_hl[:, 0], wst[:], ACT.Copy).then_inc(s_hi, 1)
            act.wait_ge(s_e, 1)
            nc.scalar.activation(ge[:], ge[:], ACT.Exp).then_inc(s_e2, 1)
            act.wait_ge(s_e, 2)
            nc.scalar.activation(s8[:, 6], s8[:, 6], ACT.Exp).then_inc(s_e2, 1)

        @block.tensor
        def _(pe):
            pe.wait_ge(s_lo, 1)
            for t in range(T):
                tok = slice(t * P, (t + 1) * P)
                for k in range(KT):
                    last = mm3(nc, ps_l[:, t], (hl[:, 0, k, tok], hl[:, 1, k, tok]), (w_hl[:, 0, k], w_hl[:, 1, k]), k == 0, k == KT - 1)
            last.then_inc(s_mm, 1)
            pe.wait_ge(s_c, 5)
            pe.wait_ge(s_o, 1)
            nc.tensor.matmul(ps_r[:], before[:], o[:], start=True, stop=False)
            nc.tensor.matmul(ps_r[:], ones[:], oc[:, 0:T], start=False, stop=True)
            nc.tensor.matmul(ps_n[:], ones[:], oc[:, T], start=True, stop=True).then_inc(s_rank, 1)

        @block.vector
        def _(dve):
            v, ch = nc.vector, Chain(dve, s_ch)
            wide = lambda ap, n: ap.unsqueeze(2).to_broadcast([P, T, n])
            rows = lambda ap: ap.unsqueeze(1).to_broadcast([P, T, ap.shape[1]])

            def first_of(vals, top, n, scratch, idx, hot):
                ch.link(v.tensor_reduce(top, vals, AX, ALU.max))
                ch.link(v.tensor_tensor(scratch, vals, wide(top, n), ALU.is_equal))
                ch.link(v.scalar_tensor_tensor(scratch, scratch, -64.0, rows(io[:, 0:n]), ALU.mult, ALU.add))
                ch.link(v.tensor_reduce(idx, scratch, AX, ALU.min))
                ch.link(v.tensor_tensor(hot, rows(iom[:, 0:n]), wide(idx, n), ALU.is_equal))

            dve.wait_ge(s_hi, 1)
            v.tensor_tensor(w_hl[:, 1], wst[:], f32(w_hl[:, 0]), ALU.subtract).then_inc(s_lo, 1)
            dve.wait_ge(s_c, 5)
            ch.inc(v.tensor_copy(jj[:], io_i[:, NE:]))
            ch.link(v.tensor_copy(io[:], io_i[:, 0:NE]))
            ch.inc(v.tensor_scalar(iom[:], io[:], -64.0, None, ALU.add))
            ch.inc(v.memset(one32[:], 1.0))
            ch.inc(v.memset(nx[:], 0.0))
            ch.inc(v.memset(jr[:], 0.0))
            ch.inc(v.memset(oc[:, 0], 0.0))
            dve.wait_ge(s_b, 32)
            dve.wait_ge(s_mm, 1)
            ch.inc(v.tensor_tensor(gl[:], ps_l[:, :, 0:NGR], rows(bias[:, 0:NGR]), ALU.add))
            ch.link(v.tensor_tensor(el[:], ps_l[:, :, NGR:], rows(bias[:, NGR:]), ALU.add))
            first_of(gl[:], s8[:, 0], NGR, cand4[:], s8[:, 1], gh[:])
            v.tensor_tensor(ge[:], gl[:], wide(s8[:, 0], NGR), ALU.subtract).then_inc(s_e, 1)
            per_group = lambda ap: ap.rearrange("p t g -> p (t g)").unsqueeze(2).to_broadcast([P, T * NGR, EG])
            groups = lambda ap: ap.rearrange("p t (g e) -> p (t g) e", e=EG)
            ch.inc(v.tensor_scalar(gpen[:], gh[:], -1.0, 1e30, ALU.add, ALU.mult))
            ch.link(v.tensor_tensor(groups(el[:]), groups(el[:]), per_group(gh[:]), ALU.mult))
            ch.link(v.tensor_tensor(groups(el[:]), groups(el[:]), per_group(gpen[:]), ALU.add))
            first_of(el[:], s8[:, 2], NE, cand[:], s8[:, 3], oh1[:])
            ch.link(v.scalar_tensor_tensor(el2[:], oh1[:], -2e30, el[:], ALU.mult, ALU.add))
            first_of(el2[:], s8[:, 4], NE, cand[:], s8[:, 5], oh2[:])
            v.tensor_tensor(s8[:, 6], s8[:, 4], s8[:, 2], ALU.subtract).then_inc(s_e, 1)
            ch.link(v.tensor_tensor(o[:], oh1[:], oh2[:], ALU.add))
            for t in range(T):
                ins = v.tensor_tensor(oc[:, t + 1], oc[:, t], o[:, t], ALU.add)
                if t + 1 < T:
                    ch.link(ins)
                else:
                    ins.then_inc(s_o, 1)
            dve.wait_ge(s_e2, 2)
            ch.link(v.tensor_reduce(s8[:, 7], ge[:], AX, ALU.add))
            ch.inc(v.reciprocal(s8[:, 7], s8[:, 7]))
            ch.link(v.tensor_scalar(s8[:, 8], s8[:, 6], 1.0, None, ALU.add))
            ch.link(v.reciprocal(s8[:, 8], s8[:, 8]))
            ch.link(v.tensor_tensor(scr.gate[:, 0], s8[:, 8], s8[:, 7], ALU.mult))
            ch.link(v.tensor_tensor(scr.gate[:, 1], scr.gate[:, 0], s8[:, 6], ALU.mult))
            dve.wait_ge(s_rank, 1)
            ch.link(v.tensor_copy(n_e[:], ps_n[:]))
            for m in range(1, MOST + 1):
                ch.link(v.scalar_tensor_tensor(nx[:], n_e[:], float(P * m), nx[:], ALU.is_gt, ALU.add))
            ch.link(v.tensor_tensor_scan(xe[:], one32[:], nx[:], 0.0, ALU.mult, ALU.add))
            ch.link(v.tensor_tensor(xb[:], xe[:], nx[:], ALU.subtract))
            ch.link(v.tensor_scalar(dd[:], xb[:], float(NE - 1), None, ALU.add))
            ch.link(v.tensor_tensor(dd[:], dd[:], io[:], ALU.subtract))
            ch.link(v.tensor_copy(q[:], ps_r[:]))
            for m in range(1, MOST + 1):
                ch.link(v.scalar_tensor_tensor(jr[:], q[:], float(P * m), jr[:], ALU.is_ge, ALU.add))
            ch.link(v.scalar_tensor_tensor(q[:], jr[:], -float(P), q[:], ALU.mult, ALU.add))
            ch.link(v.tensor_tensor(tmp[:], jr[:], rows(dd[:]), ALU.add))
            ch.link(v.scalar_tensor_tensor(tl[:], jr[:], 0.0, tmp[:], ALU.is_gt, ALU.mult))
            ch.link(v.tensor_tensor(tl[:], tl[:], rows(io[:]), ALU.add))
            ch.inc(v.scalar_tensor_tensor(pa[:], q[:], float(NT), tl[:], ALU.mult, ALU.add))
            ch.link(v.scalar_tensor_tensor(pb[:], tl[:], float(P), q[:], ALU.mult, ALU.add))
            for n, (hot, pos) in enumerate([(oh1, pa), (oh2, pa), (oh1, pb), (oh2, pb)]):
                ch.link(v.tensor_tensor(tmp[:], hot[:], pos[:], ALU.mult))
                ch.link(v.tensor_reduce(sel[:, n], tmp[:], AX, ALU.add))
            v.tensor_copy(place[:], sel[:, 0:2]).then_inc(s_pos, 1)
            ch.inc(v.tensor_copy(scr.row[:], sel[:, 2:4]))
            over = lambda ap: ap.unsqueeze(1).to_broadcast([P, NX + 1, NE])
            jw = jj[:].unsqueeze(2).to_broadcast([P, NX + 1, NE])
            ch.inc(v.tensor_tensor(ina[:], jw, over(xb[:]), ALU.is_ge))
            ch.link(v.tensor_tensor(inb[:], jw, over(xe[:]), ALU.is_lt))
            ch.link(v.tensor_tensor(ina[:], ina[:], inb[:], ALU.mult))
            ch.link(v.tensor_tensor(ina[:], ina[:], over(io[:]), ALU.mult))
            ch.link(v.tensor_reduce(more[:], ina[:], AX, ALU.add))
            ch.link(v.tensor_copy(more[:, NX:], xe[:, NE - 1:NE]))
            ch.link(v.tensor_copy(scr.more[:], more[:]))


def weight_unit(A, u, e):
    if u < 8:
        w = (A.exp_w_gate_2 if u < 4 else A.exp_w_up_2)[0].rearrange("e (k p) n -> e p k n", p=P)
        return w[e][:, 2 * (u % 4):2 * (u % 4) + 2]
    return A.exp_w_down_2[0].rearrange("e (k p) n -> e p k n", p=P)[e][:, u - 8]


def experts(nc, A, scr):
    NE, D, F = A.exp_w_gate_2.shape[1:]
    KT, FT, NU, NS = D // P, F // P, 12, 6
    assert NE % 2 == 0 and F == 512 and D == 1024
    with ExitStack() as ctx:
        c = Core(nc, ctx)
        stage = c.sb("ex_stage", [P, NS, D])
        w_hl = [c.sb(f"ex_w_hl{u}", [P, 2, D], F32R) for u in range(NU)]
        xg = c.sb("ex_rows", [P, 2, D])
        xs_hl = [c.sb(f"ex_x_hl{b}", [P, 2, KT, P], F32R) for b in range(2)]
        silu, act_f = c.sb("ex_silu", [P, F]), c.sb("ex_act", [P, F])
        a_hl = c.sb("ex_act_hl", [P, 2, FT, P], F32R)
        ys = c.sb("ex_ys", [P, 2, D])
        ident = c.sb("ex_ident", [P, P])
        lst = c.sb("ex_list", [P, scr.NT], U32)
        ps_g, ps_u, ps_a = c.ps("ex_ps_g", [P, F]), c.ps("ex_ps_u", [P, F]), c.ps("ex_ps_a", [P, FT, P])
        ps_d, ps_x = c.ps("ex_ps_d", [P, D]), c.ps("ex_ps_x", [P, KT, P])
        zero, s_zero, s_zst = c.sb("ex_zero", [P, D]), c.sem("ex_zeroed"), c.sem("ex_zeros_stored")
        s_w, s_row, s_st = c.sems("ex_w_loaded", NS), c.sems("ex_rows_gathered", 2), c.sems("ex_ys_stored", 2)
        s_hi, s_lo, s_use = c.sem("ex_w_high"), c.sem("ex_w_low"), c.sem("ex_w_used")
        s_xt, s_xh, s_xl = c.sem("ex_rows_turned"), c.sem("ex_x_high"), c.sem("ex_x_low")
        s_silu, s_act, s_at, s_ah, s_al = (c.sem(f"ex_{n}") for n in ("silu_ready", "act_ready", "act_turned", "act_high", "act_low"))
        s_ys, s_lst, s_id, s_id0 = c.sem("ex_ys_ready"), c.sem("ex_list_loaded"), c.sem("ex_ident_ready"), c.sem("ex_ident_steps")
        block = ctx.enter_context(nc.Block())

        def number(e, u):
            at = e + 1 if u >= 8 else e
            if isinstance(at, int) and at in (0, NE):
                return NU * at + u - (12 if at else 0)
            return NU * at + u - 4

        def used_before(e, u):
            if isinstance(e, int) and e == 0:
                return 0
            return number(e - 1, u) + 1
        slot = lambda e, u: number(e, u) % NS if isinstance(e, int) else (u - 4) % NS
        in_order = [(e, u) for e in range(NE + 1) for u in range(NU) if not (e == NE and u < 8) and not (e == 0 and u >= 8)]

        @block.sync
        def _(sp):
            for at, u in in_order:
                e = at - 1 if u >= 8 else at
                n = number(e, u)
                wait(sp, s_lo, n - NS + 1)
                dst = stage[:, n % NS]
                sp.dma_start(dst if u >= 8 else dst.rearrange("p (k n) -> p k n", n=F), weight_unit(A, u, e)).then_inc(s_w[n % NS], 16)

        @block.gpsimd
        def _(pool):
            identity(nc, pool, s_id, s_id0, ident[:], 0)
            pool.dma_start(lst[:], scr.list.rearrange("(p t) a -> p (t a)", t=scr.NT).bitcast(U32)).then_inc(s_lst, 16)
            pool.wait_ge(s_lst, 16)
            nc.gpsimd.memset(zero[:], 0.0).then_inc(s_zero, 1)
            pool.wait_ge(s_zero, 1)
            for e in range(NE + 2):
                if 2 <= e < 2 + scr.NX:
                    pool.dma_start(scr.ys[(NE + e - 2) * P:(NE + e - 1) * P, :], zero[:]).then_inc(s_zst, 16)
                if e < NE:
                    wait(pool, s_xt, e - 1)
                    pool.indirect_dma_start(out=xg[:, e % 2], out_offset=None, in_=scr.h,
                                            in_offset=bass.IndirectOffsetOnAxis(ap=lst[:, e:e + 1], axis=0)).then_inc(s_row[e % 2], 16)
                if e >= 2:
                    pool.wait_ge(s_ys, e - 1)
                    pool.dma_start(scr.ys[(e - 2) * P:(e - 1) * P, :], ys[:, e % 2]).then_inc(s_st[e % 2], 16)
            for b in range(2):
                pool.wait_ge(s_st[b], 16 * (NE // 2))
            pool.wait_ge(s_zst, 16 * scr.NX)

        def loads(e, u):
            if isinstance(e, int):
                return 16 * (number(e, u) // NS + 1)
            at = e + 1 if u >= 8 else e
            return 32 * at + 16 * ((u - 4) // NS + 1)

        @block.scalar
        def _(act):
            def high(e, u):
                s = slot(e, u)
                act.wait_ge(s_w[s], loads(e, u))
                wait(act, s_use, used_before(e, u))
                nc.scalar.activation(w_hl[u][:, 0], stage[:, s], ACT.Copy).then_inc(s_hi, 1)

            def x_high(e, b):
                act.wait_ge(s_xt, e + 1)
                if b == "first":
                    b = 0
                else:
                    wait(act, s_use, number(e - 2, 7) + 1 if not (isinstance(e, int) and e < 2) else 0)
                nc.scalar.activation(xs_hl[b][:, 0], ps_x[:], ACT.Copy).then_inc(s_xh, 1)

            def step(i, last=False):
                for b in range(2):
                    e = 2 * i + b
                    if isinstance(e, int) and e == 0:
                        for u in range(4):
                            high(0, u)
                        x_high(0, "first")
                        for u in range(4, 8):
                            high(0, u)
                    end = last and b == 1
                    act.wait_ge(s_use, number(e, 3) + 1)
                    wait(act, s_act, e)
                    nc.scalar.activation(silu[:], ps_g[:], ACT.Silu).then_inc(s_silu, 1)
                    if not end:
                        for u in range(4):
                            high(e + 1, u)
                        x_high(e + 1, 1 - b)
                        for u in range(4, 8):
                            high(e + 1, u)
                    for u in range(8, 12):
                        high(e, u)
                    if not (isinstance(e, int) and e == 0):
                        rows_out(e - 1, 1 - b)
                    act.wait_ge(s_at, e + 1)
                    if not (isinstance(e, int) and e == 0):
                        wait(act, s_use, number(e - 1, 11) + 1)
                    nc.scalar.activation(a_hl[:, 0], ps_a[:], ACT.Copy).then_inc(s_ah, 1)

            def rows_out(e, b):
                act.wait_ge(s_use, number(e, 11) + 1)
                if isinstance(e, int):
                    wait(act, s_st[b], 16 * (e // 2))
                else:
                    act.wait_ge(s_st[b], 8 * e - 8 * b)
                nc.scalar.activation(ys[:, b], ps_d[:], ACT.Copy).then_inc(s_ys, 1)

            steps(act, NE // 2, step, end=NE // 2 - 1)
            step(NE // 2 - 1, True)
            rows_out(NE - 1, 1)

        @block.vector
        def _(dve):
            v = nc.vector

            def low(e, u):
                dve.wait_ge(s_hi, number(e, u) + 1)
                v.tensor_tensor(w_hl[u][:, 1], stage[:, slot(e, u)], f32(w_hl[u][:, 0]), ALU.subtract).then_inc(s_lo, 1)

            def x_low(e, b):
                dve.wait_ge(s_xh, e + 1)
                v.tensor_tensor(xs_hl[b][:, 1], ps_x[:], f32(xs_hl[b][:, 0]), ALU.subtract).then_inc(s_xl, 1)

            def step(i, last=False):
                for b in range(2):
                    e = 2 * i + b
                    if isinstance(e, int) and e == 0:
                        for u in range(4):
                            low(0, u)
                        x_low(0, 0)
                        for u in range(4, 8):
                            low(0, u)
                    end = last and b == 1
                    if not end:
                        for u in range(4):
                            low(e + 1, u)
                        x_low(e + 1, 1 - b)
                        for u in range(4, 8):
                            low(e + 1, u)
                    dve.wait_ge(s_silu, e + 1)
                    dve.wait_ge(s_use, number(e, 7) + 1)
                    wait(dve, s_at, e)
                    v.tensor_tensor(act_f[:], silu[:], ps_u[:], ALU.mult).then_inc(s_act, 1)
                    for u in range(8, 12):
                        low(e, u)
                    dve.wait_ge(s_ah, e + 1)
                    v.tensor_tensor(a_hl[:, 1], ps_a[:], f32(a_hl[:, 0]), ALU.subtract).then_inc(s_al, 1)

            steps(dve, NE // 2, step, end=NE // 2 - 1)
            step(NE // 2 - 1, True)

        @block.tensor
        def _(pe):
            def turn(e, b):
                pe.wait_ge(s_row[b], 16 * (e // 2 + 1) if isinstance(e, int) else 8 * e - 8 * b + 16)
                wait(pe, s_xl, e)
                for k in range(KT):
                    last = nc.tensor.transpose(ps_x[:, k], xg[:, b, k * P:(k + 1) * P], ident[:])
                last.then_inc(s_xt, 1)

            def hidden(e, b, ps, u0):
                for u in range(u0, u0 + 4):
                    pe.wait_ge(s_lo, number(e, u) + 1)
                    for kk in range(2):
                        k = 2 * (u - u0) + kk
                        last = mm3(nc, ps[:], (xs_hl[b][:, 0, k], xs_hl[b][:, 1, k]),
                                   (w_hl[u][:, 0, kk * F:(kk + 1) * F], w_hl[u][:, 1, kk * F:(kk + 1) * F]),
                                   k == 0, k == KT - 1)
                    last.then_inc(s_use, 1)

            def down(e):
                wait(pe, s_ys, e)
                pe.wait_ge(s_al, e + 1)
                for u in range(8, 12):
                    k = u - 8
                    pe.wait_ge(s_lo, number(e, u) + 1)
                    for h in range(2):
                        cols = slice(h * 512, (h + 1) * 512)
                        last = mm3(nc, ps_d[:, cols], (a_hl[:, 0, k], a_hl[:, 1, k]), (w_hl[u][:, 0, cols], w_hl[u][:, 1, cols]),
                                   k == 0, k == FT - 1)
                    last.then_inc(s_use, 1)

            def turn_act(e):
                pe.wait_ge(s_act, e + 1)
                wait(pe, s_al, e)
                for k in range(FT):
                    last = nc.tensor.transpose(ps_a[:, k], act_f[:, k * P:(k + 1) * P], ident[:])
                last.then_inc(s_at, 1)

            def step(i, last=False):
                for b in range(2):
                    e = 2 * i + b
                    if isinstance(e, int) and e == 0:
                        turn(0, 0)
                    pe.wait_ge(s_xl, e + 1)
                    wait(pe, s_silu, e)
                    hidden(e, b, ps_g, 0)
                    if not (last and b == 1):
                        turn(e + 1, 1 - b)
                    wait(pe, s_act, e)
                    hidden(e, b, ps_u, 4)
                    if not (isinstance(e, int) and e == 0):
                        down(e - 1)
                    turn_act(e)

            pe.wait_ge(s_id, 1)
            steps(pe, NE // 2, step, end=NE // 2 - 1)
            step(NE // 2 - 1, True)
            down(NE - 1)


def further_tiles(nc, A, scr):
    NE, D, F = A.exp_w_gate_2.shape[1:]
    KT, FT, NX = D // P, F // P, scr.NX
    with ExitStack() as ctx:
        c = Core(nc, ctx)
        stage = c.sb("fx_stage", [P, 4, D])
        w_hl = c.sb("fx_w_hl", [P, 2, 4, D], F32R)
        xg = c.sb("fx_rows", [P, D])
        xs_hl = c.sb("fx_x_hl", [P, 2, KT, P], F32R)
        silu, act_f = c.sb("fx_silu", [P, F]), c.sb("fx_act", [P, F])
        a_hl = c.sb("fx_act_hl", [P, 2, FT, P], F32R)
        ys = c.sb("fx_ys", [P, D])
        ident = c.sb("fx_ident", [P, P])
        lst = c.sb("fx_list", [P, scr.NT], U32)
        ps_g, ps_u, ps_a = c.ps("fx_ps_g", [P, F]), c.ps("fx_ps_u", [P, F]), c.ps("fx_ps_a", [P, FT, P])
        ps_d, ps_x = c.ps("fx_ps_d", [P, D]), c.ps("fx_ps_x", [P, KT, P])
        s_w, s_hi, s_lo, s_use = c.sem("fx_w_loaded"), c.sem("fx_w_high"), c.sem("fx_w_low"), c.sem("fx_w_used")
        s_row, s_xt, s_xh, s_xl = c.sem("fx_row_gathered"), c.sem("fx_rows_turned"), c.sem("fx_x_high"), c.sem("fx_x_low")
        s_silu, s_act, s_at, s_ah, s_al = (c.sem(f"fx_{n}") for n in ("silu_ready", "act_ready", "act_turned", "act_high", "act_low"))
        s_ys, s_st, s_lst, s_id, s_id0 = (c.sem(f"fx_{n}") for n in ("ys_ready", "ys_stored", "list_loaded", "ident_ready", "ident_steps"))
        block = ctx.enter_context(nc.Block())
        count = scr.more[0:1, NX:NX + 1]

        def for_tiles(eng, body):
            n = eng.value_load(count, min_val=0, max_val=NX)
            with eng.If(n > 0):
                with eng.Fori(0, n) as j:
                    body(j)

        @block.gpsimd
        def _(pool):
            identity(nc, pool, s_id, s_id0, ident[:], 0)
            pool.dma_start(lst[:], scr.list.rearrange("(p t) a -> p (t a)", t=scr.NT).bitcast(U32)).then_inc(s_lst, 16)
            pool.wait_ge(s_lst, 16)
            n = pool.value_load(count, min_val=0, max_val=NX)
            for j in range(NX):
                with pool.If(n > j):
                    wait(pool, s_xt, j)
                    pool.indirect_dma_start(out=xg[:], out_offset=None, in_=scr.h,
                                            in_offset=bass.IndirectOffsetOnAxis(ap=lst[:, NE + j:NE + j + 1], axis=0)).then_inc(s_row, 16)

        @block.scalar
        def _(act):
            def body(j):
                e = act.value_load(scr.more[0:1, bass.ds(j, 1)], min_val=0, max_val=NE - 1)
                for r in range(3):
                    act.wait_ge(s_lo, 3 * j + r + 1)
                    for u in range(4 * r, 4 * r + 4):
                        dst = stage[:, u % 4]
                        src = weight_unit(A, u, e)
                        act.dma_start(dst if r == 2 else dst.rearrange("p (k n) -> p k n", n=F), src).then_inc(s_w, 16)
                    if r == 1:
                        act.wait_ge(s_xt, j + 1)
                        nc.scalar.activation(xs_hl[:, 0], ps_x[:], ACT.Copy).then_inc(s_xh, 1)
                    act.wait_ge(s_w, 64 * (3 * j + r + 1))
                    act.wait_ge(s_use, 3 * j + r + 1)
                    nc.scalar.activation(w_hl[:, 0], stage[:], ACT.Copy).then_inc(s_hi, 1)
                    if r == 1:
                        nc.scalar.activation(silu[:], ps_g[:], ACT.Silu).then_inc(s_silu, 1)
                act.wait_ge(s_at, j + 1)
                nc.scalar.activation(a_hl[:, 0], ps_a[:], ACT.Copy).then_inc(s_ah, 1)
                act.wait_ge(s_use, 3 * j + 4)
                nc.scalar.activation(ys[:], ps_d[:], ACT.Copy).then_inc(s_ys, 1)
                act.wait_ge(s_ys, j + 1)
                act.dma_start(scr.ys.rearrange("(t p) d -> t p d", p=P)[NE + j], ys[:]).then_inc(s_st, 16)
                act.wait_ge(s_st, 16 * j + 16)
            for_tiles(act, body)

        @block.vector
        def _(dve):
            v = nc.vector
            dve.sem_inc(s_lo, 1)

            def body(j):
                def low(r):
                    dve.wait_ge(s_hi, 3 * j + r + 1)
                    v.tensor_tensor(w_hl[:, 1], stage[:], f32(w_hl[:, 0]), ALU.subtract).then_inc(s_lo, 1)
                low(0)
                dve.wait_ge(s_xh, j + 1)
                v.tensor_tensor(xs_hl[:, 1], ps_x[:], f32(xs_hl[:, 0]), ALU.subtract).then_inc(s_xl, 1)
                low(1)
                dve.wait_ge(s_silu, j + 1)
                dve.wait_ge(s_use, 3 * j + 3)
                v.tensor_tensor(act_f[:], silu[:], ps_u[:], ALU.mult).then_inc(s_act, 1)
                low(2)
                dve.wait_ge(s_ah, j + 1)
                v.tensor_tensor(a_hl[:, 1], ps_a[:], f32(a_hl[:, 0]), ALU.subtract).then_inc(s_al, 1)
            for_tiles(dve, body)

        @block.tensor
        def _(pe):
            pe.sem_inc(s_use, 1)
            pe.wait_ge(s_id, 1)

            def body(j):
                pe.wait_ge(s_row, 16 * j + 16)
                for k in range(KT):
                    last = nc.tensor.transpose(ps_x[:, k], xg[:, k * P:(k + 1) * P], ident[:])
                last.then_inc(s_xt, 1)
                pe.wait_ge(s_xl, j + 1)
                for r, ps in enumerate((ps_g, ps_u)):
                    pe.wait_ge(s_lo, 3 * j + r + 2)
                    for k in range(KT):
                        w = w_hl[:, :, k // 2, (k % 2) * F:(k % 2 + 1) * F]
                        last = mm3(nc, ps[:], (xs_hl[:, 0, k], xs_hl[:, 1, k]), (w[:, 0], w[:, 1]), k == 0, k == KT - 1)
                    last.then_inc(s_use, 1)
                pe.wait_ge(s_act, j + 1)
                for k in range(FT):
                    last = nc.tensor.transpose(ps_a[:, k], act_f[:, k * P:(k + 1) * P], ident[:])
                last.then_inc(s_at, 1)
                pe.wait_ge(s_al, j + 1)
                pe.wait_ge(s_lo, 3 * j + 4)
                for k in range(FT):
                    for h in range(2):
                        cols = slice(h * 512, (h + 1) * 512)
                        last = mm3(nc, ps_d[:, cols], (a_hl[:, 0, k], a_hl[:, 1, k]), (w_hl[:, 0, k, cols], w_hl[:, 1, k, cols]),
                                   k == 0, k == FT - 1)
                last.then_inc(s_use, 1)
            for_tiles(pe, body)


def combine(nc, A, scr, out):
    T, D = scr.T, A.x.shape[2]
    with ExitStack() as ctx:
        c = Core(nc, ctx)
        x_tm = c.sb("cb_x", [P, T, D])
        s_in = c.sems("cb_x_loaded", T)
        y = c.sb("cb_rows", [P, 2, 2, D])
        rowg, square = c.sb("cb_gain", [P, D]), c.sb("cb_square", [P, D])
        ssq, eps = c.sb("cb_ssq", [P, 3, T]), c.sb("cb_eps", [P, 1])
        res = c.sb("cb_res", [P, 2, D])
        s_y = c.sems("cb_gathered", 2)
        s_g, s_eps, s_a, s_x, s_sq, s_std, s_rs, s_res = (c.sem(f"cb_{n}") for n in (
            "gain_loaded", "eps_ready", "first_added", "added", "squared", "std_ready", "rstd_ready", "result"))
        s_st = c.sems("cb_stored", 2)
        block = ctx.enter_context(nc.Block())

        @block.sync
        def _(sp):
            for t in range(T):
                sp.dma_start(x_tm[:, t], scr.x5[t * P:(t + 1) * P, :]).then_inc(s_in[t], 16)
            sp.dma_start(rowg[:], A.norm_f_w_2.rearrange("(a n) -> a n", a=1).broadcast_to([P, D])).then_inc(s_g, 16)
            for t in range(T):
                sp.wait_ge(s_res, t + 1)
                sp.dma_start(out[t * P:(t + 1) * P, :], res[:, t % 2]).then_inc(s_st[t % 2], 16)
            for b in range(2):
                sp.wait_ge(s_st[b], 16 * (T // 2))

        @block.gpsimd
        def _(pool):
            nc.gpsimd.memset(eps[:], EPS).then_inc(s_eps, 1)
            for t in range(T):
                wait(pool, s_x, t - 1)
                for n in range(2):
                    pool.indirect_dma_start(out=y[:, t % 2, n], out_offset=None, in_=scr.ys,
                                            in_offset=bass.IndirectOffsetOnAxis(ap=scr.row[:, n, t:t + 1], axis=0)).then_inc(s_y[t % 2], 16)

        @block.scalar
        def _(act):
            act.wait_ge(s_eps, 1)
            for t in range(T):
                act.wait_ge(s_x, t + 1)
                nc.scalar.activation(square[:], x_tm[:, t], ACT.Square, accum_out=ssq[:, 0, t:t + 1]).then_inc(s_sq, 1)
                act.wait_ge(s_sq, t + 1)
                nc.scalar.activation(ssq[:, 1, t:t + 1], ssq[:, 0, t:t + 1], ACT.Sqrt, scale=1.0 / D, bias=eps[:]).then_inc(s_std, 1)

        @block.vector
        def _(dve):
            v = nc.vector

            def add(t):
                dve.wait_ge(s_in[t], 16)
                dve.wait_ge(s_y[t % 2], 32 * (t // 2 + 1))
                v.scalar_tensor_tensor(x_tm[:, t], y[:, t % 2, 0], scr.gate[:, 0, t:t + 1], x_tm[:, t], ALU.mult, ALU.add).then_inc(s_a, 1)
                dve.wait_ge(s_a, t + 1)
                v.scalar_tensor_tensor(x_tm[:, t], y[:, t % 2, 1], scr.gate[:, 1, t:t + 1], x_tm[:, t], ALU.mult, ALU.add).then_inc(s_x, 1)

            def finish(t):
                dve.wait_ge(s_std, t + 1)
                v.reciprocal(ssq[:, 2, t:t + 1], ssq[:, 1, t:t + 1]).then_inc(s_rs, 1)
                dve.wait_ge(s_rs, t + 1)
                wait(dve, s_st[t % 2], 16 * (t // 2))
                v.scalar_tensor_tensor(res[:, t % 2], x_tm[:, t], ssq[:, 2, t:t + 1], rowg[:], ALU.mult, ALU.mult).then_inc(s_res, 1)

            dve.wait_ge(s_g, 16)
            for t in range(T):
                add(t)
                if t:
                    finish(t - 1)
            finish(T - 1)


def second_block(nc, A, x_dram, scr, hl):
    T, KT = scr.T, hl.shape[2]
    second_mixers(nc, A, hl, scr)
    recycle_semaphores(nc)
    w_out = A.w_out_2[0].rearrange("(k p) n -> p k n", p=P)
    with nc.sbuf_tensor("x_rows3", [P, T, KT * P], F32) as x_tm:
        add_product(nc, "w1", x_tm, [(hl, KT)], w_out[:, KT:], x_dram=x_dram)
        load_split(nc, "ys", scr.y_ssd, hl)
        add_product(nc, "w2", x_tm, [(hl, KT)], w_out[:, :KT])
        norm_transpose(nc, "n4", x_tm, A.norm2_w_2[0], hl, rows_out=scr.h, x_out=scr.x5)
    route(nc, A, hl, scr)
    recycle_semaphores(nc)


def routed_experts(nc, A, scr, out):
    experts(nc, A, scr)
    recycle_semaphores(nc)
    further_tiles(nc, A, scr)
    combine(nc, A, scr, out)


def scratch(nc, ctx, A):
    S, D, NE = A.x.shape[1], A.x.shape[2], A.router_e_w_2.shape[2]
    T, KT = S // P, D // P
    scr = Names()
    scr.T, scr.NX = T, 2 * T - 1
    scr.NT = NE + 2 * T
    dram = lambda name, shape, dt=F32: nc.dram_tensor(f"scratch_{name}", shape, dt).ap()
    scr.ya, scr.yb, scr.sga, scr.sgb = (dram(n, [KT, P, S]) for n in ("y_a", "y_b", "gate_a", "gate_b"))
    scr.y_ssd, scr.o = dram("y_ssd", [KT, P, S]), dram("o", [KT, P, S])
    scr.x4, scr.x5, scr.h = dram("x4", [S, D]), dram("x5", [S, D]), dram("h", [S, D])
    scr.ys, scr.list = dram("ys", [(NE + scr.NX) * P, D]), dram("list", [P * scr.NT, 1], I32)
    scr.gate = ctx.enter_context(nc.sbuf_tensor("pair_gates", [P, 2, T], F32))
    scr.row = ctx.enter_context(nc.sbuf_tensor("pair_rows", [P, 2, T], U32))
    scr.more = ctx.enter_context(nc.sbuf_tensor("further_tiles", [P, scr.NX + 1], I32))
    return scr


def program(nc, A, out):
    T, KT = A.x.shape[1] // P, A.x.shape[2] // P
    with ExitStack() as ctx:
        scr = scratch(nc, ctx, A)
        with nc.sbuf_tensor("h_hl", [P, 2, KT, A.x.shape[1]], F32R) as hl:
            with nc.sbuf_tensor("x_rows", [P, T, KT * P], F32) as x_tm:
                norm_transpose(nc, "n1", x_tm, A.ln1_g[0], hl, x_dram=A.x[0])
            first_mixers(nc, A, hl, scr)
            merge_mixers(nc, A, scr, hl)
            recycle_semaphores(nc)
            with nc.sbuf_tensor("x_rows2", [P, T, KT * P], F32) as x_tm:
                add_product(nc, "wo", x_tm, [(hl, KT)], A.w_o[0].rearrange("(k p) n -> p k n", p=P), x_dram=A.x[0])
                norm_transpose(nc, "n2", x_tm, A.ln2_g[0], hl)
                feed_forward(nc, A, x_tm, hl)
                norm_transpose(nc, "n3", x_tm, A.norm1_w_2[0], hl, row_gain=A.final_g, x_out=scr.x4)
            recycle_semaphores(nc)
            second_block(nc, A, scr.x4, scr, hl)
        routed_experts(nc, A, scr, out[0])


_INS = ["x", "ln1_g", "w_in", "conv_a_w", "conv_b_w", "conv_b_b", "lru_wa", "lru_ba", "lru_wx", "lru_bx",
        "lru_lambda", "w_out_a", "w_out_b", "gate_bias", "w_o", "ln2_g", "w_ffn_gate", "w_ffn_up",
        "w_ffn_down", "final_g", "norm1_w_2", "w_in_2", "ssd_conv_w_2", "ssd_conv_b_2", "ssd_dt_bias_2",
        "ssd_a_log_2", "ssd_d_2", "ssd_norm_w_2", "ml_conv_w_2", "ml_conv_b_2", "ml_i_bias_2", "ml_f_bias_2",
        "ml_norm_w_2", "w_out_2", "norm2_w_2", "router_g_w_2", "router_g_b_2", "router_e_w_2", "router_e_b_2",
        "exp_w_gate_2", "exp_w_up_2", "exp_w_down_2", "norm_f_w_2"]
_OUTS = [((1, 1024, 1024), "float32")]


def kernel(**inputs):
    import numpy as _np
    import concourse.bacc as _bacc
    from concourse import mybir as _mybir
    from concourse.bass_utils import run_bass_kernel_spmd as _run

    nc = _bacc.Bacc("TRN2", target_bir_lowering=False, num_devices=1)
    arrays, args = {}, Names()
    for name in _INS:
        a = _np.ascontiguousarray(inputs[name])
        arrays[f"in_{name}_dram"] = a
        args.__dict__[name] = nc.dram_tensor(f"in_{name}_dram", a.shape, _mybir.dt.from_np(a.dtype), kind="ExternalInput").ap()
    outs = [nc.dram_tensor(f"out_{i}_dram", shape, _mybir.dt.from_np(_np.dtype(dtype)), kind="ExternalOutput").ap()
            for i, (shape, dtype) in enumerate(_OUTS)]
    program(nc, args, outs[0])
    r = _run(nc, [arrays], core_ids=[0])
    return r.results[0]["out_0_dram"]
```

```python
from contextlib import ExitStack

import concourse.bass as bass
from concourse import mybir

F32 = mybir.dt.float32
F32R = mybir.dt.float32r
I32 = mybir.dt.int32
U32 = mybir.dt.uint32
ACT = mybir.ActivationFunctionType
ALU = mybir.AluOpType
AX = mybir.AxisListType.X
P = 128
EPS = 1e-6
USED = []


def wait(eng, sem, value):
    if isinstance(value, int) and value <= 0:
        return
    eng.wait_ge(sem, value)


def steps(eng, n, body, end=None):
    body(0)
    body(1)
    with eng.Fori(2, n if end is None else end) as i:
        body(i)


class Chain:

    def __init__(self, eng, sem, per=0):
        self.eng, self.sem, self.per, self.base, self.n = eng, sem, per, 0, 0

    def start(self, i, n=0):
        self.base, self.n = i * self.per, n

    def inc(self, ins):
        ins.then_inc(self.sem, 1)
        self.n += 1

    def wait(self):
        self.eng.wait_ge(self.sem, self.base + self.n)

    def link(self, ins):
        self.inc(ins)
        self.wait()

    def end(self):
        assert self.n == self.per, (self.n, self.per)


class Names:
    pass


class Core:

    def __init__(self, nc, ctx):
        self.nc, self.ctx = nc, ctx

    def sb(self, name, shape, dt=F32):
        return self.ctx.enter_context(self.nc.sbuf_tensor(name, shape, dt))

    def ps(self, name, shape, dt=F32):
        return self.ctx.enter_context(self.nc.psum_tensor(name, shape, dt))

    def sem(self, name):
        s = self.nc.alloc_semaphore(name)
        USED.append(s)
        return s

    def sems(self, name, n):
        return [self.sem(f"{name}{i}") for i in range(n)]


def recycle_semaphores(nc):
    nc.clear_and_free_semaphores(list(USED))
    nc.all_engine_barrier()
    USED.clear()


def f32(ap):
    return ap.bitcast(F32)


def log1p_exp_neg(nc, c, e, z, z2, p):
    v = nc.vector
    c.link(v.tensor_scalar(p, e, 2.0, None, ALU.add))
    c.link(v.reciprocal(p, p))
    c.link(v.tensor_tensor(z, e, p, ALU.mult))
    c.link(v.tensor_tensor(z2, z, z, ALU.mult))
    c.link(v.tensor_scalar(p, z2, 1.0 / 19.0, None, ALU.mult))
    for k in range(8, 0, -1):
        c.link(v.scalar_tensor_tensor(p, p, 1.0 / (2 * k + 1), z2, ALU.add, ALU.mult))
    c.link(v.scalar_tensor_tensor(p, p, 1.0, z, ALU.add, ALU.mult))
    c.link(v.tensor_scalar(p, p, 2.0, None, ALU.mult))


def norm_parts(nc, c, tag, x_tm, gain_row, out_hl, x_dram=None, x_out=None, row_gain=None, rows_out=None, x_ready=None):
    tiles, d = x_tm.shape[1], x_tm.shape[2]
    kt = d // P
    ident = c.sb(f"{tag}_ident", [P, P])
    gain = c.sb(f"{tag}_gain", [P, kt])
    square = c.sb(f"{tag}_square", [P, d])
    ssq = c.sb(f"{tag}_ssq", [P, 2 * tiles])
    std = c.sb(f"{tag}_std", [P, 2 * tiles])
    rstd = c.sb(f"{tag}_rstd", [P, 2 * tiles])
    eps = c.sb(f"{tag}_eps", [P, 1])
    xn = c.sb(f"{tag}_xn", [P, 2, d])
    xg = c.sb(f"{tag}_xg", [P, 2, kt, P])
    rowg = c.sb(f"{tag}_rowg", [P, d]) if row_gain is not None else None
    turned = [c.ps(f"{tag}_turned{b}", [P, kt, P]) for b in range(2)]
    if rows_out is not None:
        gain_b, hrow = c.sb(f"{tag}_gain_rows", [P, d]), c.sb(f"{tag}_h_rows", [P, 2, d])
        s_gr, s_hr = c.sem(f"{tag}_gain_rows_loaded"), c.sem(f"{tag}_h_rows_ready")
        s_hs = c.sems(f"{tag}_h_rows_stored", 2)
    s_x = c.sems(f"{tag}_x_loaded", tiles if x_dram is not None else 0)
    s_g = c.sem(f"{tag}_gain_loaded")
    s_id = c.sem(f"{tag}_ident_ready")
    s_sq = c.sem(f"{tag}_squares")
    s_std = c.sem(f"{tag}_std_ready")
    s_rs = c.sem(f"{tag}_rstd_ready")
    s_x2 = c.sem(f"{tag}_x_normed")
    s_xn = c.sem(f"{tag}_scaled")
    s_t = c.sem(f"{tag}_transposed")
    s_xg = c.sem(f"{tag}_gained")
    s_hi = c.sem(f"{tag}_high")
    s_lo = c.sem(f"{tag}_low")
    s_st = c.sem(f"{tag}_x_stored")
    NR = 1 if rowg is None else 2

    def loads(sp):
        with nc.allow_non_contiguous_dma(reason="gain column layout"):
            sp.dma_start(gain[:], gain_row.rearrange("(k p) -> p k", p=P)).then_inc(s_g, 16)
        if rowg is not None:
            sp.dma_start(rowg[:], row_gain.rearrange("(a n) -> a n", a=1).broadcast_to([P, d])).then_inc(s_g, 16)
        if x_dram is not None:
            for t in range(tiles):
                sp.dma_start(x_tm[:, t, :], x_dram[t * P:(t + 1) * P, :]).then_inc(s_x[t], 16)
        if rows_out is not None:
            sp.dma_start(gain_b[:], gain_row.rearrange("(a n) -> a n", a=1).broadcast_to([P, d])).then_inc(s_gr, 16)

    def stores(sp):
        for t in range(tiles):
            if x_out is not None:
                if rowg is not None:
                    sp.wait_ge(s_x2, t + 1)
                elif x_ready is not None:
                    x_ready(sp, t)
                sp.dma_start(x_out[t * P:(t + 1) * P, :], x_tm[:, t, :]).then_inc(s_st, 16)
            if rows_out is not None:
                sp.wait_ge(s_hr, t + 1)
                sp.dma_start(rows_out[t * P:(t + 1) * P, :], hrow[:, t % 2]).then_inc(s_hs[t % 2], 16)
        if rows_out is not None:
            for b in range(2):
                sp.wait_ge(s_hs[b], 16 * (tiles // 2))
        if x_out is not None:
            sp.wait_ge(s_st, 16 * tiles)

    def pool_part(pool):
        nc.gpsimd.memset(ident[:], 0.0).then_inc(s_id, 1)
        pool.wait_ge(s_id, 1)
        nc.gpsimd.affine_select(out=ident[:], in_=ident[:], compare_op=ALU.not_equal, fill=1.0, base=0,
                                pattern=[[-1, P]], channel_multiplier=1).then_inc(s_id, 1)
        nc.gpsimd.memset(eps[:], EPS).then_inc(s_id, 1)
        if rows_out is not None:
            pool.wait_ge(s_gr, 16)
            for t in range(tiles):
                pool.wait_ge(s_xn, t + 1)
                wait(pool, s_hs[t % 2], 16 * (t // 2))
                nc.gpsimd.tensor_tensor(hrow[:, t % 2], xn[:, t % 2, :], gain_b[:], ALU.mult).then_inc(s_hr, 1)

    def deviation(act, n, t, col):
        nc.scalar.activation(square[:], x_tm[:, t, :], ACT.Square, accum_out=ssq[:, col:col + 1]).then_inc(s_sq, 1)
        act.wait_ge(s_sq, n + 1)
        nc.scalar.activation(std[:, col:col + 1], ssq[:, col:col + 1], ACT.Sqrt, scale=1.0 / d,
                             bias=eps[:]).then_inc(s_std, 1)

    def measure(act, t):
        if t == 0:
            act.wait_ge(s_id, 3)
        if x_dram is not None:
            act.wait_ge(s_x[t], 16)
        if x_ready is not None:
            x_ready(act, t)
        if rowg is not None:
            deviation(act, NR * t, t, t)
            act.wait_ge(s_x2, t + 1)
        deviation(act, NR * t + NR - 1, t, tiles + t)

    def scale(act, t):
        act.wait_ge(s_rs, NR * (t + 1))
        if t >= 2:
            act.wait_ge(s_t, t - 1)
            if rows_out is not None:
                act.wait_ge(s_hr, t - 1)
        nc.scalar.activation(xn[:, t % 2, :], x_tm[:, t, :], ACT.Copy,
                             scale=rstd[:, tiles + t:tiles + t + 1]).then_inc(s_xn, 1)

    def high(act, t):
        act.wait_ge(s_xg, t + 1)
        nc.scalar.activation(out_hl[:, 0, :, t * P:(t + 1) * P], xg[:, t % 2], ACT.Copy).then_inc(s_hi, 1)

    def invert(dve, t):
        if t == 0:
            dve.wait_ge(s_g, 16 if rowg is None else 32)
        if rowg is not None:
            dve.wait_ge(s_std, NR * t + 1)
            nc.vector.reciprocal(rstd[:, t:t + 1], std[:, t:t + 1]).then_inc(s_rs, 1)
            dve.wait_ge(s_rs, NR * t + 1)
            nc.vector.scalar_tensor_tensor(x_tm[:, t, :], x_tm[:, t, :], rstd[:, t:t + 1], rowg[:], ALU.mult,
                                           ALU.mult).then_inc(s_x2, 1)
        dve.wait_ge(s_std, NR * (t + 1))
        nc.vector.reciprocal(rstd[:, tiles + t:tiles + t + 1], std[:, tiles + t:tiles + t + 1]).then_inc(s_rs, 1)

    def gained(dve, t):
        dve.wait_ge(s_t, t + 1)
        if t >= 2:
            dve.wait_ge(s_lo, t - 1)
            dve.wait_ge(s_hi, t - 1)
        nc.vector.tensor_tensor(xg[:, t % 2], turned[t % 2][:], gain[:].unsqueeze(2).to_broadcast([P, kt, P]),
                                ALU.mult).then_inc(s_xg, 1)

    def low(dve, t):
        dve.wait_ge(s_hi, t + 1)
        nc.vector.tensor_tensor(out_hl[:, 1, :, t * P:(t + 1) * P], xg[:, t % 2],
                                f32(out_hl[:, 0, :, t * P:(t + 1) * P]), ALU.subtract).then_inc(s_lo, 1)

    def turn(pe, t):
        if t == 0:
            pe.wait_ge(s_id, 3)
        pe.wait_ge(s_xn, t + 1)
        if t >= 2:
            pe.wait_ge(s_xg, t - 1)
        for k in range(kt):
            last = nc.tensor.transpose(turned[t % 2][:, k, :], xn[:, t % 2, k * P:(k + 1) * P], ident[:])
        last.then_inc(s_t, 1)

    return loads, stores, pool_part, measure, scale, high, invert, gained, low, turn


def norm_transpose(nc, tag, x_tm, gain_row, out_hl, x_dram=None, x_out=None, row_gain=None):
    tiles = x_tm.shape[1]
    with ExitStack() as ctx:
        c = Core(nc, ctx)
        (loads, stores, on_pool, measure, scale, high, invert, gained, low, turn) = norm_parts(
            nc, c, tag, x_tm, gain_row, out_hl, x_dram, x_out, row_gain)
        block = ctx.enter_context(nc.Block())

        @block.sync
        def _(sp):
            loads(sp)
            stores(sp)

        @block.gpsimd
        def _(pool):
            on_pool(pool)

        @block.scalar
        def _(act):
            for t in range(tiles):
                measure(act, t)
                if t >= 1:
                    scale(act, t - 1)
                if t >= 2:
                    high(act, t - 2)
            scale(act, tiles - 1)
            high(act, tiles - 2)
            high(act, tiles - 1)

        @block.vector
        def _(dve):
            for t in range(tiles):
                invert(dve, t)
                if t >= 2:
                    gained(dve, t - 2)
                    low(dve, t - 2)
            for t in range(tiles - 2, tiles):
                gained(dve, t)
                low(dve, t)

        @block.tensor
        def _(pe):
            for t in range(tiles):
                turn(pe, t)


def mm3(nc, out, w_hl, x_hl, first, last):
    nc.tensor.matmul(out, w_hl[0], x_hl[0], start=first, stop=False)
    nc.tensor.matmul(out, w_hl[0], x_hl[1], start=False, stop=False)
    return nc.tensor.matmul(out, w_hl[1], x_hl[0], start=False, stop=last)


def first_mixers(nc, A, h_hl, scr):
    S, D = A.x.shape[1], A.x.shape[2]
    KT, FT, HALF = D // P, D // P, S // 2
    C_A, X_A, B_A, X_B, G_B, GATE_A, GATE_B = 1, 2, 0, 3, 4, 5, 6
    ORDER = [C_A, X_A, B_A, X_B, G_B, GATE_A, GATE_B]
    NJ = len(ORDER)
    SLOT = [0, 1, 2, 0, 1, 2, 1]
    USES = [SLOT.count(s) for s in range(3)]
    ORD = [SLOT[:j].count(SLOT[j]) for j in range(NJ)]
    BACK = [next(b for b in range(1, 2 * NJ) if SLOT[(j - b) % NJ] == SLOT[j]) for j in range(NJ)]
    with ExitStack() as ctx:
        c = Core(nc, ctx)
        stage = c.sb("m1_stage", [P, 3, KT, P])
        w_hl = [c.sb(f"m1_w_hl{s}", [P, 2, KT, P], F32R) for s in range(3)]
        cw_a = c.sb("m1_conv_a_w", [P, FT, 3])
        cw_b = c.sb("m1_conv_b_w", [P, FT, 4])
        cols = c.sb("m1_cols", [P, 6, FT])
        CB, BA, BX, GA, GB, LAM = range(6)
        sp_t = c.sb("m1_softplus", [P, 6, FT])
        gate_w = c.sb("m1_gate_w", [P, 2, P])
        ca = c.sb("m1_ca", [P, S])
        cx = c.sb("m1_cx", [P, S + 2])
        acc = c.sb("m1_acc", [P, S])
        ya = c.sb("m1_ya", [P, S])
        xb = c.sb("m1_xb", [P, S + 3])
        u = c.sb("m1_u", [P, S])
        r = c.sb("m1_r", [P, S])
        gi = c.sb("m1_i", [P, S])
        a = c.sb("m1_a", [P, S])
        th = c.sb("m1_t", [P, S])
        g = c.sb("m1_g", [P, S])
        yb = c.sb("m1_yb", [P, S])
        sg = c.sb("m1_sg", [P, 2, S])
        ps = [c.ps(f"m1_ps{s}", [P, 2, HALF]) for s in range(3)]
        ps_g = c.ps("m1_ps_gate", [P, 2, HALF])
        loaded = c.sems("m1_w_loaded", 3)
        s_hi, s_lo, s_mm = c.sem("m1_w_high"), c.sem("m1_w_low"), c.sem("m1_products")
        s_par, s_zero, s_dv, s_spe = c.sem("m1_params"), c.sem("m1_zeroed"), c.sem("m1_dve_chain"), c.sem("m1_sp_exp")
        s_spc = c.sem("m1_sp_chain")
        s_ca, s_cx, s_ya, s_yast = c.sem("m1_ca_ready"), c.sem("m1_cx_ready"), c.sem("m1_ya_ready"), c.sem("m1_ya_stored")
        s_xb, s_u, s_gw = c.sem("m1_xb_ready"), c.sem("m1_u_ready"), c.sem("m1_gate_w_loaded")
        s_rmm, s_r, s_imm, s_i = c.sem("m1_r_product"), c.sem("m1_r_ready"), c.sem("m1_i_product"), c.sem("m1_i_ready")
        s_at, s_g, s_scan, s_yb, s_ybst = (c.sem("m1_a_t_ready"), c.sem("m1_g_ready"), c.sem("m1_scanned"),
                                           c.sem("m1_yb_ready"), c.sem("m1_yb_stored"))
        s_sga, s_sgb, s_sgast, s_sgbst = (c.sem("m1_sga_ready"), c.sem("m1_sgb_ready"), c.sem("m1_sga_stored"),
                                          c.sem("m1_sgb_stored"))
        s_b, s_q, s_root = c.sem("m1_b_ready"), c.sem("m1_ratio_ready"), c.sem("m1_root_ready")
        block = ctx.enter_context(nc.Block())
        w_v = A.w_in[0].rearrange("(k p) (j f m) -> p k j f m", p=P, m=P, f=FT)

        @block.sync
        def _(sp):
            def step(i):
                for j, col in enumerate(ORDER):
                    t, s = NJ * i + j, SLOT[j]
                    wait(sp, s_lo, t - BACK[j] + 1)
                    sp.dma_start(stage[:, s], w_v[:, :, col, i, :]).then_inc(loaded[s], 16)
                    if i == 0 and j == 1:
                        parameters()

            def parameters():
                with nc.allow_non_contiguous_dma(reason="per-channel constants as columns"):
                    for k in range(3):
                        sp.dma_start(cw_a[:, :, k], A.conv_a_w[0, k].rearrange("(f p) -> p f", p=P)).then_inc(s_par, 16)
                    for k in range(4):
                        sp.dma_start(cw_b[:, :, k], A.conv_b_w[0, k].rearrange("(f p) -> p f", p=P)).then_inc(s_par, 16)
                    for n, row in enumerate([A.conv_b_b[0], A.lru_ba[0], A.lru_bx[0], A.gate_bias[0, 0], A.gate_bias[0, 1],
                                             A.lru_lambda[0]]):
                        sp.dma_start(cols[:, n, :], row.rearrange("(f p) -> p f", p=P)).then_inc(s_par, 16)

            for i in range(FT):
                step(i)

        @block.gpsimd
        def _(pool):
            nc.gpsimd.memset(gate_w[:], 0.0).then_inc(s_zero, 1)
            nc.gpsimd.memset(cx[:, 0:2], 0.0).then_inc(s_zero, 1)
            nc.gpsimd.memset(xb[:, 0:3], 0.0).then_inc(s_zero, 1)
            pool.wait_ge(s_zero, 3)
            def step(i):
                wait(pool, s_imm, i)
                for n, w in enumerate([A.lru_wa, A.lru_wx]):
                    for b in range(2):
                        pool.dma_start(gate_w[64 * b:64 * b + 64, n, 64 * b:64 * b + 64],
                                       w[0].rearrange("(f b) d e -> f b d e", b=2)[i, b]).then_inc(s_gw, 16)
                pool.wait_ge(s_ya, i + 1)
                pool.dma_start(scr.ya[i], ya[:]).then_inc(s_yast, 16)
                pool.wait_ge(s_sga, i + 1)
                pool.dma_start(scr.sga[i], sg[:, 0]).then_inc(s_sgast, 16)
                pool.wait_ge(s_sgb, i + 1)
                pool.dma_start(scr.sgb[i], sg[:, 1]).then_inc(s_sgbst, 16)
                pool.wait_ge(s_yb, i + 1)
                pool.dma_start(scr.yb[i], yb[:]).then_inc(s_ybst, 16)
            for i in range(FT):
                step(i)
            for s in (s_yast, s_sgast, s_sgbst, s_ybst):
                pool.wait_ge(s, 16 * FT)

        NP_DMAS = 13

        @block.scalar
        def _(act):
            def split(i, j):
                t, s = NJ * i + j, SLOT[j]
                act.wait_ge(loaded[s], 16 * (USES[s] * i + ORD[j] + 1))
                wait(act, s_mm, t - BACK[j] + 1)
                nc.scalar.activation(w_hl[s][:, 0], stage[:, s], ACT.Copy).then_inc(s_hi, 1)

            def after(i, j):
                s = SLOT[j]
                pair = ps[s][:].rearrange("p h n -> p (h n)")
                if ORDER[j] == C_A:
                    act.wait_ge(s_mm, NJ * i + j + 1)
                    wait(act, s_cx, i)
                    nc.scalar.activation(ca[:], pair, ACT.Copy).then_inc(s_ca, 1)
                elif ORDER[j] == X_B:
                    act.wait_ge(s_mm, NJ * i + j + 1)
                    wait(act, s_u, i)
                    act.wait_ge(s_zero, 3)
                    nc.scalar.activation(xb[:, 3:S + 3], pair, ACT.Copy).then_inc(s_xb, 1)
                elif ORDER[j] == G_B:
                    act.wait_ge(s_mm, NJ * i + j + 1)
                    wait(act, s_yb, i)
                    nc.scalar.activation(g[:], pair, ACT.Gelu_apprx_tanh).then_inc(s_g, 1)
                elif ORDER[j] == GATE_A:
                    act.wait_ge(s_rmm, i + 1)
                    wait(act, s_at, 2 * i)
                    nc.scalar.activation(r[:], ps_g[:].rearrange("p h n -> p (h n)"), ACT.Sigmoid,
                                         bias=cols[:, BA, bass.ds(i, 1)]).then_inc(s_r, 1)
                    act.wait_ge(s_mm, NJ * i + j + 1)
                    wait(act, s_sgast, 16 * i)
                    nc.scalar.activation(sg[:, 0], pair, ACT.Sigmoid, bias=cols[:, GA, bass.ds(i, 1)]).then_inc(s_sga, 1)
                elif ORDER[j] == GATE_B:
                    act.wait_ge(s_mm, NJ * i + j + 1)
                    wait(act, s_sgbst, 16 * i)
                    nc.scalar.activation(sg[:, 1], pair, ACT.Sigmoid, bias=cols[:, GB, bass.ds(i, 1)]).then_inc(s_sgb, 1)
                    act.wait_ge(s_imm, i + 1)
                    wait(act, s_scan, i)
                    nc.scalar.activation(gi[:], ps_g[:].rearrange("p h n -> p (h n)"), ACT.Sigmoid,
                                         bias=cols[:, BX, bass.ds(i, 1)]).then_inc(s_i, 1)
                    act.wait_ge(s_r, i + 1)
                    nc.scalar.activation(a[:], r[:], ACT.Exp, scale=sp_t[:, 4, bass.ds(i, 1)]).then_inc(s_at, 1)
                    nc.scalar.activation(th[:], r[:], ACT.Tanh, scale=sp_t[:, 5, bass.ds(i, 1)]).then_inc(s_at, 1)
                    act.wait_ge(s_q, i + 1)
                    nc.scalar.activation(th[:], th[:], ACT.Sqrt, scale=2.0).then_inc(s_root, 1)

            def step(i):
                for j in range(NJ):
                    split(i, j)
                    if j >= 2:
                        after(i, j - 2)
                    elif not (isinstance(i, int) and i == 0):
                        after(i - 1, j - 2 + NJ)
                    elif j == 1:
                        act.wait_ge(s_par, 16 * NP_DMAS)
                        act.wait_ge(s_spc, 1)
                        nc.scalar.activation(sp_t[:, 1], sp_t[:, 0], ACT.Exp, scale=-1.0).then_inc(s_spe, 1)
                        act.wait_ge(s_spc, SPC)

            SPC = 20
            steps(act, FT, step)
            after(FT - 1, NJ - 2)
            after(FT - 1, NJ - 1)

        @block.vector
        def _(dve):
            v = nc.vector
            chain = Chain(dve, s_dv, 9)

            def split(i, j):
                s = SLOT[j]
                dve.wait_ge(s_hi, NJ * i + j + 1)
                v.tensor_tensor(w_hl[s][:, 1], stage[:, s], f32(w_hl[s][:, 0]), ALU.subtract).then_inc(s_lo, 1)

            def after(i, j):
                s = SLOT[j]
                pair = ps[s][:].rearrange("p h n -> p (h n)")
                w = lambda t, k: t[:, bass.ds(i, 1), k:k + 1].rearrange("p a b -> p (a b)")
                if ORDER[j] == X_A:
                    chain.start(i)
                    dve.wait_ge(s_mm, NJ * i + j + 1)
                    dve.wait_ge(s_ca, i + 1)
                    v.tensor_tensor(cx[:, 2:S + 2], ca[:], pair, ALU.mult).then_inc(s_cx, 1)
                    dve.wait_ge(s_cx, i + 1)
                    chain.link(v.tensor_scalar(acc[:], cx[:, 0:S], w(cw_a, 0), None, ALU.mult))
                    chain.link(v.scalar_tensor_tensor(acc[:], cx[:, 1:S + 1], w(cw_a, 1), acc[:], ALU.mult, ALU.add))
                    chain.link(v.scalar_tensor_tensor(acc[:], cx[:, 2:S + 2], w(cw_a, 2), acc[:], ALU.mult, ALU.add))
                elif ORDER[j] == B_A:
                    dve.wait_ge(s_mm, NJ * i + j + 1)
                    wait(dve, s_yast, 16 * i)
                    v.tensor_tensor(ya[:], acc[:], pair, ALU.mult).then_inc(s_ya, 1)
                elif ORDER[j] == X_B:
                    dve.wait_ge(s_xb, i + 1)
                    chain.link(v.tensor_scalar(u[:], xb[:, 0:S], w(cw_b, 0), cols[:, CB, bass.ds(i, 1)], ALU.mult, ALU.add))
                    for k in (1, 2):
                        chain.link(v.scalar_tensor_tensor(u[:], xb[:, k:S + k], w(cw_b, k), u[:], ALU.mult, ALU.add))
                    v.scalar_tensor_tensor(u[:], xb[:, 3:S + 3], w(cw_b, 3), u[:], ALU.mult, ALU.add).then_inc(s_u, 1)
                elif ORDER[j] == GATE_B:
                    chain.start(i, 6)
                    dve.wait_ge(s_at, 2 * i + 2)
                    dve.wait_ge(s_i, i + 1)
                    chain.link(v.tensor_scalar(acc[:], th[:], 1.0, None, ALU.add))
                    chain.inc(v.tensor_tensor(gi[:], gi[:], u[:], ALU.mult))
                    chain.link(v.reciprocal(acc[:], acc[:]))
                    v.tensor_tensor(th[:], th[:], acc[:], ALU.mult).then_inc(s_q, 1)
                    dve.wait_ge(s_root, i + 1)
                    v.tensor_tensor(th[:], th[:], gi[:], ALU.mult).then_inc(s_b, 1)
                    dve.wait_ge(s_b, i + 1)
                    v.tensor_tensor_scan(acc[:], a[:], th[:], 0.0, ALU.mult, ALU.add).then_inc(s_scan, 1)
                    dve.wait_ge(s_scan, i + 1)
                    dve.wait_ge(s_g, i + 1)
                    wait(dve, s_ybst, 16 * i)
                    v.tensor_tensor(yb[:], acc[:], g[:], ALU.mult).then_inc(s_yb, 1)
                    chain.end()

            def softplus():
                dve.wait_ge(s_zero, 3)
                c0 = Chain(dve, s_spc)
                dve.wait_ge(s_par, 16 * NP_DMAS)
                c0.link(v.scalar_tensor_tensor(sp_t[:, 0], cols[:, LAM], -1.0, cols[:, LAM], ALU.mult, ALU.max))
                dve.wait_ge(s_spe, 1)
                log1p_exp_neg(nc, c0, sp_t[:, 1], sp_t[:, 2], sp_t[:, 3], sp_t[:, 5])
                c0.link(v.tensor_scalar(sp_t[:, 0], cols[:, LAM], -1.0, 0.0, ALU.mult, ALU.max))
                c0.link(v.tensor_tensor(sp_t[:, 5], sp_t[:, 5], sp_t[:, 0], ALU.add))
                c0.link(v.tensor_scalar(sp_t[:, 4], sp_t[:, 5], -8.0, None, ALU.mult))
                c0.link(v.tensor_scalar(sp_t[:, 5], sp_t[:, 5], 8.0, None, ALU.mult))

            def step(i):
                for j in range(NJ):
                    split(i, j)
                    if j >= 2:
                        after(i, j - 2)
                    elif not (isinstance(i, int) and i == 0):
                        after(i - 1, j - 2 + NJ)
                    elif j == 1:
                        softplus()
            steps(dve, FT, step)
            after(FT - 1, NJ - 2)
            after(FT - 1, NJ - 1)

        @block.tensor
        def _(pe):
            def gate(i, n, done, prev, prev_value):
                wait(pe, prev, prev_value)
                for h in range(2):
                    last = nc.tensor.matmul(ps_g[:, h], gate_w[:, n], u[:, h * HALF:(h + 1) * HALF], start=True, stop=True)
                last.then_inc(done, 1)

            def step(i):
                for j in range(NJ):
                    s = SLOT[j]
                    pe.wait_ge(s_lo, NJ * i + j + 1)
                    prev, pi = (j - BACK[j], i) if j >= BACK[j] else (j - BACK[j] + NJ, i - 1)
                    if not (isinstance(pi, int) and pi < 0):
                        sem, per_step = {C_A: (s_ca, 1), X_A: (s_cx, 1), B_A: (s_ya, 1), X_B: (s_xb, 1), G_B: (s_g, 1),
                                         GATE_A: (s_sga, 1), GATE_B: (s_sgb, 1)}[ORDER[prev]]
                        wait(pe, sem, pi + 1)
                    for k in range(KT):
                        for h in range(2):
                            last = mm3(nc, ps[s][:, h], (w_hl[s][:, 0, k], w_hl[s][:, 1, k]),
                                       (h_hl[:, 0, k, h * HALF:(h + 1) * HALF], h_hl[:, 1, k, h * HALF:(h + 1) * HALF]),
                                       k == 0, k == KT - 1)
                    last.then_inc(s_mm, 1)
                    if ORDER[j] == G_B:
                        pe.wait_ge(s_u, i + 1)
                        pe.wait_ge(s_gw, 64 * (i + 1))
                        gate(i, 0, s_rmm, s_i, i)
                    if ORDER[j] == GATE_A:
                        gate(i, 1, s_imm, s_r, i + 1)
            steps(pe, FT, step)


def merge_mixers(nc, A, scr, hl):
    S, D = A.x.shape[1], A.x.shape[2]
    KT, HALF = D // P, S // 2
    with ExitStack() as ctx:
        c = Core(nc, ctx)
        yb_hl = c.sb("mg_yb_hl", [P, 2, KT, S], F32R)
        NY = 3
        ystage = c.sb("mg_y_stage", [P, NY, S])
        sg = c.sb("mg_sg", [P, 2, S])
        part = c.sb("mg_part", [P, KT, S])
        stage = c.sb("mg_stage", [P, 2, KT, P])
        w_hl = [c.sb(f"mg_w_hl{s}", [P, 2, KT, P], F32R) for s in range(2)]
        ps = [c.ps(f"mg_ps{s}", [P, 2, HALF]) for s in range(2)]
        y_in, w_in, g_in = c.sems("mg_y_loaded", NY), c.sems("mg_w_loaded", 2), c.sems("mg_sg_loaded", 2)
        s_yh, s_yl, s_wh, s_wl = c.sem("mg_y_high"), c.sem("mg_y_low"), c.sem("mg_w_high"), c.sem("mg_w_low")
        s_mm, s_read, s_sum, s_mh, s_ml = (c.sem("mg_products"), c.sem("mg_gated"), c.sem("mg_summed"),
                                                  c.sem("mg_high"), c.sem("mg_low"))
        block = ctx.enter_context(nc.Block())
        w_v = [w[0].rearrange("(k p) (m n) -> p k m n", p=P, n=P) for w in (A.w_out_a, A.w_out_b)]
        ysplit = [(hl, k) for k in range(KT)] + [(yb_hl, k) for k in range(KT)]

        order = [("w", 0)] + [("y", n) for n in range(KT)] + [("w", 1), ("y", KT)]
        later = [[("w", t)] + [("y", KT + t - 1)] * (t <= KT) for t in range(2, 2 * KT)]

        @block.sync
        def _(sp):
            for what, n in order + sum(later, []):
                if what == "w":
                    q, m = divmod(n, KT)
                    wait(sp, s_wl, n - 1)
                    sp.dma_start(stage[:, n % 2], w_v[q][:, :, m, :]).then_inc(w_in[n % 2], 16)
                else:
                    wait(sp, s_yl, n - NY + 1)
                    sp.dma_start(ystage[:, n % NY], (scr.ya if n < KT else scr.yb)[n % KT]).then_inc(y_in[n % NY], 16)

        @block.gpsimd
        def _(pool):
            for n in range(2 * KT):
                wait(pool, s_read, min(n - 1, KT))
                wait(pool, s_sum, n - 1 - KT)
                pool.dma_start(sg[:, n % 2], (scr.sga if n < KT else scr.sgb)[n % KT]).then_inc(g_in[n % 2], 16)

        @block.scalar
        def _(act):
            def high(what, n):
                if what == "w":
                    act.wait_ge(w_in[n % 2], 16 * (n // 2 + 1))
                    wait(act, s_mm, n - 1)
                    nc.scalar.activation(w_hl[n % 2][:, 0], stage[:, n % 2], ACT.Copy).then_inc(s_wh, 1)
                else:
                    dst, k = ysplit[n]
                    act.wait_ge(y_in[n % NY], 16 * (n // NY + 1))
                    nc.scalar.activation(dst[:, 0, k], ystage[:, n % NY], ACT.Copy).then_inc(s_yh, 1)

            def result_high(m):
                act.wait_ge(s_sum, m + 1)
                nc.scalar.activation(hl[:, 0, m], part[:, m], ACT.Copy).then_inc(s_mh, 1)

            for what, n in order:
                high(what, n)
            for t in range(2, 2 * KT):
                for what, n in later[t - 2]:
                    high(what, n)
                if t > KT + 1:
                    result_high(t - 2 - KT)
            for m in range(KT - 2, KT):
                result_high(m)

        @block.vector
        def _(dve):
            v = nc.vector

            def low(what, n):
                if what == "w":
                    dve.wait_ge(s_wh, n + 1)
                    v.tensor_tensor(w_hl[n % 2][:, 1], stage[:, n % 2], f32(w_hl[n % 2][:, 0]), ALU.subtract).then_inc(s_wl, 1)
                else:
                    dst, k = ysplit[n]
                    dve.wait_ge(s_yh, n + 1)
                    v.tensor_tensor(dst[:, 1, k], ystage[:, n % NY], f32(dst[:, 0, k]), ALU.subtract).then_inc(s_yl, 1)

            def gate(t):
                m = t % KT
                pair = ps[t % 2][:].rearrange("p h n -> p (h n)")
                dve.wait_ge(s_mm, t + 1)
                dve.wait_ge(g_in[t % 2], 16 * (t // 2 + 1))
                if t < KT:
                    v.tensor_tensor(part[:, m], sg[:, t % 2], pair, ALU.mult).then_inc(s_read, 1)
                    return
                v.tensor_tensor(sg[:, t % 2], sg[:, t % 2], pair, ALU.mult).then_inc(s_read, 1)
                dve.wait_ge(s_read, t + 1)
                v.tensor_tensor(part[:, m], part[:, m], sg[:, t % 2], ALU.add).then_inc(s_sum, 1)

            def result_low(m):
                dve.wait_ge(s_mh, m + 1)
                v.tensor_tensor(hl[:, 1, m], part[:, m], f32(hl[:, 0, m]), ALU.subtract).then_inc(s_ml, 1)

            for what, n in order:
                low(what, n)
            for t in range(2 * KT):
                gate(t)
                if t + 2 < 2 * KT:
                    for what, n in later[t]:
                        low(what, n)
                if t > KT:
                    result_low(t - 1 - KT)
            result_low(KT - 1)

        @block.tensor
        def _(pe):
            for t in range(2 * KT):
                pe.wait_ge(s_wl, t + 1)
                wait(pe, s_read, t - 1)
                x_hl = hl if t < KT else yb_hl
                for k in range(KT):
                    if t % KT == 0:
                        pe.wait_ge(s_yl, (t // KT) * KT + k + 1)
                    for h in range(2):
                        last = mm3(nc, ps[t % 2][:, h], (w_hl[t % 2][:, 0, k], w_hl[t % 2][:, 1, k]),
                                   (x_hl[:, 0, k, h * HALF:(h + 1) * HALF], x_hl[:, 1, k, h * HALF:(h + 1) * HALF]),
                                   k == 0, k == KT - 1)
                last.then_inc(s_mm, 1)


def add_product(nc, tag, x_tm, hl, w_v, x_dram=None, norm=None):
    tiles, D = x_tm.shape[1], x_tm.shape[2]
    HALF, K = D // 2, hl.shape[2]
    NB, NS = 4, 4
    with ExitStack() as ctx:
        c = Core(nc, ctx)
        stage = c.sb(f"{tag}_stage", [P, NS, HALF])
        w_hl = [c.sb(f"{tag}_w_hl{h}", [P, 2, K, HALF], F32R) for h in range(2)]
        ps = [c.ps(f"{tag}_ps{b}", [P, HALF]) for b in range(NB)]
        s_w, s_x = c.sems(f"{tag}_w_loaded", NS), c.sem(f"{tag}_x_loaded")
        s_hi, s_lo, s_mm, s_add = c.sem(f"{tag}_w_high"), c.sem(f"{tag}_w_low"), c.sem(f"{tag}_products"), c.sem(f"{tag}_added")
        if norm is not None:
            norm_tag, gain_row, more = norm
            (loads, stores, on_pool, measure, scale, high, invert, gained, low, turn) = norm_parts(
                nc, c, norm_tag, x_tm, gain_row, hl, x_ready=lambda eng, t: eng.wait_ge(s_add, 2 * t + 2), **more)
        block = ctx.enter_context(nc.Block())

        @block.sync
        def _(sp):
            for n in range(2 * K):
                h, k = divmod(n, K)
                wait(sp, s_lo, n - NS + 1)
                sp.dma_start(stage[:, n % NS], w_v[:, k, h * HALF:(h + 1) * HALF]).then_inc(s_w[n % NS], 16)
            if norm is not None:
                loads(sp)
                stores(sp)

        @block.gpsimd
        def _(pool):
            if x_dram is not None:
                pool.dma_start(x_tm[:], x_dram.rearrange("(t p) d -> p t d", p=P)).then_inc(s_x, 16)
                pool.wait_ge(s_x, 16)
            if norm is not None:
                on_pool(pool)

        @block.scalar
        def _(act):
            for n in range(2 * K):
                h, k = divmod(n, K)
                act.wait_ge(s_w[n % NS], 16 * (n // NS + 1))
                nc.scalar.activation(w_hl[h][:, 0, k], stage[:, n % NS], ACT.Copy).then_inc(s_hi, 1)
            if norm is not None:
                for t in range(tiles):
                    measure(act, t)
                    scale(act, t)
                    if t:
                        high(act, t - 1)
                high(act, tiles - 1)

        @block.vector
        def _(dve):
            for n in range(2 * K):
                h, k = divmod(n, K)
                dve.wait_ge(s_hi, n + 1)
                nc.vector.tensor_tensor(w_hl[h][:, 1, k], stage[:, n % NS], f32(w_hl[h][:, 0, k]), ALU.subtract).then_inc(s_lo, 1)
            if x_dram is not None:
                dve.wait_ge(s_x, 16)
            for t in range(tiles):
                for h in range(2):
                    g = 2 * t + h
                    dve.wait_ge(s_mm, g + 1)
                    dst = x_tm[:, t, h * HALF:(h + 1) * HALF]
                    nc.vector.tensor_tensor(dst, dst, ps[g % NB][:], ALU.add).then_inc(s_add, 1)
                if norm is not None:
                    invert(dve, t)
                    if t:
                        gained(dve, t - 1)
                        low(dve, t - 1)
            if norm is not None:
                gained(dve, tiles - 1)
                low(dve, tiles - 1)

        @block.tensor
        def _(pe):
            for t in range(tiles):
                tok = slice(t * P, (t + 1) * P)
                for h in range(2):
                    g = 2 * t + h
                    wait(pe, s_add, g - NB + 1)
                    for k in range(K):
                        if t == 0:
                            pe.wait_ge(s_lo, h * K + k + 1)
                        last = mm3(nc, ps[g % NB][:], (hl[:, 0, k, tok], hl[:, 1, k, tok]),
                                   (w_hl[h][:, 0, k], w_hl[h][:, 1, k]), k == 0, k == K - 1)
                    last.then_inc(s_mm, 1)
                if norm is not None and t:
                    turn(pe, t - 1)
            if norm is not None:
                turn(pe, tiles - 1)


def feed_forward(nc, A, x_tm, hl):
    tiles, D = x_tm.shape[1], x_tm.shape[2]
    S = tiles * P
    KT, HALF = D // P, 512
    NF = A.w_ffn_gate.shape[2] // P
    assert NF % 2 == 0
    ND = 2 * tiles
    NB = 4
    with ExitStack() as ctx:
        c = Core(nc, ctx)
        st = c.sb("ff_stage", [P, 3, S])
        wg_hl = [[c.sb(f"ff_w{n}{b}", [P, 2, KT, P], F32R) for b in range(2)] for n in "gu"]
        wd_hl = [c.sb(f"ff_wd{b}", [P, 2, D], F32R) for b in range(2)]
        silu = c.sb("ff_silu", [P, S])
        act_f = c.sb("ff_act", [P, S])
        a_hl = [c.sb(f"ff_act_hl{b}", [P, 2, S], F32R) for b in range(2)]
        ps_gu = [c.ps(f"ff_ps{n}", [P, 2, HALF]) for n in "gu"]
        ps_d = [c.ps(f"ff_psd{b}", [P, HALF]) for b in range(NB)]
        w_in = c.sems("ff_w_loaded", 3)
        s_hi, s_lo = c.sems("ff_w_high", 3), c.sems("ff_w_low", 3)
        s_g, s_u, s_d, s_down = c.sem("ff_gate_done"), c.sem("ff_up_done"), c.sem("ff_piece_done"), c.sem("ff_down_done")
        s_silu, s_act, s_ah, s_al, s_add = (c.sem("ff_silu_ready"), c.sem("ff_act_ready"), c.sem("ff_act_high"),
                                            c.sem("ff_act_low"), c.sem("ff_added"))
        block = ctx.enter_context(nc.Block())
        w_v = [w[0].rearrange("(k p) (f m) -> p k f m", p=P, m=P) for w in (A.w_ffn_gate, A.w_ffn_up)]
        wd_v = A.w_ffn_down[0].rearrange("(f p) n -> p f n", p=P)
        stage2 = [st[:, n].rearrange("p (k m) -> p k m", m=P) for n in range(2)]

        @block.sync
        def _(sp):
            def step(i):
                for b in range(2):
                    f = 2 * i + b
                    for n in range(2):
                        wait(sp, s_lo[n], f)
                        sp.dma_start(stage2[n], w_v[n][:, :, f, :]).then_inc(w_in[n], 16)
                    wait(sp, s_lo[2], f)
                    sp.dma_start(st[:, 2], wd_v[:, f, :]).then_inc(w_in[2], 16)
            for i in range(NF // 2):
                step(i)

        @block.scalar
        def _(act):
            def high(n, f, b):
                act.wait_ge(w_in[n], 16 * (f + 1))
                wait(act, (s_g, s_u, s_down)[n], f - 1)
                if n < 2:
                    nc.scalar.activation(wg_hl[n][b][:, 0], stage2[n], ACT.Copy).then_inc(s_hi[n], 1)
                else:
                    nc.scalar.activation(wd_hl[b][:, 0], st[:, 2], ACT.Copy).then_inc(s_hi[2], 1)

            def step(i, last=False):
                for b in range(2):
                    f = 2 * i + b
                    if isinstance(i, int) and i == 0 and b == 0:
                        high(0, 0, 0)
                        high(1, 0, 0)
                    if not (last and b == 1):
                        high(0, f + 1, 1 - b)
                        high(1, f + 1, 1 - b)
                    high(2, f, b)
                    act.wait_ge(s_g, f + 1)
                    wait(act, s_act, f)
                    nc.scalar.activation(silu[:], ps_gu[0][:].rearrange("p h n -> p (h n)"), ACT.Silu).then_inc(s_silu, 1)
                    act.wait_ge(s_act, f + 1)
                    wait(act, s_down, f - 1)
                    nc.scalar.activation(a_hl[b][:, 0], act_f[:], ACT.Copy).then_inc(s_ah, 1)
            steps(act, NF // 2, step, end=NF // 2 - 1)
            step(NF // 2 - 1, True)

        @block.vector
        def _(dve):
            v = nc.vector

            def low(n, f, b):
                dve.wait_ge(s_hi[n], f + 1)
                if n < 2:
                    v.tensor_tensor(wg_hl[n][b][:, 1], stage2[n], f32(wg_hl[n][b][:, 0]), ALU.subtract).then_inc(s_lo[n], 1)
                else:
                    v.tensor_tensor(wd_hl[b][:, 1], st[:, 2], f32(wd_hl[b][:, 0]), ALU.subtract).then_inc(s_lo[2], 1)

            def add_down(f):
                for g in range(ND):
                    t, h = divmod(g, 2)
                    dve.wait_ge(s_d, ND * f + g + 1)
                    dst = x_tm[:, t, h * HALF:(h + 1) * HALF]
                    v.tensor_tensor(dst, dst, ps_d[g % NB][:], ALU.add).then_inc(s_add, 1)

            def step(i, last=False):
                for b in range(2):
                    f = 2 * i + b
                    if isinstance(i, int) and i == 0 and b == 0:
                        low(0, 0, 0)
                        low(1, 0, 0)
                    if not (last and b == 1):
                        low(0, f + 1, 1 - b)
                        low(1, f + 1, 1 - b)
                    low(2, f, b)
                    if not (isinstance(i, int) and i == 0 and b == 0):
                        add_down(f - 1)
                    dve.wait_ge(s_u, f + 1)
                    dve.wait_ge(s_silu, f + 1)
                    wait(dve, s_ah, f)
                    wait(dve, s_al, f)
                    v.tensor_tensor(act_f[:], silu[:], ps_gu[1][:].rearrange("p h n -> p (h n)"), ALU.mult).then_inc(s_act, 1)
                    dve.wait_ge(s_ah, f + 1)
                    v.tensor_tensor(a_hl[b][:, 1], act_f[:], f32(a_hl[b][:, 0]), ALU.subtract).then_inc(s_al, 1)
            steps(dve, NF // 2, step, end=NF // 2 - 1)
            step(NF // 2 - 1, True)
            add_down(NF - 1)

        @block.tensor
        def _(pe):
            def down(f, b):
                pe.wait_ge(s_al, f + 1)
                pe.wait_ge(s_lo[2], f + 1)
                for g in range(ND):
                    t, h = divmod(g, 2)
                    tok = slice(t * P, (t + 1) * P)
                    cols = slice(h * HALF, (h + 1) * HALF)
                    wait(pe, s_add, ND * f + g - NB + 1)
                    last = mm3(nc, ps_d[g % NB][:], (a_hl[b][:, 0, tok], a_hl[b][:, 1, tok]),
                               (wd_hl[b][:, 0, cols], wd_hl[b][:, 1, cols]), True, True)
                    last.then_inc(s_d, 1)
                pe.wait_ge(s_d, ND * (f + 1))
                pe.sem_inc(s_down, 1)

            def step(i):
                for b in range(2):
                    f = 2 * i + b
                    for n, (read, done) in enumerate([(s_silu, s_g), (s_act, s_u)]):
                        pe.wait_ge(s_lo[n], f + 1)
                        wait(pe, read, f)
                        for k in range(KT):
                            for h in range(2):
                                last = mm3(nc, ps_gu[n][:, h], (wg_hl[n][b][:, 0, k], wg_hl[n][b][:, 1, k]),
                                           (hl[:, 0, k, h * HALF:(h + 1) * HALF], hl[:, 1, k, h * HALF:(h + 1) * HALF]),
                                           k == 0, k == KT - 1)
                        last.then_inc(done, 1)
                    if not (isinstance(i, int) and i == 0 and b == 0):
                        down(f - 1, 1 - b)
            steps(pe, NF // 2, step)
            down(NF - 1, 1)


def narrow_rows(nc, ps, w_hl, hl):
    KT, HALF = hl.shape[2], ps.shape[2]
    for k in range(KT):
        for h in range(2):
            last = mm3(nc, ps[:, h], (w_hl[:, 0, k], w_hl[:, 1, k]),
                       (hl[:, 0, k, h * HALF:(h + 1) * HALF], hl[:, 1, k, h * HALF:(h + 1) * HALF]), k == 0, k == KT - 1)
    return last


def turn_rows(nc, ps, rows, ident):
    n = rows.shape[0]
    for t in range(ps.shape[1]):
        last = nc.tensor.transpose(ps[:, t], rows[:, t * P:(t + 1) * P], ident[0:n, 0:n])
    return last


def row_product(nc, tag, hl, w_v, out, func, gates=None):
    KT, S = hl.shape[2], hl.shape[3]
    tiles, HALF = S // P, 512
    NH = w_v.shape[2] // HALF
    NB, NS = 4, 4
    with ExitStack() as ctx:
        c = Core(nc, ctx)
        stage = c.sb(f"{tag}_stage", [P, NS, HALF])
        w_hl = [c.sb(f"{tag}_w_hl{h}", [P, 2, KT, HALF], F32R) for h in range(NH)]
        ps = [c.ps(f"{tag}_ps{b}", [P, HALF]) for b in range(NB)]
        s_w = c.sems(f"{tag}_w_loaded", NS)
        s_hi, s_lo, s_mm, s_out = c.sem(f"{tag}_w_high"), c.sem(f"{tag}_w_low"), c.sem(f"{tag}_products"), c.sem(f"{tag}_out")
        if gates is not None:
            NG = gates[0].shape[2]
            gstage = c.sb(f"{tag}_g_stage", [P, KT, NG])
            g_hl = c.sb(f"{tag}_g_hl", [P, 2, KT, NG], F32R)
            g_rows, ident = c.sb(f"{tag}_g_rows", [NG, S]), c.sb(f"{tag}_ident", [P, P])
            ps_g, ps_gr = c.ps(f"{tag}_ps_g", [P, tiles, NG]), c.ps(f"{tag}_ps_g_rows", [NG, 2, HALF])
            s_id, s_id0, s_gt = c.sem(f"{tag}_ident_ready"), c.sem(f"{tag}_ident_steps"), c.sem(f"{tag}_g_turned")
            s_g = c.sem(f"{tag}_g_loaded")
            s_gh, s_gl, s_gm, s_go = c.sem(f"{tag}_g_high"), c.sem(f"{tag}_g_low"), c.sem(f"{tag}_g_products"), c.sem(f"{tag}_g_out")
        block = ctx.enter_context(nc.Block())

        @block.sync
        def _(sp):
            for n in range(NH * KT):
                h, k = divmod(n, KT)
                wait(sp, s_lo, n - NS + 1)
                sp.dma_start(stage[:, n % NS], w_v[:, k, h * HALF:(h + 1) * HALF]).then_inc(s_w[n % NS], 16)
            if gates is not None:
                with nc.allow_non_contiguous_dma(reason="a few gate columns"):
                    for src, off, n in gates[2]:
                        sp.dma_start(gstage[:, :, off:off + n], src).then_inc(s_g, 16)

        @block.scalar
        def _(act):
            def high(n):
                h, k = divmod(n, KT)
                act.wait_ge(s_w[n % NS], 16 * (n // NS + 1))
                nc.scalar.activation(w_hl[h][:, 0, k], stage[:, n % NS], ACT.Copy).then_inc(s_hi, 1)

            for n in range(KT):
                high(n)
            for g in range(NH * tiles):
                h, t = divmod(g, tiles)
                if h + 1 < NH:
                    high(KT * (h + 1) + t)
                if gates is not None and g == NH * tiles // 2 + 2:
                    act.wait_ge(s_g, 16 * len(gates[2]))
                    nc.scalar.activation(g_hl[:, 0], gstage[:], ACT.Copy).then_inc(s_gh, 1)
                act.wait_ge(s_mm, g + 1)
                if len(out.shape) == 3:
                    dst, src = out[:, t, h * HALF:(h + 1) * HALF], ps[g % NB][:]
                else:
                    dst = out[:, t, h * HALF // P:(h + 1) * HALF // P, 0:P]
                    src = ps[g % NB][:].rearrange("p (a b) -> p a b", b=P)
                nc.scalar.activation(dst, src, func).then_inc(s_out, 1)

        @block.vector
        def _(dve):
            for n in range(NH * KT):
                h, k = divmod(n, KT)
                dve.wait_ge(s_hi, n + 1)
                nc.vector.tensor_tensor(w_hl[h][:, 1, k], stage[:, n % NS], f32(w_hl[h][:, 0, k]), ALU.subtract).then_inc(s_lo, 1)
            if gates is not None:
                dve.wait_ge(s_gh, 1)
                nc.vector.tensor_tensor(g_hl[:, 1], gstage[:], f32(g_hl[:, 0]), ALU.subtract).then_inc(s_gl, 1)
                dve.wait_ge(s_gm, 1)
                nc.vector.tensor_copy(g_rows[:], ps_gr[:].rearrange("p h n -> p (h n)")).then_inc(s_go, 1)
                dve.wait_ge(s_gt, 1)
                nc.vector.tensor_copy(gates[1][:], ps_g[:]).then_inc(s_go, 1)

        @block.gpsimd
        def _(pool):
            if gates is not None:
                identity(nc, pool, s_id, s_id0, ident[:], 0)

        @block.tensor
        def _(pe):
            for g in range(NH * tiles):
                h, t = divmod(g, tiles)
                tok = slice(t * P, (t + 1) * P)
                wait(pe, s_out, g - NB + 1)
                for k in range(KT):
                    if t == 0:
                        pe.wait_ge(s_lo, h * KT + k + 1)
                    last = mm3(nc, ps[g % NB][:], (hl[:, 0, k, tok], hl[:, 1, k, tok]), (w_hl[h][:, 0, k], w_hl[h][:, 1, k]),
                               k == 0, k == KT - 1)
                last.then_inc(s_mm, 1)
            if gates is not None:
                pe.wait_ge(s_gl, 1)
                narrow_rows(nc, ps_gr, g_hl, hl).then_inc(s_gm, 1)
                pe.wait_ge(s_id, 1)
                pe.wait_ge(s_go, 1)
                turn_rows(nc, ps_g, g_rows, ident).then_inc(s_gt, 1)


def column_product(nc, tag, hl, w_v, n, out=None, conv=None, gain=None, store=None):
    KT, S = hl.shape[2], hl.shape[3]
    HALF = S // 2
    assert n % 2 == 0
    with ExitStack() as ctx:
        c = Core(nc, ctx)
        stage = c.sb(f"{tag}_stage", [P, 2, KT, P])
        w_hl = [c.sb(f"{tag}_w_hl{b}", [P, 2, KT, P], F32R) for b in range(2)]
        ps = [c.ps(f"{tag}_ps{b}", [P, 2, HALF]) for b in range(2)]
        s_w = c.sems(f"{tag}_w_loaded", 2)
        s_hi, s_lo, s_mm, s_read = c.sem(f"{tag}_w_high"), c.sem(f"{tag}_w_low"), c.sem(f"{tag}_products"), c.sem(f"{tag}_psum_read")
        s_par, s_dv, s_res = c.sem(f"{tag}_params"), c.sem(f"{tag}_dve_chain"), c.sem(f"{tag}_result")
        s_fin, s_zero = c.sem(f"{tag}_finished"), c.sem(f"{tag}_zeroed")
        if conv is not None:
            K = conv[0].shape[0]
            xb = [c.sb(f"{tag}_x{b}", [P, S + K - 1]) for b in range(2)]
            u = [c.sb(f"{tag}_u{b}", [P, S]) for b in range(2)]
            cw = c.sb(f"{tag}_conv_w", [P, n, K])
            cb = c.sb(f"{tag}_conv_b", [P, n])
        else:
            res = c.sb(f"{tag}_res", [P, 2, S])
            cb = c.sb(f"{tag}_gain", [P, n])
            s_st = c.sem(f"{tag}_stored0"), c.sem(f"{tag}_stored1")
        block = ctx.enter_context(nc.Block())

        @block.sync
        def _(sp):
            for f in range(n):
                wait(sp, s_lo, f - 1)
                sp.dma_start(stage[:, f % 2], w_v[:, :, f, :]).then_inc(s_w[f % 2], 16)

        @block.gpsimd
        def _(pool):
            with nc.allow_non_contiguous_dma(reason="per-channel constants as columns"):
                pool.dma_start(cb[:], (conv[1] if conv is not None else gain).rearrange("(f p) -> p f", p=P)).then_inc(s_par, 16)
                if conv is not None:
                    for k in range(K):
                        pool.dma_start(cw[:, :, k], conv[0][k].rearrange("(f p) -> p f", p=P)).then_inc(s_par, 16)
                    for b in range(2):
                        nc.gpsimd.memset(xb[b][:, 0:K - 1], 0.0).then_inc(s_zero, 1)
            if store is not None:
                for f in range(n):
                    pool.wait_ge(s_fin, f + 1)
                    pool.dma_start(store[f], res[:, f % 2]).then_inc(s_st[f % 2], 16)
                for b in range(2):
                    pool.wait_ge(s_st[b], 16 * (n // 2))
        NPAR = 16 * (1 + K) if conv is not None else 16

        @block.scalar
        def _(act):
            def high(f, b):
                act.wait_ge(s_w[b], 16 * (f // 2 + 1) if isinstance(f, int) else 8 * f + 16 - 8 * b)
                wait(act, s_mm, f - 1)
                nc.scalar.activation(w_hl[b][:, 0], stage[:, b], ACT.Copy).then_inc(s_hi, 1)

            def read(f, b):
                pair = ps[b][:].rearrange("p h n -> p (h n)")
                act.wait_ge(s_mm, f + 1)
                if conv is not None:
                    wait(act, s_res, f - 1)
                    nc.scalar.activation(xb[b][:, K - 1:], pair, ACT.Copy).then_inc(s_read, 1)
                else:
                    if isinstance(f, int):
                        wait(act, s_st[b], 16 * (f // 2))
                    else:
                        act.wait_ge(s_st[b], 8 * f - 8 * b)
                    nc.scalar.activation(res[:, b], pair, ACT.Sigmoid).then_inc(s_read, 1)

            def finish(f, b):
                if conv is not None:
                    act.wait_ge(s_res, f + 1)
                    nc.scalar.activation(out[:, bass.ds(f, 1)].rearrange("p a s -> p (a s)"), u[b][:], ACT.Silu).then_inc(s_fin, 1)

            def step(i):
                first = isinstance(i, int) and i == 0
                for b in range(2):
                    f = 2 * i + b
                    high(f, b)
                    if not (first and b == 0):
                        read(f - 1, 1 - b)
                    if not first:
                        finish(f - 2, b)
            if conv is not None:
                act.wait_ge(s_zero, 2)
            steps(act, n // 2, step)
            read(n - 1, 1)
            finish(n - 2, 0)
            finish(n - 1, 1)

        @block.vector
        def _(dve):
            v = nc.vector
            chain = Chain(dve, s_dv, K - 1 if conv is not None else 0)

            def low(f, b):
                dve.wait_ge(s_hi, f + 1)
                v.tensor_tensor(w_hl[b][:, 1], stage[:, b], f32(w_hl[b][:, 0]), ALU.subtract).then_inc(s_lo, 1)

            def work(f, b):
                dve.wait_ge(s_read, f + 1)
                col = cb[:, bass.ds(f, 1)]
                if conv is None:
                    v.tensor_scalar(res[:, b], res[:, b], col, None, ALU.mult).then_inc(s_fin, 1)
                    return
                chain.start(f)
                wait(dve, s_fin, f - 1)
                w = lambda k: cw[:, bass.ds(f, 1), k:k + 1].rearrange("p a b -> p (a b)")
                chain.link(v.tensor_scalar(u[b][:], xb[b][:, 0:S], w(0), col, ALU.mult, ALU.add))
                for k in range(1, K - 1):
                    chain.link(v.scalar_tensor_tensor(u[b][:], xb[b][:, k:S + k], w(k), u[b][:], ALU.mult, ALU.add))
                v.scalar_tensor_tensor(u[b][:], xb[b][:, K - 1:], w(K - 1), u[b][:], ALU.mult, ALU.add).then_inc(s_res, 1)

            def step(i):
                first = isinstance(i, int) and i == 0
                for b in range(2):
                    low(2 * i + b, b)
                    if not (first and b == 0):
                        work(2 * i + b - 1, 1 - b)
            dve.wait_ge(s_par, NPAR)
            if conv is not None:
                dve.wait_ge(s_zero, 2)
            steps(dve, n // 2, step)
            work(n - 1, 1)

        @block.tensor
        def _(pe):
            def step(i):
                for b in range(2):
                    f = 2 * i + b
                    pe.wait_ge(s_lo, f + 1)
                    wait(pe, s_read, f - 1)
                    for k in range(KT):
                        for h in range(2):
                            last = mm3(nc, ps[b][:, h], (w_hl[b][:, 0, k], w_hl[b][:, 1, k]),
                                       (hl[:, 0, k, h * HALF:(h + 1) * HALF], hl[:, 1, k, h * HALF:(h + 1) * HALF]),
                                       k == 0, k == KT - 1)
                    last.then_inc(s_mm, 1)
            steps(pe, n // 2, step)


SSD_HEADS, SSD_GROUPS, ML_HEADS = 16, 2, 8


def gate_values(nc, A, gates, scr):
    tiles = gates.shape[1]
    S = tiles * P
    HS, HM = SSD_HEADS, ML_HEADS
    with ExitStack() as ctx:
        c = Core(nc, ctx)
        bias = c.sb("gv_bias", [P, HS + 2 * HM])
        alog = c.sb("gv_alog", [P, HS])
        sgn = c.sb("gv_x", [P, tiles, HS + HM])
        t1, t2, t3, t4 = (c.sb(f"gv_t{n}", [P, tiles, HS + HM]) for n in range(4))
        ident = c.sb("gv_ident", [P, P])
        rows = c.sb("gv_rows", [HM, 2, S])
        ones = c.sb("gv_ones", [HM, P])
        b_r, u_r = c.sb("gv_b", [HM, S]), c.sb("gv_u", [HM, S])
        m0 = c.sb("gv_m0", [HM, tiles + 1])
        e_in = c.sb("gv_e_in", [HM, 3, S])
        e_out = c.sb("gv_e_out", [HM, 3, S])
        ps_r = c.ps("gv_ps_rows", [HM, 2, S])
        ps_c = c.ps("gv_ps_cols", [P, tiles, 4, HM])
        s_in, s_id, s_ch, s_e = c.sem("gv_loaded"), c.sem("gv_ident_ready"), c.sem("gv_dve_chain"), c.sem("gv_exp")
        s_gate, s_t, s_er, s_t2 = c.sem("gv_gates_ready"), c.sem("gv_rows_turned"), c.sem("gv_rows_exp"), c.sem("gv_cols_turned")
        s_rows, s_fin = c.sem("gv_rows_ready"), c.sem("gv_finished")
        block = ctx.enter_context(nc.Block())

        @block.sync
        def _(sp):
            for row, off in ((A.ssd_dt_bias_2[0], 0), (A.ml_i_bias_2[0], HS), (A.ml_f_bias_2[0], HS + HM)):
                n = row.shape[0]
                sp.dma_start(bias[:, off:off + n], row.rearrange("(a n) -> a n", a=1).broadcast_to([P, n])).then_inc(s_in, 16)
            sp.dma_start(alog[:], A.ssd_a_log_2[0].rearrange("(a n) -> a n", a=1).broadcast_to([P, HS])).then_inc(s_in, 16)

        @block.gpsimd
        def _(pool):
            nc.gpsimd.memset(ones[:], 1.0).then_inc(s_id, 1)
            nc.gpsimd.memset(ident[:], 0.0).then_inc(s_id, 1)
            nc.gpsimd.memset(m0[:, 0:1], -1e30).then_inc(s_id, 1)
            pool.wait_ge(s_id, 3)
            nc.gpsimd.affine_select(out=ident[:], in_=ident[:], compare_op=ALU.not_equal, fill=1.0, base=0,
                                    pattern=[[-1, P]], channel_multiplier=1).then_inc(s_id, 1)

        @block.vector
        def _(dve):
            v, ch = nc.vector, Chain(dve, s_ch)
            dve.wait_ge(s_in, 64)
            dve.wait_ge(s_id, 4)
            wide = lambda ap: ap.unsqueeze(1).to_broadcast([P, tiles, ap.shape[1]])
            ch.link(v.tensor_tensor(gates[:], gates[:], wide(bias[:]), ALU.add))
            ch.inc(v.tensor_copy(sgn[:, :, 0:HS], gates[:, :, 0:HS]))
            ch.link(v.tensor_scalar(sgn[:, :, HS:], gates[:, :, HS + HM:], -1.0, None, ALU.mult))
            ch.link(v.scalar_tensor_tensor(t1[:], sgn[:], -1.0, sgn[:], ALU.mult, ALU.max))
            dve.wait_ge(s_e, 1)
            log1p_exp_neg(nc, ch, t1[:], t2[:], t3[:], t4[:])
            ch.link(v.scalar_tensor_tensor(t4[:], sgn[:], 0.0, t4[:], ALU.max, ALU.add))
            ch.inc(v.tensor_copy(scr.dt[:], t4[:, :, 0:HS]))
            dve.wait_ge(s_e, 2)
            ch.inc(v.scalar_tensor_tensor(scr.adt[:], t4[:, :, 0:HS], -1.0, wide(alog[:]), ALU.mult, ALU.mult))
            v.tensor_scalar(t4[:, :, HS:], t4[:, :, HS:], -1.0, None, ALU.mult).then_inc(s_gate, 1)
            dve.wait_ge(s_t, 1)
            ch.link(v.tensor_copy(rows[:], ps_r[:]))
            for k in range(tiles):
                cut = slice(k * P, (k + 1) * P)
                last = slice((k + 1) * P - 1, (k + 1) * P)
                ch.link(v.tensor_tensor_scan(b_r[:, cut], ones[:], rows[:, 1, cut], 0.0, ALU.mult, ALU.add))
                ch.link(v.tensor_tensor(u_r[:, cut], rows[:, 0, cut], b_r[:, cut], ALU.subtract))
                ch.link(v.tensor_tensor_scan(scr.g[:, cut], u_r[:, cut], u_r[:, cut], m0[:, k:k + 1], ALU.max, ALU.max))
                ch.inc(v.tensor_tensor(m0[:, k + 1:k + 2], b_r[:, last], scr.g[:, last], ALU.add))
                ch.inc(v.tensor_scalar(e_in[:, 0, cut], scr.g[:, cut], m0[:, k:k + 1], -1.0, ALU.subtract, ALU.mult))
                ch.inc(v.scalar_tensor_tensor(e_in[:, 1, cut], b_r[:, cut], -1.0, scr.g[:, cut], ALU.mult, ALU.subtract))
                ch.link(v.tensor_scalar(e_in[:, 2, cut], u_r[:, cut], scr.g[:, last], None, ALU.subtract))
            v.tensor_copy(rows[:, 0], u_r[:]).then_inc(s_rows, 1)
            dve.wait_ge(s_t2, 1)
            v.tensor_copy(scr.cols[:], ps_c[:]).then_inc(s_fin, 1)

        @block.scalar
        def _(act):
            act.wait_ge(s_ch, 4)
            nc.scalar.activation(t1[:], t1[:], ACT.Exp, scale=-1.0).then_inc(s_e, 1)
            act.wait_ge(s_in, 64)
            nc.scalar.activation(alog[:], alog[:], ACT.Exp).then_inc(s_e, 1)
            act.wait_ge(s_rows, 1)
            nc.scalar.activation(e_out[:], e_in[:], ACT.Exp).then_inc(s_er, 1)

        @block.tensor
        def _(pe):
            pe.wait_ge(s_id, 4)
            pe.wait_ge(s_gate, 1)
            for k in range(tiles):
                cut = slice(k * P, (k + 1) * P)
                nc.tensor.transpose(ps_r[:, 0, cut], gates[:, k, HS:HS + HM], ident[:])
                last = nc.tensor.transpose(ps_r[:, 1, cut], t4[:, k, HS:], ident[:])
            last.then_inc(s_t, 1)
            pe.wait_ge(s_er, 1)
            for k in range(tiles):
                cut = slice(k * P, (k + 1) * P)
                for n in range(4):
                    src = rows[:, 0, cut] if n == 0 else e_out[:, n - 1, cut]
                    last = nc.tensor.transpose(ps_c[:, k, n], src, ident[0:HM, 0:HM])
            last.then_inc(s_t2, 1)


def triangle(nc, pool, s_done, s_step, upper, neg):
    nc.gpsimd.memset(upper, 1.0).then_inc(s_step, 1)
    nc.gpsimd.memset(neg, 0.0).then_inc(s_step, 1)
    pool.wait_ge(s_step, 2)
    nc.gpsimd.affine_select(out=upper, in_=upper, compare_op=ALU.is_ge, fill=0.0, base=0, pattern=[[1, P]],
                            channel_multiplier=-1).then_inc(s_done, 1)
    nc.gpsimd.affine_select(out=neg, in_=neg, compare_op=ALU.is_ge, fill=-1e30, base=0,
                            pattern=[[0, neg.shape[1]], [1, P]], channel_multiplier=-1).then_inc(s_done, 1)


def identity(nc, pool, s_done, s_step, ident, steps_before=2):
    nc.gpsimd.memset(ident, 0.0).then_inc(s_step, 1)
    pool.wait_ge(s_step, steps_before + 1)
    nc.gpsimd.affine_select(out=ident, in_=ident, compare_op=ALU.not_equal, fill=1.0, base=0, pattern=[[-1, P]],
                            channel_multiplier=1).then_inc(s_done, 1)


def ssd_chunks(nc, A, xbc, z, scr):
    S = xbc.shape[2]
    NC, H, G, W = S // P, SSD_HEADS, SSD_GROUPS, 1024
    HG, HD, XT = H // G, W // H, W // P
    GW = W // G
    with ExitStack() as ctx:
        c = Core(nc, ctx)
        upper, neg, ident, ones = c.sb("sd_upper", [P, P]), c.sb("sd_neg", [P, 4, P]), c.sb("sd_ident", [P, P]), c.sb("sd_ones", [P, P])
        after = c.sb("sd_after", [P, P])
        d_row, norm, eps = c.sb("sd_d", [P, H]), c.sb("sd_norm", [P, XT]), c.sb("sd_eps", [P, 1])
        e3s = c.sb("sd_e3", [P, 2, 3, H])
        nacs2 = c.sb("sd_neg_c", [P, 2, H])
        x_r, xdt, xdec, xd = (c.sb(f"sd_{n}", [P, W]) for n in ("x", "xdt", "xdec", "xd"))
        b_r = c.sb("sd_b", [P, G, P])
        lt = c.sb("sd_l", [P, H, P])
        mt = lt
        state = c.sb("sd_state", [P, W])
        y, sq = c.sb("sd_y", [P, W]), c.sb("sd_sq", [P, W])
        ssq, std, rstd = c.sb("sd_ssq", [P, G]), c.sb("sd_std", [P, G]), c.sb("sd_rstd", [P, G])
        yt = c.sb("sd_yt", [P, XT, P])
        psA = c.ps("sd_psA", [P, 2, 512])
        psB = c.ps("sd_psB", [P, 2, 512])
        psC = c.ps("sd_psC", [P, 2, 512])
        psD = c.ps("sd_psD", [P, 512])
        psE = c.ps("sd_psE", [P, 512])
        cbt = psD[:, 0:G * P].rearrange("p (g n) -> p g n", g=G)
        sums = psD[:, G * P:G * P + 3 * H].rearrange("p (n h) -> p n h", n=3)
        (s_in, s_c0, s_c1, s_c2) = (c.sem(f"sd_{n}") for n in ("loaded", "const_steps", "consts", "ones_ready"))
        (p_sums, p_A, p_turn, p_in, p_inter, p_state) = (
            c.sem(f"sd_pe_{n}") for n in ("sums", "psA_written", "turned_b", "intra", "inter", "state"))
        (a_e, a_x, a_A, a_sq, a_std) = (c.sem(f"sd_act_{n}") for n in ("exps", "b", "psA_read", "squares", "std"))
        (d_xdt, d_m, d_y1, d_y, d_st1, d_st, d_ch, d_rs, d_n, d_yt) = (
            c.sem(f"sd_dve_{n}") for n in ("xdt", "m", "y1", "y", "state1", "state", "chain", "rstd", "normed", "yt"))
        T2 = 2 * scr.T
        zero, s_zero, s_zst = c.sb("sd_zero", [P, W]), c.sem("sd_zeroed"), c.sem("sd_zeros_stored")
        (g_x, s_st) = (c.sem("sd_pool_x"), c.sem("sd_stored"))
        block = ctx.enter_context(nc.Block())
        heads = lambda ap: ap.rearrange("p (h d) -> p h d", d=HD)
        per_head = lambda ap: ap.unsqueeze(2).to_broadcast([P, H, HD])

        @block.sync
        def _(sp):
            sp.dma_start(d_row[:], A.ssd_d_2[0].rearrange("(a n) -> a n", a=1).broadcast_to([P, H])).then_inc(s_in, 16)
            with nc.allow_non_contiguous_dma(reason="gain column layout"):
                sp.dma_start(norm[:], A.ssd_norm_w_2[0].rearrange("(k p) -> p k", p=P)).then_inc(s_in, 16)
            for k in range(NC):
                sp.wait_ge(d_yt, 2 * k + 2)
                sp.dma_start(scr.y_ssd[:, :, k * P:(k + 1) * P].rearrange("f p s -> p f s"), yt[:]).then_inc(s_st, 16)
            sp.wait_ge(s_st, 16 * NC)

        @block.gpsimd
        def _(pool):
            triangle(nc, pool, s_c1, s_c0, upper[:], neg[:])
            identity(nc, pool, s_c1, s_c0, ident[:])
            nc.gpsimd.memset(ones[:], 1.0).then_inc(s_c1, 1)
            nc.gpsimd.memset(eps[:], EPS).then_inc(s_c1, 1)
            nc.gpsimd.memset(after[:], 1.0).then_inc(s_c2, 1)
            pool.wait_ge(s_c2, 1)
            nc.gpsimd.affine_select(out=after[:], in_=after[:], compare_op=ALU.is_gt, fill=0.0, base=0, pattern=[[-1, P]],
                                    channel_multiplier=1).then_inc(s_c1, 1)
            nc.gpsimd.memset(zero[:], 0.0).then_inc(s_zero, 1)
            pool.wait_ge(s_zero, 1)
            for x in range(scr.NX):
                row = (scr.NT - T2 + x) * P
                pool.dma_start(scr.ys[row:row + P, :], zero[:]).then_inc(s_zst, 16)
            pool.wait_ge(s_in, 32)
            for k in range(NC):
                pool.wait_ge(a_A, 6 * k + 2)
                if k:
                    pool.wait_ge(d_y, k)
                nc.gpsimd.tensor_tensor(heads(xd[:]), heads(x_r[:]), per_head(d_row[:]), ALU.mult).then_inc(g_x, 1)
            pool.wait_ge(s_zst, 16 * scr.NX)

        NF = 6

        def use(k, j):
            return j if k == 0 else 8 * k - 2 + j

        def result_use(k, j):
            return 8 * k + (12 if k + 1 < NC else 6) + j
        readers = {}
        for k in range(NC):
            for j in range(NF):
                readers[use(k, j)] = (a_A, NF * k + j + 1)
            for j in range(2):
                readers[result_use(k, j)] = (d_yt, 2 * k + j + 1)
        quarter = lambda j: psA[:, j % 2].rearrange("p (h n) -> p h n", n=P)

        @block.scalar
        def _(act):
            def front(k):
                act.wait_ge(p_sums, k + 1)
                if k > 1:
                    act.wait_ge(d_st1, k - 1)
                    act.wait_ge(d_y1, k - 1)
                if k:
                    act.wait_ge(d_xdt, k)
                    act.wait_ge(g_x, k)
                nc.scalar.activation(e3s[:, k % 2], sums, ACT.Exp)
                nc.scalar.activation(nacs2[:, k % 2], sums[:, 0], ACT.Copy, scale=-1.0).then_inc(a_e, 1)
                for j in range(2):
                    act.wait_ge(p_A, use(k, j) + 1)
                    nc.scalar.activation(x_r[:, j * 512:(j + 1) * 512], psA[:, j], ACT.Copy).then_inc(a_A, 1)
                act.wait_ge(p_turn, k + 1)
                if k:
                    act.wait_ge(p_state, k)
                nc.scalar.activation(b_r[:].rearrange("p g n -> p (g n)"), psE[:, 0:G * P], ACT.Copy).then_inc(a_x, 1)

            def decay(k):
                act.wait_ge(a_e, k + 1)
                if k:
                    act.wait_ge(p_in, k)
                for j in range(4):
                    act.wait_ge(p_A, use(k, 2 + j) + 1)
                    for h in range(4):
                        hh = 4 * j + h
                        last = nc.scalar.activation(lt[:, hh], quarter(j)[:, h], ACT.Exp, bias=nacs2[:, k % 2, hh:hh + 1])
                    last.then_inc(a_A, 1)

            act.wait_ge(s_c1, 6)
            front(0)
            decay(0)
            for k in range(NC):
                if k + 1 < NC:
                    front(k + 1)
                act.wait_ge(d_y, k + 1)
                for g in range(G):
                    cut = slice(g * GW, (g + 1) * GW)
                    nc.scalar.activation(sq[:, cut], y[:, cut], ACT.Square, accum_out=ssq[:, g:g + 1]).then_inc(a_sq, 1)
                act.wait_ge(a_sq, G * (k + 1))
                if k:
                    act.wait_ge(d_rs, k)
                nc.scalar.activation(std[:], ssq[:], ACT.Sqrt, scale=1.0 / GW, bias=eps[:]).then_inc(a_std, 1)
                if k + 1 < NC:
                    decay(k + 1)

        @block.vector
        def _(dve):
            v, ch = nc.vector, Chain(dve, d_ch)

            def inputs(k):
                dve.wait_ge(a_A, NF * k + 2)
                if k:
                    dve.wait_ge(p_in, k)
                    dve.wait_ge(p_state, k)
                ch.link(v.tensor_tensor(heads(xdt[:]), heads(x_r[:]), per_head(scr.dt[:, k]), ALU.mult))
                dve.wait_ge(a_e, k + 1)
                v.tensor_tensor(heads(xdec[:]), heads(xdt[:]), per_head(e3s[:, k % 2, 1]), ALU.mult).then_inc(d_xdt, 1)

            def matrices(k):
                for g in range(G):
                    dve.wait_ge(a_A, NF * k + 4 + 2 * g)
                    m = mt[:, g * HG:(g + 1) * HG]
                    v.tensor_tensor(m, m, cbt[:, g].unsqueeze(1).to_broadcast([P, HG, P]), ALU.mult).then_inc(d_m, 1)

            dve.wait_ge(s_in, 32)
            dve.wait_ge(s_c1, 6)
            inputs(0)
            matrices(0)
            both = lambda ps: ps[:].rearrange("p a (h d) -> p (a h) d", d=HD)
            for k in range(NC):
                if k:
                    dve.wait_ge(p_inter, k + 1)
                    dve.wait_ge(p_A, result_use(k - 1, 1) + 1)
                    v.tensor_tensor(heads(y[:]), both(psC), per_head(e3s[:, k % 2, 0]), ALU.mult).then_inc(d_y1, 1)
                    dve.wait_ge(d_y1, k + 1)
                    dve.wait_ge(p_in, k + 1)
                    ch.link(v.tensor_tensor(heads(y[:]), heads(y[:]), both(psB), ALU.add))
                else:
                    dve.wait_ge(p_in, 1)
                    v.tensor_copy(heads(y[:]), both(psB)).then_inc(d_y1, 1)
                    dve.wait_ge(d_y1, 1)
                dve.wait_ge(g_x, k + 1)
                ch.link(v.tensor_tensor(y[:], y[:], xd[:], ALU.add))
                v.tensor_tensor(y[:], y[:], z[:, k], ALU.mult).then_inc(d_y, 1)
                if k:
                    v.tensor_tensor(heads(state[:]), heads(state[:]), per_head(e3s[:, k % 2, 2]), ALU.mult).then_inc(d_st1, 1)
                    dve.wait_ge(d_st1, k + 1)
                    dve.wait_ge(p_state, k + 1)
                    v.tensor_tensor(state[:], state[:], psC[:].rearrange("p a n -> p (a n)"), ALU.add).then_inc(d_st, 1)
                else:
                    dve.wait_ge(p_state, 1)
                    v.tensor_copy(state[:], psC[:].rearrange("p a n -> p (a n)")).then_inc(d_st, 1)
                    dve.sem_inc(d_st1, 1)
                if k + 1 < NC:
                    inputs(k + 1)
                dve.wait_ge(a_std, k + 1)
                v.reciprocal(rstd[:], std[:]).then_inc(d_rs, 1)
                dve.wait_ge(d_rs, k + 1)
                for g in range(G):
                    cut = slice(g * GW, (g + 1) * GW)
                    v.tensor_scalar(y[:, cut], y[:, cut], rstd[:, g:g + 1], None, ALU.mult).then_inc(d_n, 1)
                if k + 1 < NC:
                    matrices(k + 1)
                if k:
                    dve.wait_ge(s_st, 16 * k)
                for j in range(2):
                    dve.wait_ge(p_A, result_use(k, j) + 1)
                    v.tensor_tensor(yt[:, 4 * j:4 * j + 4], quarter(j), norm[:, 4 * j:4 * j + 4].unsqueeze(2).to_broadcast([P, 4, P]),
                                    ALU.mult).then_inc(d_yt, 1)

        @block.tensor
        def _(pe):
            def take(n):
                if n >= 2:
                    pe.wait_ge(*readers[n - 2])

            def front(k):
                tok = slice(k * P, (k + 1) * P)
                adt = scr.adt[:, k]
                if k:
                    pe.wait_ge(d_m, G * k)
                    pe.wait_ge(a_e, k)
                for n, m in enumerate((upper, after, ones)):
                    nc.tensor.matmul(sums[:, n], m[:], adt, start=True, stop=True)
                for g in range(G):
                    last = nc.tensor.matmul(cbt[:, g], xbc[:, XT + g, tok], xbc[:, XT + G + g, tok], start=True, stop=True)
                last.then_inc(p_sums, 1)
                for j in range(2):
                    take(use(k, j))
                    for t in range(4):
                        last = nc.tensor.transpose(quarter(j)[:, t], xbc[:, 4 * j + t, tok], ident[:])
                    last.then_inc(p_A, 1)
                wait(pe, a_x, k)
                for g in range(G):
                    last = nc.tensor.transpose(psE[:, g * P:(g + 1) * P], xbc[:, XT + g, tok], ident[:])
                last.then_inc(p_turn, 1)
                for j in range(4):
                    take(use(k, 2 + j))
                    for h in range(4):
                        hh = 4 * j + h
                        nc.tensor.matmul(quarter(j)[:, h], adt[:, hh:hh + 1].to_broadcast([P, P]), upper[:], start=(h == 0),
                                         stop=False, skip_group_check=True)
                    nc.tensor.matmul(psA[:, j % 2], ident[:], neg[:].rearrange("p h n -> p (h n)"), start=False, stop=True,
                                     skip_group_check=True).then_inc(p_A, 1)

            def result(k):
                pe.wait_ge(d_n, G * (k + 1))
                for j in range(2):
                    take(result_use(k, j))
                    for t in range(4):
                        last = nc.tensor.transpose(quarter(j)[:, t], y[:, (4 * j + t) * P:(4 * j + t + 1) * P], ident[:])
                    last.then_inc(p_A, 1)

            pe.wait_ge(s_c1, 6)
            front(0)
            for k in range(NC):
                tok = slice(k * P, (k + 1) * P)
                if k:
                    pe.wait_ge(d_st, k)
                    for g in range(G):
                        last = nc.tensor.matmul(psC[:, g], xbc[:, XT + G + g, tok], state[:, g * GW:(g + 1) * GW], start=True, stop=True)
                    last.then_inc(p_inter, 1)
                    pe.wait_ge(d_y, k)
                else:
                    pe.sem_inc(p_inter, 1)
                pe.wait_ge(d_xdt, k + 1)
                for h in range(H):
                    if h % HG == 0:
                        pe.wait_ge(d_m, G * k + h // HG + 1)
                    last = nc.tensor.matmul(psB[:, h // HG, (h % HG) * HD:(h % HG + 1) * HD], mt[:, h], xdt[:, h * HD:(h + 1) * HD],
                                            start=True, stop=True)
                last.then_inc(p_in, 1)
                pe.wait_ge(d_y1, k + 1) if k else None
                pe.wait_ge(a_x, k + 1)
                for g in range(G):
                    last = nc.tensor.matmul(psC[:, g], b_r[:, g], xdec[:, g * GW:(g + 1) * GW], start=True, stop=True)
                last.then_inc(p_state, 1)
                if k + 1 < NC:
                    front(k + 1)
                result(k)


def mlstm_chunks(nc, A, qk, v1, scr, hl):
    S = qk.shape[2]
    NC, H, D = S // P, ML_HEADS, P
    SCALE = float(D) ** -0.5
    QH = 4
    NG = H // QH
    with ExitStack() as ctx:
        c = Core(nc, ctx)
        upper, neg, ident = c.sb("ml_upper", [P, P]), c.sb("ml_neg", [P, QH, P]), c.sb("ml_ident", [P, P])
        last_row = c.sb("ml_last_row", [P, P])
        ones, eps = c.sb("ml_ones", [P, 2]), c.sb("ml_eps", [P, 1])
        nsel = c.sb("ml_neg_select", [H, H])
        w = c.sb("ml_w", [P, 2, QH, P])
        kw = c.sb("ml_kw", [P, 2, QH, P])
        state = c.sb("ml_state", [P, H, D])
        nvec = c.sb("ml_n", [P, H])
        carry = c.sb("ml_carry", [P, NC, H])
        h_r = c.sb("ml_h", [P, 2, H, D])
        sq = c.sb("ml_sq", [P, H, D])
        sm = c.sb("ml_small", [P, 8, H])
        DEN, INV, SUM, SQ, STD, RSTD, SHIFT, MEAN = range(8)
        gate = c.sb("ml_o", [P, 2, H, P])
        yt = c.sb("ml_yt", [P, 2, QH, P])
        ps_s, ps_w, ps_k, ps_n, ps_i, ps_c, ps_t, ps_v = (c.ps(f"ml_ps_{n}", [P, 512]) for n in "swknictv")
        den_i, den_x, n_up = (ps_v[:, n * H:(n + 1) * H] for n in range(3))
        all_carries = ps_v[:, 0:NC * H].rearrange("p (k h) -> p k h", h=H)
        (s_c0, s_c1, s_c2, s_o0, s_o1) = (c.sem(f"ml_{n}") for n in ("const_steps", "consts", "more_steps", "o_loaded0", "o_loaded1"))
        s_o = (s_o0, s_o1)
        (p_s, p_w, p_k, p_n, p_c, p_den, p_nup, p_cs, p_t) = (
            c.sem(f"ml_pe_{n}") for n in ("scores", "rows", "turned_k", "num", "state", "den", "n", "carry", "turned"))
        (a_w, a_scaled, a_sq, a_std, a_hn, a_h) = (c.sem(f"ml_act_{n}") for n in (
            "w", "scaled", "square", "std", "normed", "high"))
        (d_p, d_kw, d_i, d_num, d_ch, d_cs, d_st, d_n, d_inv, d_mean, d_rs, d_y, d_l) = (
            c.sem(f"ml_dve_{n}") for n in ("p", "kw", "inter", "num", "chain", "carry", "state", "n", "inverse", "mean",
                                           "rstd", "y", "low"))
        g_st = c.sem("ml_pool_state")
        block = ctx.enter_context(nc.Block())
        grp = lambda ps: ps[:].rearrange("p (h n) -> p h n", n=P)
        per_head = lambda ap, n=QH: ap.unsqueeze(2).to_broadcast([P, n, P])
        col = lambda k, n: scr.cols[:, k, n]

        @block.sync
        def _(sp):
            for k in range(NC):
                if k >= 2:
                    sp.wait_ge(d_y, NG * (k - 1))
                sp.dma_start(gate[:, k % 2], scr.o[:, :, k * P:(k + 1) * P].rearrange("f p s -> p f s")).then_inc(s_o[k % 2], 16)

        @block.gpsimd
        def _(pool):
            triangle(nc, pool, s_c1, s_c0, upper[:], neg[:])
            identity(nc, pool, s_c1, s_c0, ident[:])
            nc.gpsimd.memset(ones[:], 1.0).then_inc(s_c1, 1)
            nc.gpsimd.memset(eps[:], EPS).then_inc(s_c1, 1)
            nc.gpsimd.memset(last_row[:], 1.0).then_inc(s_c2, 1)
            nc.gpsimd.memset(nsel[:], 0.0).then_inc(s_c2, 1)
            pool.wait_ge(s_c2, 2)
            nc.gpsimd.affine_select(out=last_row[:], in_=last_row[:], compare_op=ALU.is_equal, fill=0.0, base=-(P - 1),
                                    pattern=[[0, P]], channel_multiplier=1).then_inc(s_c1, 1)
            nc.gpsimd.affine_select(out=nsel[:], in_=nsel[:], compare_op=ALU.not_equal, fill=-1.0, base=0,
                                    pattern=[[-1, H]], channel_multiplier=1).then_inc(s_c1, 1)
            pool.wait_ge(d_cs, 1)
            for k in range(1, NC):
                for g in range(NG):
                    pool.wait_ge(p_n, NG * k + g + 1)
                    pool.wait_ge(d_st, NG * (k - 1) + g + 1)
                    st = state[:, g * QH:(g + 1) * QH]
                    nc.gpsimd.tensor_tensor(st, st, per_head(carry[:, k, g * QH:(g + 1) * QH]), ALU.mult).then_inc(g_st, 1)

        @block.scalar
        def _(act):
            def weights(k, g):
                act.wait_ge(p_w, NG * k + g + 1)
                wait(act, p_den, k)
                for h in range(QH):
                    last = nc.scalar.activation(w[:, g, h], grp(ps_w)[:, h], ACT.Exp, bias=col(k, 0)[:, g * QH + h:g * QH + h + 1])
                last.then_inc(a_w, 1)

            def high(k):
                for g in range(NG):
                    act.wait_ge(d_y, NG * k + g + 1)
                    nc.scalar.activation(hl[:, 0, g * QH:(g + 1) * QH, k * P:(k + 1) * P], yt[:, g], ACT.Copy).then_inc(a_h, 1)

            act.wait_ge(s_c1, 7)
            weights(0, 0)
            weights(0, 1)
            for k in range(NC):
                one = lambda row, h: sm[:, row, h:h + 1]
                h_k = h_r[:, k % 2]
                if k:
                    high(k - 1)
                act.wait_ge(d_inv, k + 1)
                act.wait_ge(d_num, NG * (k + 1))
                for h in range(H):
                    last = nc.scalar.activation(h_k[:, h], h_k[:, h], ACT.Copy, scale=one(INV, h), accum_out=one(SUM, h))
                last.then_inc(a_scaled, 1)
                if k + 1 < NC:
                    weights(k + 1, 0)
                act.wait_ge(d_mean, k + 1)
                act.wait_ge(a_scaled, k + 1)
                for h in range(H):
                    last = nc.scalar.activation(sq[:, h], h_k[:, h], ACT.Square, bias=one(MEAN, h), accum_out=one(SQ, h))
                last.then_inc(a_sq, 1)
                act.wait_ge(a_sq, k + 1)
                nc.scalar.activation(sm[:, STD], sm[:, SQ], ACT.Sqrt, scale=1.0 / D, bias=eps[:]).then_inc(a_std, 1)
                if k + 1 < NC:
                    weights(k + 1, 1)
                act.wait_ge(d_rs, k + 1)
                for h in range(H):
                    last = nc.scalar.activation(h_k[:, h], h_k[:, h], ACT.Identity, scale=one(RSTD, h), bias=one(SHIFT, h))
                last.then_inc(a_hn, 1)
            high(NC - 1)

        @block.vector
        def _(dve):
            v, ch = nc.vector, Chain(dve, d_ch)
            dve.wait_ge(s_c1, 7)
            dve.wait_ge(p_cs, 1)
            v.tensor_copy(carry[:], all_carries).then_inc(d_cs, 1)

            def operands(k, g):
                n, hs = NG * k + g, slice(g * QH, (g + 1) * QH)
                dve.wait_ge(a_w, n + 1)
                dve.wait_ge(p_s, n + 1)
                v.scalar_tensor_tensor(w[:, g], grp(ps_s), SCALE, w[:, g], ALU.mult, ALU.mult).then_inc(d_p, 1)
                dve.wait_ge(p_k, n + 1)
                wait(dve, p_nup, k)
                v.scalar_tensor_tensor(kw[:, g], grp(ps_k), SCALE, per_head(col(k, 3)[:, hs]), ALU.mult, ALU.mult).then_inc(d_kw, 1)

            def numerator(k, g):
                n, hs = NG * k + g, slice(g * QH, (g + 1) * QH)
                h_k = h_r[:, k % 2, hs]
                dve.wait_ge(p_n, n + 1)
                if k:
                    v.tensor_tensor(h_k, grp(ps_i), per_head(col(k, 1)[:, hs]), ALU.mult).then_inc(d_i, 1)
                    dve.wait_ge(d_i, n + 1)
                    v.tensor_tensor(h_k, h_k, grp(ps_n), ALU.add).then_inc(d_num, 1)
                    dve.wait_ge(g_st, NG * (k - 1) + g + 1)
                    dve.wait_ge(p_c, n + 1)
                    v.tensor_tensor(state[:, hs], state[:, hs], grp(ps_c), ALU.add).then_inc(d_st, 1)
                else:
                    dve.sem_inc(d_i, 1)
                    v.tensor_copy(h_k, grp(ps_n)).then_inc(d_num, 1)
                    dve.wait_ge(p_c, n + 1)
                    v.tensor_copy(state[:, hs], grp(ps_c)).then_inc(d_st, 1)

            def gated(k, g):
                n, hs = NG * k + g, slice(g * QH, (g + 1) * QH)
                dve.wait_ge(s_o[k % 2], 16 * (k // 2 + 1))
                dve.wait_ge(p_t, n + 1)
                if k:
                    dve.wait_ge(a_h, n - 1)
                    dve.wait_ge(d_l, n - 1)
                v.tensor_tensor(yt[:, g], grp(ps_t), gate[:, k % 2, hs], ALU.mult).then_inc(d_y, 1)

            def low(k):
                for g in range(NG):
                    hs = slice(g * QH, (g + 1) * QH)
                    dve.wait_ge(a_h, NG * k + g + 1)
                    v.tensor_tensor(hl[:, 1, hs, k * P:(k + 1) * P], yt[:, g], f32(hl[:, 0, hs, k * P:(k + 1) * P]),
                                    ALU.subtract).then_inc(d_l, 1)

            def denominator(k):
                dve.wait_ge(p_nup, k + 1)
                if k:
                    ch.link(v.tensor_tensor(sm[:, DEN], col(k, 1), den_x, ALU.mult))
                    ch.link(v.tensor_tensor(sm[:, DEN], sm[:, DEN], den_i, ALU.add))
                    ch.link(v.tensor_tensor(nvec[:], nvec[:], carry[:, k], ALU.mult))
                    v.tensor_tensor(nvec[:], nvec[:], n_up, ALU.add).then_inc(d_n, 1)
                else:
                    ch.link(v.tensor_copy(sm[:, DEN], den_i))
                    v.tensor_copy(nvec[:], n_up).then_inc(d_n, 1)
                ch.link(v.scalar_tensor_tensor(sm[:, INV], sm[:, DEN], -1.0, sm[:, DEN], ALU.mult, ALU.max))
                ch.link(v.tensor_tensor(sm[:, INV], sm[:, INV], col(k, 2), ALU.max))
                v.reciprocal(sm[:, INV], sm[:, INV]).then_inc(d_inv, 1)

            operands(0, 0)
            operands(0, 1)
            for k in range(NC):
                for g in range(NG):
                    numerator(k, g)
                if k:
                    gated(k - 1, 0)
                    gated(k - 1, 1)
                denominator(k)
                if k:
                    low(k - 1)
                if k + 1 < NC:
                    operands(k + 1, 0)
                dve.wait_ge(a_scaled, k + 1)
                v.tensor_scalar(sm[:, MEAN], sm[:, SUM], -1.0 / D, None, ALU.mult).then_inc(d_mean, 1)
                if k + 1 < NC:
                    operands(k + 1, 1)
                dve.wait_ge(a_std, k + 1)
                dve.wait_ge(d_mean, k + 1)
                ch.link(v.reciprocal(sm[:, RSTD], sm[:, STD]))
                v.tensor_tensor(sm[:, SHIFT], sm[:, MEAN], sm[:, RSTD], ALU.mult).then_inc(d_rs, 1)
            gated(NC - 1, 0)
            gated(NC - 1, 1)
            low(NC - 1)

        @block.tensor
        def _(pe):
            q = lambda h, k: qk[:, h, k * P:(k + 1) * P]
            kk = lambda h, k: qk[:, H + h, k * P:(k + 1) * P]
            mm = nc.tensor.matmul

            def front(k, g):
                n = NG * k + g
                wait(pe, d_p, n)
                for h in range(QH):
                    last = mm(grp(ps_s)[:, h], kk(g * QH + h, k), q(g * QH + h, k), start=True, stop=True)
                last.then_inc(p_s, 1)
                wait(pe, a_w, n)
                for h in range(QH):
                    mm(grp(ps_w)[:, h], nsel[:, g * QH + h:g * QH + h + 1].to_broadcast([H, P]), scr.g[:, k * P:(k + 1) * P], start=(h == 0),
                       stop=False, skip_group_check=True)
                last = mm(ps_w[:], ident[:], neg[:].rearrange("p h n -> p (h n)"), start=False, stop=True,
                          skip_group_check=True)
                last.then_inc(p_w, 1)
                wait(pe, d_kw, n)
                for h in range(QH):
                    last = nc.tensor.transpose(grp(ps_k)[:, h], kk(g * QH + h, k), ident[:])
                last.then_inc(p_k, 1)

            def products(k, g):
                n = NG * k + g
                pe.wait_ge(d_p, n + 1)
                wait(pe, d_num, n)
                for h in range(QH):
                    last = mm(grp(ps_n)[:, h], w[:, g, h], v1[:, k, g * QH + h], start=True, stop=True)
                if k:
                    pe.wait_ge(d_st, n - NG + 1)
                    wait(pe, d_i, n)
                    for h in range(QH):
                        last = mm(grp(ps_i)[:, h], q(g * QH + h, k), state[:, g * QH + h], start=True, stop=True)
                last.then_inc(p_n, 1)
                pe.wait_ge(d_kw, n + 1)
                wait(pe, d_st, n)
                for h in range(QH):
                    last = mm(grp(ps_c)[:, h], kw[:, g, h], v1[:, k, g * QH + h], start=True, stop=True)
                last.then_inc(p_c, 1)

            def turn(k, g):
                n = NG * k + g
                pe.wait_ge(a_hn, k + 1)
                wait(pe, d_y, n)
                for h in range(QH):
                    last = nc.tensor.transpose(grp(ps_t)[:, h], h_r[:, k % 2, g * QH + h], ident[:])
                last.then_inc(p_t, 1)

            pe.wait_ge(s_c1, 7)
            mm(all_carries, last_row[:], scr.cols[:, :, 1], start=True, stop=True).then_inc(p_cs, 1)
            front(0, 0)
            front(0, 1)
            for k in range(NC):
                for g in range(NG):
                    products(k, g)
                if k:
                    turn(k - 1, 0)
                pe.wait_ge(d_cs, 1)
                wait(pe, d_n, k)
                wait(pe, d_inv, k)
                for h in range(H):
                    last = mm(den_i[:, h:h + 1], w[:, h // QH, h % QH], ones[:, 0:1], start=True, stop=True)
                    if k:
                        last = mm(den_x[:, h:h + 1], q(h, k), nvec[:, h:h + 1], start=True, stop=True)
                last.then_inc(p_den, 1)
                if k:
                    turn(k - 1, 1)
                for h in range(H):
                    last = mm(n_up[:, h:h + 1], kw[:, h // QH, h % QH], ones[:, 0:1], start=True, stop=True)
                last.then_inc(p_nup, 1)
                if k + 1 < NC:
                    front(k + 1, 0)
                    front(k + 1, 1)
            turn(NC - 1, 0)
            turn(NC - 1, 1)


def load_split(nc, tag, src, hl):
    KT = hl.shape[2]
    with ExitStack() as ctx:
        c = Core(nc, ctx)
        stage = c.sb(f"{tag}_stage", [P, 4, hl.shape[3]])
        s_in = c.sems(f"{tag}_loaded", 4)
        s_hi, s_lo = c.sem(f"{tag}_high"), c.sem(f"{tag}_low")
        block = ctx.enter_context(nc.Block())

        @block.sync
        def _(sp):
            for k in range(KT):
                wait(sp, s_lo, k - 3)
                sp.dma_start(stage[:, k % 4], src[k]).then_inc(s_in[k % 4], 16)

        @block.scalar
        def _(act):
            for k in range(KT):
                act.wait_ge(s_in[k % 4], 16 * (k // 4 + 1))
                nc.scalar.activation(hl[:, 0, k], stage[:, k % 4], ACT.Copy).then_inc(s_hi, 1)

        @block.vector
        def _(dve):
            for k in range(KT):
                dve.wait_ge(s_hi, k + 1)
                nc.vector.tensor_tensor(hl[:, 1, k], stage[:, k % 4], f32(hl[:, 0, k]), ALU.subtract).then_inc(s_lo, 1)


def second_mixers(nc, A, hl, scr):
    KT, S = hl.shape[2], hl.shape[3]
    D, T = KT * P, S // P
    w_in = A.w_in_2[0].rearrange("(k p) n -> p k n", p=P)
    cols = lambda a, n: w_in[:, :, a:a + n]
    tiles = lambda a, n: cols(a, n).rearrange("p k (f m) -> p k f m", m=P)
    Z, XBC, DT = 0, D, D + 1536
    QK = DT + SSD_HEADS
    V = QK + 2 * D
    O = V + D
    IF = O + D
    with ExitStack() as ctx:
        c = Core(nc, ctx)
        small = Names()
        scr.dt, scr.adt = c.sb("dt", [P, T, SSD_HEADS]), c.sb("adt", [P, T, SSD_HEADS])
        scr.cols, scr.g = c.sb("ml_cols", [P, T, 4, ML_HEADS]), c.sb("ml_g", [ML_HEADS, S])
        with nc.sbuf_tensor("silu_z", [P, T, D], F32) as z:
            with nc.sbuf_tensor("gates", [P, T, 32], F32) as gates:
                row_product(nc, "pz", hl, cols(Z, D), z, ACT.Silu,
                            (cols(DT, 32), gates, [(cols(DT, 16), 0, 16), (cols(IF, 16), 16, 16)]))
                gate_values(nc, A, gates, scr)
            with nc.sbuf_tensor("xbc", [P, 12, S], F32) as xbc:
                column_product(nc, "px", hl, tiles(XBC, 1536), 12, out=xbc, conv=(A.ssd_conv_w_2[0], A.ssd_conv_b_2[0]))
                ssd_chunks(nc, A, xbc, z, scr)
        with nc.sbuf_tensor("v_rows", [P, T, ML_HEADS, P], F32) as v1:
            row_product(nc, "pv", hl, cols(V, D), v1, ACT.Copy)
            column_product(nc, "po", hl, tiles(O, D), ML_HEADS, gain=A.ml_norm_w_2[0], store=scr.o)
            with nc.sbuf_tensor("qk", [P, 2 * ML_HEADS, S], F32) as qk:
                column_product(nc, "pq", hl, tiles(QK, 2 * D), 16, out=qk, conv=(A.ml_conv_w_2[0], A.ml_conv_b_2[0]))
                mlstm_chunks(nc, A, qk, v1, scr, hl)


def route(nc, A, hl, scr):
    T, KT = scr.T, hl.shape[2]
    NE, NGR = A.router_e_w_2.shape[2], A.router_g_w_2.shape[2]
    EG, NL = NE // NGR, NE + NGR
    NT, NX = scr.NT, scr.NX
    MOST = T - 1
    with ExitStack() as ctx:
        c = Core(nc, ctx)
        wst = c.sb("rt_w", [P, KT, NL])
        w_hl = c.sb("rt_w_hl", [P, 2, KT, NL], F32R)
        bias = c.sb("rt_bias", [P, NL])
        before, ones = c.sb("rt_before", [P, P]), c.sb("rt_ones", [P, P])
        io_i = c.sb("rt_iota_i", [P, NE + NX + 1], I32)
        io = c.sb("rt_iota", [P, NE])
        iom = c.sb("rt_iota_m", [P, NE])
        jj = c.sb("rt_jj", [P, NX + 1])
        tok_id = c.sb("rt_token", [P, T], I32)
        zero = c.sb("rt_zero", [P, NT], I32)
        gl, ge, gh, gpen, cand4 = (c.sb(f"rt_g{n}", [P, T, NGR]) for n in range(5))
        el, el2, cand, oh1, oh2, o = (c.sb(f"rt_e{n}", [P, T, NE]) for n in range(6))
        jr, q, tl, pa, pb, tmp = (c.sb(f"rt_p{n}", [P, T, NE]) for n in range(6))
        oc = c.sb("rt_oc", [P, T + 1, NE])
        s8 = c.sb("rt_s8", [P, 10, T])
        n_e, nx, xb, xe, dd, one32 = (c.sb(f"rt_n{n}", [P, NE]) for n in range(6))
        ina, inb = c.sb("rt_ina", [P, NX + 1, NE]), c.sb("rt_inb", [P, NX + 1, NE])
        more = c.sb("rt_more", [P, NX + 1])
        sel = c.sb("rt_sel", [P, 4, T])
        place = c.sb("rt_place", [P, 2, T], U32)
        l_rows, ident = c.sb("rt_l_rows", [NL, T * P]), c.sb("rt_ident", [P, P])
        s_id, s_id0, s_mr, s_lr = c.sem("rt_ident_ready"), c.sem("rt_ident_steps"), c.sem("rt_logit_rows"), c.sem("rt_rows_copied")
        ps_l, ps_lr = c.ps("rt_ps_l", [P, T, NL]), c.ps("rt_ps_l_rows", [NL, 2, T * P // 2])
        ps_r = c.ps("rt_ps_r", [P, T, NE])
        ps_n = c.ps("rt_ps_n", [P, NE])
        s_w, s_hi, s_lo, s_mm, s_b = c.sem("rt_w_loaded"), c.sem("rt_w_high"), c.sem("rt_w_low"), c.sem("rt_logits"), c.sem("rt_bias_loaded")
        s_c, s_c0 = c.sem("rt_consts"), c.sem("rt_const_steps")
        s_ch, s_e, s_o, s_rank, s_pos = c.sem("rt_chain"), c.sem("rt_exp"), c.sem("rt_counts_ready"), c.sem("rt_ranked"), c.sem("rt_places")
        s_e2 = c.sem("rt_exp_done")
        s_z, s_sc = c.sem("rt_list_zeroed"), c.sem("rt_list_written")
        block = ctx.enter_context(nc.Block())

        @block.sync
        def _(sp):
            with nc.allow_non_contiguous_dma(reason="few router columns"):
                sp.dma_start(wst[:, :, 0:NGR], A.router_g_w_2[0].rearrange("(k p) n -> p k n", p=P)).then_inc(s_w, 16)
                sp.dma_start(wst[:, :, NGR:], A.router_e_w_2[0].rearrange("(k p) n -> p k n", p=P)).then_inc(s_w, 16)
            sp.dma_start(bias[:, 0:NGR], A.router_g_b_2.broadcast_to([P, NGR])).then_inc(s_b, 16)
            sp.dma_start(bias[:, NGR:], A.router_e_b_2.broadcast_to([P, NE])).then_inc(s_b, 16)

        @block.gpsimd
        def _(pool):
            identity(nc, pool, s_id, s_id0, ident[:], 0)
            nc.gpsimd.memset(before[:], 1.0).then_inc(s_c0, 1)
            nc.gpsimd.memset(ones[:], 1.0).then_inc(s_c, 1)
            nc.gpsimd.memset(zero[:], 0).then_inc(s_c0, 1)
            nc.gpsimd.iota(io_i[:, 0:NE], pattern=[[1, NE]], base=0, channel_multiplier=0).then_inc(s_c, 1)
            nc.gpsimd.iota(io_i[:, NE:], pattern=[[1, NX + 1]], base=0, channel_multiplier=0).then_inc(s_c, 1)
            nc.gpsimd.iota(tok_id[:], pattern=[[P, T]], base=0, channel_multiplier=1).then_inc(s_c, 1)
            pool.wait_ge(s_c0, 2)
            nc.gpsimd.affine_select(out=before[:], in_=before[:], compare_op=ALU.is_gt, fill=0.0, base=0, pattern=[[1, P]],
                                    channel_multiplier=-1).then_inc(s_c, 1)
            pool.dma_start(scr.list.rearrange("(p t) a -> p (t a)", t=NT), zero[:]).then_inc(s_z, 16)
            pool.wait_ge(s_z, 16)
            pool.wait_ge(s_pos, 1)
            pool.wait_ge(s_c, 5)
            for n in range(2 * T):
                pool.indirect_dma_start(out=scr.list, out_offset=bass.IndirectOffsetOnAxis(ap=place[:, n // T, n % T:n % T + 1], axis=0),
                                        in_=tok_id[:, n % T:n % T + 1], in_offset=None).then_inc(s_sc, 16)
            pool.wait_ge(s_sc, 16 * 2 * T)

        @block.scalar
        def _(act):
            act.wait_ge(s_w, 32)
            nc.scalar.activation(w_hl[:, 0], wst[:], ACT.Copy).then_inc(s_hi, 1)
            act.wait_ge(s_e, 1)
            nc.scalar.activation(ge[:], ge[:], ACT.Exp).then_inc(s_e2, 1)
            act.wait_ge(s_e, 2)
            nc.scalar.activation(s8[:, 6], s8[:, 6], ACT.Exp).then_inc(s_e2, 1)

        @block.tensor
        def _(pe):
            pe.wait_ge(s_lo, 1)
            narrow_rows(nc, ps_lr, w_hl, hl).then_inc(s_mr, 1)
            pe.wait_ge(s_id, 1)
            pe.wait_ge(s_lr, 1)
            turn_rows(nc, ps_l, l_rows, ident).then_inc(s_mm, 1)
            pe.wait_ge(s_c, 5)
            pe.wait_ge(s_o, 1)
            nc.tensor.matmul(ps_r[:], before[:], o[:], start=True, stop=False)
            nc.tensor.matmul(ps_r[:], ones[:], oc[:, 0:T], start=False, stop=True)
            nc.tensor.matmul(ps_n[:], ones[:], oc[:, T], start=True, stop=True).then_inc(s_rank, 1)

        @block.vector
        def _(dve):
            v, ch = nc.vector, Chain(dve, s_ch)
            wide = lambda ap, n: ap.unsqueeze(2).to_broadcast([P, T, n])
            rows = lambda ap: ap.unsqueeze(1).to_broadcast([P, T, ap.shape[1]])

            def first_of(vals, top, n, scratch, idx, hot):
                ch.link(v.tensor_reduce(top, vals, AX, ALU.max))
                ch.link(v.tensor_tensor(scratch, vals, wide(top, n), ALU.is_equal))
                ch.link(v.scalar_tensor_tensor(scratch, scratch, -64.0, rows(io[:, 0:n]), ALU.mult, ALU.add))
                ch.link(v.tensor_reduce(idx, scratch, AX, ALU.min))
                ch.link(v.tensor_tensor(hot, rows(iom[:, 0:n]), wide(idx, n), ALU.is_equal))

            dve.wait_ge(s_hi, 1)
            v.tensor_tensor(w_hl[:, 1], wst[:], f32(w_hl[:, 0]), ALU.subtract).then_inc(s_lo, 1)
            dve.wait_ge(s_c, 5)
            ch.inc(v.tensor_copy(jj[:], io_i[:, NE:]))
            ch.link(v.tensor_copy(io[:], io_i[:, 0:NE]))
            ch.inc(v.tensor_scalar(iom[:], io[:], -64.0, None, ALU.add))
            ch.inc(v.memset(one32[:], 1.0))
            ch.inc(v.memset(nx[:], 0.0))
            ch.inc(v.memset(jr[:], 0.0))
            ch.inc(v.memset(oc[:, 0], 0.0))
            dve.wait_ge(s_mr, 1)
            v.tensor_copy(l_rows[:], ps_lr[:].rearrange("p h n -> p (h n)")).then_inc(s_lr, 1)
            dve.wait_ge(s_b, 32)
            dve.wait_ge(s_mm, 1)
            ch.inc(v.tensor_tensor(gl[:], ps_l[:, :, 0:NGR], rows(bias[:, 0:NGR]), ALU.add))
            ch.link(v.tensor_tensor(el[:], ps_l[:, :, NGR:], rows(bias[:, NGR:]), ALU.add))
            first_of(gl[:], s8[:, 0], NGR, cand4[:], s8[:, 1], gh[:])
            v.tensor_tensor(ge[:], gl[:], wide(s8[:, 0], NGR), ALU.subtract).then_inc(s_e, 1)
            per_group = lambda ap: ap.rearrange("p t g -> p (t g)").unsqueeze(2).to_broadcast([P, T * NGR, EG])
            groups = lambda ap: ap.rearrange("p t (g e) -> p (t g) e", e=EG)
            ch.inc(v.tensor_scalar(gpen[:], gh[:], -1.0, 1e30, ALU.add, ALU.mult))
            ch.link(v.tensor_tensor(groups(el[:]), groups(el[:]), per_group(gh[:]), ALU.mult))
            ch.link(v.tensor_tensor(groups(el[:]), groups(el[:]), per_group(gpen[:]), ALU.add))
            first_of(el[:], s8[:, 2], NE, cand[:], s8[:, 3], oh1[:])
            ch.link(v.scalar_tensor_tensor(el2[:], oh1[:], -2e30, el[:], ALU.mult, ALU.add))
            first_of(el2[:], s8[:, 4], NE, cand[:], s8[:, 5], oh2[:])
            v.tensor_tensor(s8[:, 6], s8[:, 4], s8[:, 2], ALU.subtract).then_inc(s_e, 1)
            ch.link(v.tensor_tensor(o[:], oh1[:], oh2[:], ALU.add))
            for t in range(T):
                ins = v.tensor_tensor(oc[:, t + 1], oc[:, t], o[:, t], ALU.add)
                if t + 1 < T:
                    ch.link(ins)
                else:
                    ins.then_inc(s_o, 1)
            dve.wait_ge(s_e2, 2)
            ch.link(v.tensor_reduce(s8[:, 7], ge[:], AX, ALU.add))
            ch.inc(v.reciprocal(s8[:, 7], s8[:, 7]))
            ch.link(v.tensor_scalar(s8[:, 8], s8[:, 6], 1.0, None, ALU.add))
            ch.link(v.reciprocal(s8[:, 8], s8[:, 8]))
            ch.link(v.tensor_tensor(scr.gate[:, 0], s8[:, 8], s8[:, 7], ALU.mult))
            ch.link(v.tensor_tensor(scr.gate[:, 1], scr.gate[:, 0], s8[:, 6], ALU.mult))
            dve.wait_ge(s_rank, 1)
            ch.link(v.tensor_copy(n_e[:], ps_n[:]))
            for m in range(1, MOST + 1):
                ch.link(v.scalar_tensor_tensor(nx[:], n_e[:], float(P * m), nx[:], ALU.is_gt, ALU.add))
            ch.link(v.tensor_tensor_scan(xe[:], one32[:], nx[:], 0.0, ALU.mult, ALU.add))
            ch.link(v.tensor_tensor(xb[:], xe[:], nx[:], ALU.subtract))
            ch.link(v.tensor_scalar(dd[:], xb[:], float(NE - 1), None, ALU.add))
            ch.link(v.tensor_tensor(dd[:], dd[:], io[:], ALU.subtract))
            ch.link(v.tensor_copy(q[:], ps_r[:]))
            for m in range(1, MOST + 1):
                ch.link(v.scalar_tensor_tensor(jr[:], q[:], float(P * m), jr[:], ALU.is_ge, ALU.add))
            ch.link(v.scalar_tensor_tensor(q[:], jr[:], -float(P), q[:], ALU.mult, ALU.add))
            ch.link(v.tensor_tensor(tmp[:], jr[:], rows(dd[:]), ALU.add))
            ch.link(v.scalar_tensor_tensor(tl[:], jr[:], 0.0, tmp[:], ALU.is_gt, ALU.mult))
            ch.link(v.tensor_tensor(tl[:], tl[:], rows(io[:]), ALU.add))
            ch.inc(v.scalar_tensor_tensor(pa[:], q[:], float(NT), tl[:], ALU.mult, ALU.add))
            ch.link(v.scalar_tensor_tensor(pb[:], tl[:], float(P), q[:], ALU.mult, ALU.add))
            for n, (hot, pos) in enumerate([(oh1, pa), (oh2, pa), (oh1, pb), (oh2, pb)]):
                ch.link(v.tensor_tensor(tmp[:], hot[:], pos[:], ALU.mult))
                ch.link(v.tensor_reduce(sel[:, n], tmp[:], AX, ALU.add))
            v.tensor_copy(place[:], sel[:, 0:2]).then_inc(s_pos, 1)
            ch.inc(v.tensor_copy(scr.row[:], sel[:, 2:4]))
            over = lambda ap: ap.unsqueeze(1).to_broadcast([P, NX + 1, NE])
            jw = jj[:].unsqueeze(2).to_broadcast([P, NX + 1, NE])
            ch.inc(v.tensor_tensor(ina[:], jw, over(xb[:]), ALU.is_ge))
            ch.link(v.tensor_tensor(inb[:], jw, over(xe[:]), ALU.is_lt))
            ch.link(v.tensor_tensor(ina[:], ina[:], inb[:], ALU.mult))
            ch.link(v.tensor_tensor(ina[:], ina[:], over(io[:]), ALU.mult))
            ch.link(v.tensor_reduce(more[:], ina[:], AX, ALU.add))
            ch.link(v.tensor_copy(more[:, NX:], xe[:, NE - 1:NE]))
            ch.link(v.tensor_copy(scr.more[:], more[:]))


def weight_unit(A, u, e):
    if u < 8:
        w = (A.exp_w_gate_2 if u < 4 else A.exp_w_up_2)[0].rearrange("e (k p) n -> e p k n", p=P)
        return w[e][:, 2 * (u % 4):2 * (u % 4) + 2]
    return A.exp_w_down_2[0].rearrange("e (k p) n -> e p k n", p=P)[e][:, u - 8]


def experts(nc, A, scr, x_tm):
    NE, D, F = A.exp_w_gate_2.shape[1:]
    KT, FT, NU, NS = D // P, F // P, 12, 6
    assert NE % 2 == 0 and F == 512 and D == 1024
    with ExitStack() as ctx:
        c = Core(nc, ctx)
        stage = c.sb("ex_stage", [P, NS, D])
        w_hl = [c.sb(f"ex_w_hl{u}", [P, 2, D], F32R) for u in range(NU)]
        xg = c.sb("ex_rows", [P, 2, D])
        xs_hl = [c.sb(f"ex_x_hl{b}", [P, 2, KT, P], F32R) for b in range(2)]
        silu, act_f = c.sb("ex_silu", [P, F]), c.sb("ex_act", [P, F])
        a_hl = c.sb("ex_act_hl", [P, 2, FT, P], F32R)
        ys = c.sb("ex_ys", [P, 2, D])
        ident = c.sb("ex_ident", [P, P])
        lst = c.sb("ex_list", [P, scr.NT], U32)
        ps_g, ps_u, ps_a = c.ps("ex_ps_g", [P, F]), c.ps("ex_ps_u", [P, F]), c.ps("ex_ps_a", [P, FT, P])
        ps_d, ps_x = c.ps("ex_ps_d", [P, D]), c.ps("ex_ps_x", [P, KT, P])
        s_xin = c.sem("ex_x_loaded")
        s_w, s_row, s_st = c.sems("ex_w_loaded", NS), c.sems("ex_rows_gathered", 2), c.sems("ex_ys_stored", 2)
        s_hi, s_lo, s_use = c.sem("ex_w_high"), c.sem("ex_w_low"), c.sem("ex_w_used")
        s_xt, s_xh, s_xl = c.sem("ex_rows_turned"), c.sem("ex_x_high"), c.sem("ex_x_low")
        s_silu, s_act, s_at, s_ah, s_al = (c.sem(f"ex_{n}") for n in ("silu_ready", "act_ready", "act_turned", "act_high", "act_low"))
        s_ys, s_lst, s_id, s_id0 = c.sem("ex_ys_ready"), c.sem("ex_list_loaded"), c.sem("ex_ident_ready"), c.sem("ex_ident_steps")
        block = ctx.enter_context(nc.Block())

        def number(e, u):
            at = e + 1 if u >= 8 else e
            if isinstance(at, int) and at in (0, NE):
                return NU * at + u - (12 if at else 0)
            return NU * at + u - 4

        def used_before(e, u):
            if isinstance(e, int) and e == 0:
                return 0
            return number(e - 1, u) + 1
        slot = lambda e, u: number(e, u) % NS if isinstance(e, int) else (u - 4) % NS
        in_order = [(e, u) for e in range(NE + 1) for u in range(NU) if not (e == NE and u < 8) and not (e == 0 and u >= 8)]

        @block.sync
        def _(sp):
            for at, u in in_order:
                e = at - 1 if u >= 8 else at
                n = number(e, u)
                wait(sp, s_lo, n - NS + 1)
                dst = stage[:, n % NS]
                sp.dma_start(dst if u >= 8 else dst.rearrange("p (k n) -> p k n", n=F), weight_unit(A, u, e)).then_inc(s_w[n % NS], 16)

        @block.gpsimd
        def _(pool):
            identity(nc, pool, s_id, s_id0, ident[:], 0)
            pool.dma_start(lst[:], scr.list.rearrange("(p t) a -> p (t a)", t=scr.NT).bitcast(U32)).then_inc(s_lst, 16)
            pool.wait_ge(s_lst, 16)
            for e in range(NE):
                wait(pool, s_xt, e - 1)
                pool.indirect_dma_start(out=xg[:, e % 2], out_offset=None, in_=scr.h,
                                        in_offset=bass.IndirectOffsetOnAxis(ap=lst[:, e:e + 1], axis=0)).then_inc(s_row[e % 2], 16)
                if e == NE // 2:
                    pool.dma_start(x_tm[:], scr.x5.rearrange("(t p) d -> p t d", p=P)).then_inc(s_xin, 16)
            pool.wait_ge(s_xin, 16)

        def loads(e, u):
            if isinstance(e, int):
                return 16 * (number(e, u) // NS + 1)
            at = e + 1 if u >= 8 else e
            return 16 * (NU // NS) * at + 16 * ((u - 4) // NS + 1)

        @block.scalar
        def _(act):
            def high(e, u):
                s = slot(e, u)
                act.wait_ge(s_w[s], loads(e, u))
                wait(act, s_use, used_before(e, u))
                nc.scalar.activation(w_hl[u][:, 0], stage[:, s], ACT.Copy).then_inc(s_hi, 1)

            def x_high(e, b):
                act.wait_ge(s_xt, e + 1)
                if b == "first":
                    b = 0
                else:
                    wait(act, s_use, number(e - 2, 7) + 1 if not (isinstance(e, int) and e < 2) else 0)
                nc.scalar.activation(xs_hl[b][:, 0], ps_x[:], ACT.Copy).then_inc(s_xh, 1)

            def step(i, last=False):
                for b in range(2):
                    e = 2 * i + b
                    if isinstance(e, int) and e == 0:
                        for u in range(4):
                            high(0, u)
                        x_high(0, "first")
                        for u in range(4, 8):
                            high(0, u)
                    end, first = last and b == 1, isinstance(e, int) and e == 0
                    for u in range(0 if not end else 4, 4):
                        if u == 2 and not first:
                            act_high(e - 1)
                        if u == 3:
                            gate_silu(e)
                        high(e + 1, u)
                    if end:
                        act_high(e - 1)
                        gate_silu(e)
                    else:
                        x_high(e + 1, 1 - b)
                        for u in range(4, 8):
                            high(e + 1, u)
                    for u in range(8, 11):
                        high(e, u)
                    if not first:
                        rows_out(e - 1, 1 - b)
                    high(e, 11)
                    if not first:
                        store(e - 1, 1 - b)

            def store(e, b):
                act.wait_ge(s_ys, e + 1)
                act.dma_start(scr.ys.rearrange("(t p) d -> t p d", p=P)[e], ys[:, b]).then_inc(s_st[b], 16)

            def gate_silu(e):
                act.wait_ge(s_use, number(e, 3) + 1)
                wait(act, s_act, e)
                nc.scalar.activation(silu[:], ps_g[:], ACT.Silu).then_inc(s_silu, 1)

            def act_high(e):
                act.wait_ge(s_at, e + 1)
                if not (isinstance(e, int) and e == 0):
                    act.wait_ge(s_use, number(e - 1, 11) + 1)
                nc.scalar.activation(a_hl[:, 0], ps_a[:], ACT.Copy).then_inc(s_ah, 1)

            def rows_out(e, b):
                act.wait_ge(s_use, number(e, 11) + 1)
                if isinstance(e, int):
                    wait(act, s_st[b], 16 * (e // 2))
                else:
                    act.wait_ge(s_st[b], 8 * e - 8 * b)
                nc.scalar.activation(ys[:, b], ps_d[:], ACT.Copy).then_inc(s_ys, 1)

            steps(act, NE // 2, step, end=NE // 2 - 1)
            step(NE // 2 - 1, True)
            act_high(NE - 1)
            rows_out(NE - 1, 1)
            store(NE - 1, 1)
            for b in range(2):
                act.wait_ge(s_st[b], 16 * (NE // 2))

        @block.vector
        def _(dve):
            v = nc.vector

            def low(e, u):
                dve.wait_ge(s_hi, number(e, u) + 1)
                v.tensor_tensor(w_hl[u][:, 1], stage[:, slot(e, u)], f32(w_hl[u][:, 0]), ALU.subtract).then_inc(s_lo, 1)

            def x_low(e, b):
                dve.wait_ge(s_xh, e + 1)
                v.tensor_tensor(xs_hl[b][:, 1], ps_x[:], f32(xs_hl[b][:, 0]), ALU.subtract).then_inc(s_xl, 1)

            def step(i, last=False):
                for b in range(2):
                    e = 2 * i + b
                    if isinstance(e, int) and e == 0:
                        for u in range(4):
                            low(0, u)
                        x_low(0, 0)
                        for u in range(4, 8):
                            low(0, u)
                    end, first = last and b == 1, isinstance(e, int) and e == 0
                    for u in range(0 if not end else 4, 4):
                        if u == 2 and not first:
                            act_low(e - 1)
                        low(e + 1, u)
                    if end:
                        act_low(e - 1)
                    else:
                        x_low(e + 1, 1 - b)
                        for u in range(4, 8):
                            low(e + 1, u)
                    dve.wait_ge(s_silu, e + 1)
                    dve.wait_ge(s_use, number(e, 7) + 1)
                    wait(dve, s_at, e)
                    v.tensor_tensor(act_f[:], silu[:], ps_u[:], ALU.mult).then_inc(s_act, 1)
                    for u in range(8, 12):
                        low(e, u)

            def act_low(e):
                dve.wait_ge(s_ah, e + 1)
                v.tensor_tensor(a_hl[:, 1], ps_a[:], f32(a_hl[:, 0]), ALU.subtract).then_inc(s_al, 1)

            steps(dve, NE // 2, step, end=NE // 2 - 1)
            step(NE // 2 - 1, True)
            act_low(NE - 1)

        @block.tensor
        def _(pe):
            def turn(e, b):
                pe.wait_ge(s_row[b], 16 * (e // 2 + 1) if isinstance(e, int) else 8 * e - 8 * b + 16)
                wait(pe, s_xl, e)
                for k in range(KT):
                    last = nc.tensor.transpose(ps_x[:, k], xg[:, b, k * P:(k + 1) * P], ident[:])
                last.then_inc(s_xt, 1)

            def hidden(e, b, ps, u0):
                for u in range(u0, u0 + 4):
                    pe.wait_ge(s_lo, number(e, u) + 1)
                    for kk in range(2):
                        k = 2 * (u - u0) + kk
                        last = mm3(nc, ps[:], (xs_hl[b][:, 0, k], xs_hl[b][:, 1, k]),
                                   (w_hl[u][:, 0, kk * F:(kk + 1) * F], w_hl[u][:, 1, kk * F:(kk + 1) * F]),
                                   k == 0, k == KT - 1)
                    last.then_inc(s_use, 1)

            def down(e):
                wait(pe, s_ys, e)
                pe.wait_ge(s_al, e + 1)
                for u in range(8, 12):
                    k = u - 8
                    pe.wait_ge(s_lo, number(e, u) + 1)
                    for h in range(2):
                        cols = slice(h * 512, (h + 1) * 512)
                        last = mm3(nc, ps_d[:, cols], (a_hl[:, 0, k], a_hl[:, 1, k]), (w_hl[u][:, 0, cols], w_hl[u][:, 1, cols]),
                                   k == 0, k == FT - 1)
                    last.then_inc(s_use, 1)

            def turn_act(e):
                pe.wait_ge(s_act, e + 1)
                wait(pe, s_al, e)
                for k in range(FT):
                    last = nc.tensor.transpose(ps_a[:, k], act_f[:, k * P:(k + 1) * P], ident[:])
                last.then_inc(s_at, 1)

            def step(i, last=False):
                for b in range(2):
                    e = 2 * i + b
                    if isinstance(e, int) and e == 0:
                        turn(0, 0)
                    pe.wait_ge(s_xl, e + 1)
                    wait(pe, s_silu, e)
                    hidden(e, b, ps_g, 0)
                    if not (last and b == 1):
                        turn(e + 1, 1 - b)
                    wait(pe, s_act, e)
                    hidden(e, b, ps_u, 4)
                    if not (isinstance(e, int) and e == 0):
                        down(e - 1)
                    turn_act(e)

            pe.wait_ge(s_id, 1)
            steps(pe, NE // 2, step, end=NE // 2 - 1)
            step(NE // 2 - 1, True)
            down(NE - 1)


def further_tiles(nc, A, scr):
    NE, D, F = A.exp_w_gate_2.shape[1:]
    KT, FT, NX = D // P, F // P, scr.NX
    with ExitStack() as ctx:
        c = Core(nc, ctx)
        stage = c.sb("fx_stage", [P, 4, D])
        w_hl = c.sb("fx_w_hl", [P, 2, 4, D], F32R)
        xg = c.sb("fx_rows", [P, D])
        xs_hl = c.sb("fx_x_hl", [P, 2, KT, P], F32R)
        silu, act_f = c.sb("fx_silu", [P, F]), c.sb("fx_act", [P, F])
        a_hl = c.sb("fx_act_hl", [P, 2, FT, P], F32R)
        ys = c.sb("fx_ys", [P, D])
        ident = c.sb("fx_ident", [P, P])
        lst = c.sb("fx_list", [P, scr.NT], U32)
        ps_g, ps_u, ps_a = c.ps("fx_ps_g", [P, F]), c.ps("fx_ps_u", [P, F]), c.ps("fx_ps_a", [P, FT, P])
        ps_d, ps_x = c.ps("fx_ps_d", [P, D]), c.ps("fx_ps_x", [P, KT, P])
        s_w, s_hi, s_lo, s_use = c.sem("fx_w_loaded"), c.sem("fx_w_high"), c.sem("fx_w_low"), c.sem("fx_w_used")
        s_row, s_xt, s_xh, s_xl = c.sem("fx_row_gathered"), c.sem("fx_rows_turned"), c.sem("fx_x_high"), c.sem("fx_x_low")
        s_silu, s_act, s_at, s_ah, s_al = (c.sem(f"fx_{n}") for n in ("silu_ready", "act_ready", "act_turned", "act_high", "act_low"))
        s_ys, s_st, s_lst, s_id, s_id0 = (c.sem(f"fx_{n}") for n in ("ys_ready", "ys_stored", "list_loaded", "ident_ready", "ident_steps"))
        block = ctx.enter_context(nc.Block())
        count = scr.more[0:1, NX:NX + 1]

        def for_tiles(eng, body):
            n = eng.value_load(count, min_val=0, max_val=NX)
            with eng.If(n > 0):
                with eng.Fori(0, n) as j:
                    body(j)

        @block.gpsimd
        def _(pool):
            identity(nc, pool, s_id, s_id0, ident[:], 0)
            pool.dma_start(lst[:], scr.list.rearrange("(p t) a -> p (t a)", t=scr.NT).bitcast(U32)).then_inc(s_lst, 16)
            pool.wait_ge(s_lst, 16)
            n = pool.value_load(count, min_val=0, max_val=NX)
            for j in range(NX):
                with pool.If(n > j):
                    wait(pool, s_xt, j)
                    pool.indirect_dma_start(out=xg[:], out_offset=None, in_=scr.h,
                                            in_offset=bass.IndirectOffsetOnAxis(ap=lst[:, NE + j:NE + j + 1], axis=0)).then_inc(s_row, 16)

        @block.scalar
        def _(act):
            def body(j):
                e = act.value_load(scr.more[0:1, bass.ds(j, 1)], min_val=0, max_val=NE - 1)
                for r in range(3):
                    act.wait_ge(s_lo, 3 * j + r + 1)
                    for u in range(4 * r, 4 * r + 4):
                        dst = stage[:, u % 4]
                        src = weight_unit(A, u, e)
                        act.dma_start(dst if r == 2 else dst.rearrange("p (k n) -> p k n", n=F), src).then_inc(s_w, 16)
                    if r == 1:
                        act.wait_ge(s_xt, j + 1)
                        nc.scalar.activation(xs_hl[:, 0], ps_x[:], ACT.Copy).then_inc(s_xh, 1)
                    act.wait_ge(s_w, 64 * (3 * j + r + 1))
                    act.wait_ge(s_use, 3 * j + r + 1)
                    nc.scalar.activation(w_hl[:, 0], stage[:], ACT.Copy).then_inc(s_hi, 1)
                    if r == 1:
                        nc.scalar.activation(silu[:], ps_g[:], ACT.Silu).then_inc(s_silu, 1)
                act.wait_ge(s_at, j + 1)
                nc.scalar.activation(a_hl[:, 0], ps_a[:], ACT.Copy).then_inc(s_ah, 1)
                act.wait_ge(s_use, 3 * j + 4)
                nc.scalar.activation(ys[:], ps_d[:], ACT.Copy).then_inc(s_ys, 1)
                act.wait_ge(s_ys, j + 1)
                act.dma_start(scr.ys.rearrange("(t p) d -> t p d", p=P)[NE + j], ys[:]).then_inc(s_st, 16)
                act.wait_ge(s_st, 16 * j + 16)
            for_tiles(act, body)

        @block.vector
        def _(dve):
            v = nc.vector
            dve.sem_inc(s_lo, 1)

            def body(j):
                def low(r):
                    dve.wait_ge(s_hi, 3 * j + r + 1)
                    v.tensor_tensor(w_hl[:, 1], stage[:], f32(w_hl[:, 0]), ALU.subtract).then_inc(s_lo, 1)
                low(0)
                dve.wait_ge(s_xh, j + 1)
                v.tensor_tensor(xs_hl[:, 1], ps_x[:], f32(xs_hl[:, 0]), ALU.subtract).then_inc(s_xl, 1)
                low(1)
                dve.wait_ge(s_silu, j + 1)
                dve.wait_ge(s_use, 3 * j + 3)
                v.tensor_tensor(act_f[:], silu[:], ps_u[:], ALU.mult).then_inc(s_act, 1)
                low(2)
                dve.wait_ge(s_ah, j + 1)
                v.tensor_tensor(a_hl[:, 1], ps_a[:], f32(a_hl[:, 0]), ALU.subtract).then_inc(s_al, 1)
            for_tiles(dve, body)

        @block.tensor
        def _(pe):
            pe.sem_inc(s_use, 1)
            pe.wait_ge(s_id, 1)

            def body(j):
                pe.wait_ge(s_row, 16 * j + 16)
                for k in range(KT):
                    last = nc.tensor.transpose(ps_x[:, k], xg[:, k * P:(k + 1) * P], ident[:])
                last.then_inc(s_xt, 1)
                pe.wait_ge(s_xl, j + 1)
                for r, ps in enumerate((ps_g, ps_u)):
                    pe.wait_ge(s_lo, 3 * j + r + 2)
                    for k in range(KT):
                        w = w_hl[:, :, k // 2, (k % 2) * F:(k % 2 + 1) * F]
                        last = mm3(nc, ps[:], (xs_hl[:, 0, k], xs_hl[:, 1, k]), (w[:, 0], w[:, 1]), k == 0, k == KT - 1)
                    last.then_inc(s_use, 1)
                pe.wait_ge(s_act, j + 1)
                for k in range(FT):
                    last = nc.tensor.transpose(ps_a[:, k], act_f[:, k * P:(k + 1) * P], ident[:])
                last.then_inc(s_at, 1)
                pe.wait_ge(s_al, j + 1)
                pe.wait_ge(s_lo, 3 * j + 4)
                for k in range(FT):
                    for h in range(2):
                        cols = slice(h * 512, (h + 1) * 512)
                        last = mm3(nc, ps_d[:, cols], (a_hl[:, 0, k], a_hl[:, 1, k]), (w_hl[:, 0, k, cols], w_hl[:, 1, k, cols]),
                                   k == 0, k == FT - 1)
                last.then_inc(s_use, 1)
            for_tiles(pe, body)


def combine(nc, A, scr, x_tm, out):
    T, D, NB = scr.T, A.x.shape[2], 4
    with ExitStack() as ctx:
        c = Core(nc, ctx)
        y = c.sb("cb_rows", [P, NB, 2, D])
        rowg, square = c.sb("cb_gain", [P, D]), c.sb("cb_square", [P, D])
        ssq, eps = c.sb("cb_ssq", [P, 3, T]), c.sb("cb_eps", [P, 1])
        res = c.sb("cb_res", [P, 2, D])
        s_y = c.sems("cb_gathered", NB)
        s_g, s_eps, s_a, s_x, s_sq, s_std, s_rs, s_res = (c.sem(f"cb_{n}") for n in (
            "gain_loaded", "eps_ready", "first_added", "added", "squared", "std_ready", "rstd_ready", "result"))
        s_st = c.sems("cb_stored", 2)
        block = ctx.enter_context(nc.Block())

        @block.sync
        def _(sp):
            sp.dma_start(rowg[:], A.norm_f_w_2.rearrange("(a n) -> a n", a=1).broadcast_to([P, D])).then_inc(s_g, 16)
            for t in range(T):
                sp.wait_ge(s_res, t + 1)
                sp.dma_start(out[t * P:(t + 1) * P, :], res[:, t % 2]).then_inc(s_st[t % 2], 16)
            for b in range(2):
                sp.wait_ge(s_st[b], 16 * (T // 2))

        @block.gpsimd
        def _(pool):
            nc.gpsimd.memset(eps[:], EPS).then_inc(s_eps, 1)
            for t in range(T):
                wait(pool, s_x, t - NB + 1)
                for n in range(2):
                    pool.indirect_dma_start(out=y[:, t % NB, n], out_offset=None, in_=scr.ys,
                                            in_offset=bass.IndirectOffsetOnAxis(ap=scr.row[:, n, t:t + 1], axis=0)).then_inc(s_y[t % NB], 16)

        @block.scalar
        def _(act):
            act.wait_ge(s_eps, 1)
            for t in range(T):
                act.wait_ge(s_x, t + 1)
                nc.scalar.activation(square[:], x_tm[:, t], ACT.Square, accum_out=ssq[:, 0, t:t + 1]).then_inc(s_sq, 1)
                act.wait_ge(s_sq, t + 1)
                nc.scalar.activation(ssq[:, 1, t:t + 1], ssq[:, 0, t:t + 1], ACT.Sqrt, scale=1.0 / D, bias=eps[:]).then_inc(s_std, 1)

        @block.vector
        def _(dve):
            v = nc.vector

            def add(t):
                dve.wait_ge(s_y[t % NB], 32 * (t // NB + 1))
                v.scalar_tensor_tensor(x_tm[:, t], y[:, t % NB, 0], scr.gate[:, 0, t:t + 1], x_tm[:, t], ALU.mult, ALU.add).then_inc(s_a, 1)
                dve.wait_ge(s_a, t + 1)
                v.scalar_tensor_tensor(x_tm[:, t], y[:, t % NB, 1], scr.gate[:, 1, t:t + 1], x_tm[:, t], ALU.mult, ALU.add).then_inc(s_x, 1)

            def finish(t):
                dve.wait_ge(s_std, t + 1)
                v.reciprocal(ssq[:, 2, t:t + 1], ssq[:, 1, t:t + 1]).then_inc(s_rs, 1)
                dve.wait_ge(s_rs, t + 1)
                wait(dve, s_st[t % 2], 16 * (t // 2))
                v.scalar_tensor_tensor(res[:, t % 2], x_tm[:, t], ssq[:, 2, t:t + 1], rowg[:], ALU.mult, ALU.mult).then_inc(s_res, 1)

            dve.wait_ge(s_g, 16)
            for t in range(T):
                add(t)
                if t:
                    finish(t - 1)
            finish(T - 1)


def second_block(nc, A, x_dram, scr, hl):
    T, KT = scr.T, hl.shape[2]
    second_mixers(nc, A, hl, scr)
    recycle_semaphores(nc)
    w_out = A.w_out_2[0].rearrange("(k p) n -> p k n", p=P)
    with nc.sbuf_tensor("x_rows3", [P, T, KT * P], F32) as x_tm:
        add_product(nc, "w1", x_tm, hl, w_out[:, KT:], x_dram=x_dram)
        load_split(nc, "ys", scr.y_ssd, hl)
        add_product(nc, "w2", x_tm, hl, w_out[:, :KT], norm=("n4", A.norm2_w_2[0], dict(rows_out=scr.h, x_out=scr.x5)))
    route(nc, A, hl, scr)
    recycle_semaphores(nc)


def routed_experts(nc, A, scr, out):
    T, D = scr.T, A.x.shape[2]
    with nc.sbuf_tensor("x_rows4", [P, T, D], F32) as x_tm:
        experts(nc, A, scr, x_tm)
        recycle_semaphores(nc)
        further_tiles(nc, A, scr)
        combine(nc, A, scr, x_tm, out)


def scratch(nc, ctx, A):
    S, D, NE = A.x.shape[1], A.x.shape[2], A.router_e_w_2.shape[2]
    T, KT = S // P, D // P
    scr = Names()
    scr.T, scr.NX = T, 2 * T - 1
    scr.NT = NE + 2 * T
    dram = lambda name, shape, dt=F32: nc.dram_tensor(f"scratch_{name}", shape, dt).ap()
    scr.ya, scr.yb, scr.sga, scr.sgb = (dram(n, [KT, P, S]) for n in ("y_a", "y_b", "gate_a", "gate_b"))
    scr.y_ssd, scr.o = dram("y_ssd", [KT, P, S]), dram("o", [KT, P, S])
    scr.x4, scr.x5, scr.h = dram("x4", [S, D]), dram("x5", [S, D]), dram("h", [S, D])
    scr.ys, scr.list = dram("ys", [(NE + scr.NX) * P, D]), dram("list", [P * scr.NT, 1], I32)
    scr.gate = ctx.enter_context(nc.sbuf_tensor("pair_gates", [P, 2, T], F32))
    scr.row = ctx.enter_context(nc.sbuf_tensor("pair_rows", [P, 2, T], U32))
    scr.more = ctx.enter_context(nc.sbuf_tensor("further_tiles", [P, scr.NX + 1], I32))
    return scr


def program(nc, A, out):
    T, KT = A.x.shape[1] // P, A.x.shape[2] // P
    with ExitStack() as ctx:
        scr = scratch(nc, ctx, A)
        with nc.sbuf_tensor("h_hl", [P, 2, KT, A.x.shape[1]], F32R) as hl:
            with nc.sbuf_tensor("x_rows", [P, T, KT * P], F32) as x_tm:
                norm_transpose(nc, "n1", x_tm, A.ln1_g[0], hl, x_dram=A.x[0])
            first_mixers(nc, A, hl, scr)
            merge_mixers(nc, A, scr, hl)
            recycle_semaphores(nc)
            with nc.sbuf_tensor("x_rows2", [P, T, KT * P], F32) as x_tm:
                add_product(nc, "wo", x_tm, hl, A.w_o[0].rearrange("(k p) n -> p k n", p=P), x_dram=A.x[0],
                            norm=("n2", A.ln2_g[0], {}))
                feed_forward(nc, A, x_tm, hl)
                norm_transpose(nc, "n3", x_tm, A.norm1_w_2[0], hl, row_gain=A.final_g, x_out=scr.x4)
            recycle_semaphores(nc)
            second_block(nc, A, scr.x4, scr, hl)
        routed_experts(nc, A, scr, out[0])


_INS = ["x", "ln1_g", "w_in", "conv_a_w", "conv_b_w", "conv_b_b", "lru_wa", "lru_ba", "lru_wx", "lru_bx",
        "lru_lambda", "w_out_a", "w_out_b", "gate_bias", "w_o", "ln2_g", "w_ffn_gate", "w_ffn_up",
        "w_ffn_down", "final_g", "norm1_w_2", "w_in_2", "ssd_conv_w_2", "ssd_conv_b_2", "ssd_dt_bias_2",
        "ssd_a_log_2", "ssd_d_2", "ssd_norm_w_2", "ml_conv_w_2", "ml_conv_b_2", "ml_i_bias_2", "ml_f_bias_2",
        "ml_norm_w_2", "w_out_2", "norm2_w_2", "router_g_w_2", "router_g_b_2", "router_e_w_2", "router_e_b_2",
        "exp_w_gate_2", "exp_w_up_2", "exp_w_down_2", "norm_f_w_2"]
_OUTS = [((1, 1024, 1024), "float32")]


def kernel(**inputs):
    import numpy as _np
    import concourse.bacc as _bacc
    from concourse import mybir as _mybir
    from concourse.bass_utils import run_bass_kernel_spmd as _run

    nc = _bacc.Bacc("TRN2", target_bir_lowering=False, num_devices=1)
    arrays, args = {}, Names()
    for name in _INS:
        a = _np.ascontiguousarray(inputs[name])
        arrays[f"in_{name}_dram"] = a
        args.__dict__[name] = nc.dram_tensor(f"in_{name}_dram", a.shape, _mybir.dt.from_np(a.dtype), kind="ExternalInput").ap()
    outs = [nc.dram_tensor(f"out_{i}_dram", shape, _mybir.dt.from_np(_np.dtype(dtype)), kind="ExternalOutput").ap()
            for i, (shape, dtype) in enumerate(_OUTS)]
    program(nc, args, outs[0])
    r = _run(nc, [arrays], core_ids=[0])
    return r.results[0]["out_0_dram"]
```
